# Optimizing a Trainium2 kernel written in Bass

```python
import jax, jax.numpy as jnp
from jax import lax
import numpy as np

D_MODEL = 1024
BATCH = 1
SEQ = 512
DEPTH = 1

D_POOL = D_MODEL // 2
POOL_WINDOWS = (2, 4, 8, 16)
POOL_GROUP = D_POOL // len(POOL_WINDOWS)
D_GLA_V = D_MODEL // 2
GLA_HEADS = 4
GLA_DK = (D_GLA_V // 2) // GLA_HEADS
GLA_DV = D_GLA_V // GLA_HEADS
GLA_RANK = 16
GATE_NORM = 16.0
GLA_CHUNK = 64
D_IN = D_POOL + 2 * GLA_HEADS * GLA_DK + 2 * D_GLA_V + 2 * GLA_RANK

N_EXPERTS = 32
N_GROUPS = 4
EXPERTS_PER_GROUP = N_EXPERTS // N_GROUPS
TOP_K = 2
D_FF = 512
MOE_BLOCK = 512
EPS = 1e-6

kernel_name = "hybrid_pool_gla_groupmoe_adaln_encoder"

def rms_norm(x):
    xf = x.astype(jnp.float32)
    y = xf * lax.rsqrt(jnp.mean(xf * xf, axis=-1, keepdims=True) + EPS)
    return y.astype(x.dtype)

def pool_mixer(u, w_pool, pool_scale):
    bn, sn, _ = u.shape
    uf = u.astype(jnp.float32)
    pos = jnp.arange(sn)
    outs = []
    for gi, w in enumerate(POOL_WINDOWS):
        ug = uf[..., gi * POOL_GROUP:(gi + 1) * POOL_GROUP]
        csum = jnp.concatenate([jnp.zeros((bn, 1, POOL_GROUP), jnp.float32), jnp.cumsum(ug, axis=1)], axis=1)
        lo = jnp.clip(pos - w // 2, 0, sn - 1)
        hi = jnp.clip(pos - w // 2 + w - 1, 0, sn - 1)
        cnt = (hi - lo + 1).astype(jnp.float32)[None, :, None]
        outs.append((csum[:, hi + 1] - csum[:, lo]) / cnt - ug)
    pooled = jnp.stack(outs, axis=2).astype(u.dtype)
    y = jnp.einsum('bsgc,gcd->bsgd', pooled, w_pool)
    return y.reshape(bn, sn, D_POOL) * pool_scale

def gla_chunked(q, k, v, loga, strict):
    bn, hn, sn, dk = q.shape
    dv = v.shape[-1]
    nc = sn // GLA_CHUNK
    q = q.reshape(bn, hn, nc, GLA_CHUNK, dk)
    k = k.reshape(bn, hn, nc, GLA_CHUNK, dk)
    v = v.reshape(bn, hn, nc, GLA_CHUNK, dv)
    b = jnp.cumsum(loga.reshape(bn, hn, nc, GLA_CHUNK, dk), axis=3)
    qe = q * jnp.exp(b)
    ke = k * jnp.exp(-b)
    mask = jnp.tril(jnp.ones((GLA_CHUNK, GLA_CHUNK), bool), -1 if strict else 0)
    att = jnp.where(mask, jnp.einsum('bhnid,bhnjd->bhnij', qe, ke), 0.0)
    o = jnp.einsum('bhnij,bhnjv->bhniv', att, v)
    b_last = b[..., -1:, :]
    upd = jnp.einsum('bhncd,bhncv->bhndv', k * jnp.exp(b_last - b), v)
    decay = jnp.exp(b_last[..., 0, :])

    def step(state, inp):
        u_n, g_n = inp
        return g_n[..., None] * state + u_n, state

    _, s_before = lax.scan(step, jnp.zeros((bn, hn, dk, dv), jnp.float32),
                           (jnp.moveaxis(upd, 2, 0), jnp.moveaxis(decay, 2, 0)))
    s_before = jnp.moveaxis(s_before, 0, 2)
    o = o + jnp.einsum('bhncd,bhndv->bhncv', qe, s_before)
    return o.reshape(bn, hn, sn, dv)

def gla_mixer(q, k, v, g, r_f, r_b, w_gk_up, b_gk, norm_g):
    bn, sn, _ = q.shape

    def heads(t, d):
        return t.reshape(bn, sn, GLA_HEADS, d).transpose(0, 2, 1, 3).astype(jnp.float32)

    qh = heads(q, GLA_DK) * (GLA_DK ** -0.5)
    kh = heads(k, GLA_DK)
    vh = heads(v, GLA_DV)
    la_f = heads(jax.nn.log_sigmoid((r_f @ w_gk_up[0] + b_gk[0]).astype(jnp.float32)) / GATE_NORM, GLA_DK)
    la_b = heads(jax.nn.log_sigmoid((r_b @ w_gk_up[1] + b_gk[1]).astype(jnp.float32)) / GATE_NORM, GLA_DK)
    flip = lambda t: jnp.flip(t, axis=2)
    o = gla_chunked(qh, kh, vh, la_f, False) + flip(gla_chunked(flip(qh), flip(kh), flip(vh), flip(la_b), True))
    o = o * lax.rsqrt(jnp.mean(o * o, axis=-1, keepdims=True) + EPS) * norm_g.astype(jnp.float32)
    o = o.transpose(0, 2, 1, 3).reshape(bn, sn, D_GLA_V).astype(q.dtype)
    return o * jax.nn.silu(g)

def moe_ffn(h, w_router, b_router, w1, w3, w2):
    bn, sn, d = h.shape
    t = bn * sn
    ht = h.reshape(t, d)
    s = jax.nn.sigmoid(jnp.dot(ht.astype(jnp.float32), w_router.astype(jnp.float32)))
    sel = (s + b_router.astype(jnp.float32)).reshape(t, N_GROUPS, EXPERTS_PER_GROUP)
    g_idx = jnp.argmax(lax.top_k(sel, TOP_K)[0].sum(-1), axis=-1)
    in_grp = jnp.take_along_axis(sel, g_idx[:, None, None], axis=1)[:, 0]
    _, loc = lax.top_k(in_grp, TOP_K)
    e_idx = (g_idx[:, None] * EXPERTS_PER_GROUP + loc).astype(jnp.int32)
    gw = jnp.take_along_axis(s, e_idx, axis=1)
    gw = gw / jnp.sum(gw, axis=-1, keepdims=True)

    n_assign = t * TOP_K
    flat_e = e_idx.reshape(n_assign)
    flat_w = gw.reshape(n_assign).astype(h.dtype)
    flat_tok = jnp.arange(n_assign, dtype=jnp.int32) // TOP_K
    order = jnp.argsort(flat_e)
    sorted_e = flat_e[order]
    counts = jnp.bincount(flat_e, length=N_EXPERTS).astype(jnp.int32)
    padded = (counts + MOE_BLOCK - 1) // MOE_BLOCK * MOE_BLOCK
    pad_end = jnp.cumsum(padded)
    pad_start = pad_end - padded
    start = jnp.cumsum(counts) - counts
    dest = pad_start[sorted_e] + jnp.arange(n_assign, dtype=jnp.int32) - start[sorted_e]
    n_blocks = -(-n_assign // MOE_BLOCK) + N_EXPERTS
    rows = n_blocks * MOE_BLOCK
    row_tok = jnp.full((rows,), t, jnp.int32).at[dest].set(flat_tok[order])
    row_w = jnp.zeros((rows,), h.dtype).at[dest].set(flat_w[order])
    blk_e = jnp.minimum(jnp.searchsorted(pad_end, jnp.arange(n_blocks, dtype=jnp.int32) * MOE_BLOCK, side='right'),
                        N_EXPERTS - 1)
    x_pad = jnp.concatenate([ht, jnp.zeros((1, d), h.dtype)], axis=0)

    def block_ffn(args):
        e, tok, wt = args
        xb = x_pad[tok]
        hid = jax.nn.silu(xb @ w1[e]) * (xb @ w3[e])
        return (hid @ w2[e]) * wt[:, None]

    ys = lax.map(block_ffn, (blk_e, row_tok.reshape(n_blocks, MOE_BLOCK), row_w.reshape(n_blocks, MOE_BLOCK)))
    out = jnp.zeros((t + 1, d), h.dtype).at[row_tok].add(ys.reshape(rows, d))
    return out[:t].reshape(bn, sn, d)

def setup_inputs(seed: int = 0) -> dict:
    key = jax.random.key(seed)
    ks = jax.random.split(key, 20)
    f32 = jnp.float32
    nrm = lambda k, shape, scale: jax.random.normal(k, shape, f32) * scale
    L, D = DEPTH, D_MODEL
    return {
        "x": nrm(ks[0], (BATCH, SEQ, D), 1.0),
        "c": nrm(ks[1], (BATCH, D), 1.0),
        "w_mod": nrm(ks[2], (L, D, 6 * D), 0.5 * D ** -0.5),
        "b_mod": nrm(ks[3], (L, 6 * D), 0.02),
        "w_in": nrm(ks[4], (L, D, D_IN), D ** -0.5),
        "w_pool": nrm(ks[5], (L, len(POOL_WINDOWS), POOL_GROUP, POOL_GROUP), POOL_GROUP ** -0.5),
        "pool_scale": 1.0 + nrm(ks[6], (L, D_POOL), 0.02),
        "w_gk_up": nrm(ks[7], (L, 2, GLA_RANK, GLA_HEADS * GLA_DK), GLA_RANK ** -0.5),
        "b_gk": nrm(ks[8], (L, 2, GLA_HEADS * GLA_DK), 0.1),
        "gla_norm_g": 1.0 + nrm(ks[9], (L, GLA_DV), 0.02),
        "w_out": nrm(ks[10], (L, D, D), D ** -0.5),
        "w_router": nrm(ks[11], (D, N_EXPERTS), D ** -0.5),
        "b_router": nrm(ks[12], (N_EXPERTS,), 0.01),
        "w1": nrm(ks[13], (L, N_EXPERTS, D, D_FF), D ** -0.5),
        "w3": nrm(ks[14], (L, N_EXPERTS, D, D_FF), D ** -0.5),
        "w2": nrm(ks[15], (L, N_EXPERTS, D_FF, D), D_FF ** -0.5),
        "final_g": 1.0 + nrm(ks[16], (D,), 0.02),
    }

def reference(x, c, w_mod, b_mod, w_in, w_pool, pool_scale, w_gk_up, b_gk, gla_norm_g, w_out,
              w_router, b_router, w1, w3, w2, final_g):
    split_at = np.cumsum([D_POOL, GLA_HEADS * GLA_DK, GLA_HEADS * GLA_DK, D_GLA_V, D_GLA_V, GLA_RANK]).tolist()
    c_act = jax.nn.silu(c)
    for l in range(DEPTH):
        mod = (c_act @ w_mod[l] + b_mod[l])[:, None, :]
        sh1, sc1, g1, sh2, sc2, g2 = jnp.split(mod, 6, axis=-1)
        h = rms_norm(x) * (1.0 + sc1) + sh1
        z = h @ w_in[l]
        u_pool, q, k, v, g, r_f, r_b = jnp.split(z, split_at, axis=-1)
        y_pool = pool_mixer(u_pool, w_pool[l], pool_scale[l])
        y_gla = gla_mixer(q, k, v, g, r_f, r_b, w_gk_up[l], b_gk[l], gla_norm_g[l])
        mix = jnp.concatenate([y_pool, y_gla], axis=-1) @ w_out[l]
        x = x + g1 * mix
        h = rms_norm(x) * (1.0 + sc2) + sh2
        x = x + g2 * moe_ffn(h, w_router, b_router, w1[l], w3[l], w2[l])
    return rms_norm(x) * final_g


_drawn_inputs = setup_inputs


def setup_inputs(seed=0):
    import zlib

    import numpy as np

    out = dict(_drawn_inputs(seed))
    spreads = {}
    factors = {'pool_scale': 5.452, 'b_gk': 4.255, 'gla_norm_g': 4.331, 'final_g': 2.869}
    for name, (base, spread) in spreads.items():
        noise = np.random.default_rng([zlib.crc32(name.encode()), seed]).standard_normal(out[name].shape)
        drawn = base * np.exp(spread * noise) if base else spread * noise
        out[name] = __import__('jax').numpy.asarray(drawn.astype(out[name].dtype))
    for name, factor in factors.items():
        out[name] = (out[name] * factor).astype(out[name].dtype)
    return out
```

```python
from contextlib import ExitStack

import numpy as np

import concourse.bass as bass
from concourse import mybir

F32 = mybir.dt.float32
F32R = mybir.dt.float32r
I32 = mybir.dt.int32
ALU = mybir.AluOpType
ACT = mybir.ActivationFunctionType
AX_X = mybir.AxisListType.X

P = 128
D = 1024
S = 512
KD = D // P
NT = S // P
DG = 512
WINDOWS = (2, 4, 8, 16)
HEADS, DK, DV = 4, 64, 128
RANK = 16
CHUNK = 64
NCH = S // CHUNK
GATE_NORM = 16.0
E_N, G_N, EPG = 32, 4, 8
DFF = 512
KF = DFF // P
EPS = 1e-6
CAP = 64
PAIRS = E_N // 2
ROUNDS = S // CAP
UNIT = 4096
SLOTS = 8
PRE_SLOTS = 6
UPP = 6
PPI = 4
ITERS = PAIRS // PPI
EXTRA_STEPS = 27
A_AHEAD = Y_AHEAD = 2

SC = dict(c=(0, 8), bmod=(8, 24), pscale=(24, 28), bgk=(28, 32), ng=(32, 33), eps=(33, 34))
SC_N = 34
CP = dict(ident=(0, 128), iota=(128, 192), off=(192, 200))
CP_N = 200
CT = dict(reset=(0, 512), ones=(512, 640), sel=(640, 768), lower=(768, 896))
CT_N = 896
CM_N = 256
CE_N = 2 * 26


def pool_offsets():
    out, at, ed = [], 0, 0
    for w in WINDOWS:
        out.append((at, w // 2, ed))
        at += S + w - 1
        ed += w - 1
    return out, at, ed


POOL_AT, POOL_N, EDGE_N = pool_offsets()


def constants():
    r = np.arange(P)
    cp = np.zeros((P, CP_N), np.float32)
    cp[:, 0:128] = np.eye(P)
    cp[:, 128:192] = np.arange(CAP)[None]
    cp[:, 192:200] = -CAP * np.arange(ROUNDS)[None]
    ct = np.zeros((P, CT_N), np.float32)
    ct[:, 0:512] = (np.arange(S) % CHUNK != 0)[None]
    ct[:, 512:640] = 1.0
    ct[0::32, 640:768] = 1.0
    ct[:, 768:896] = r[:, None] < r[None, :]
    cm = np.zeros((P, CM_N), np.float32)
    same = r[:, None] // CHUNK == r[None, :] // CHUNK
    cm[:, 0:128] = same & (r[:, None] <= r[None, :])
    cm[:, 128:256] = same & (r[:, None] > r[None, :])
    ce = np.zeros((P, EDGE_N), np.float32)
    t = np.arange(S)
    for w, (_, _, ed) in zip(WINDOWS, POOL_AT):
        cnt = np.minimum(t - w // 2 + w - 1, S - 1) - np.maximum(t - w // 2, 0) + 1
        f = (w / cnt).astype(np.float32)
        ce[:, ed:ed + w // 2] = f[:w // 2]
        ce[:, ed + w // 2:ed + w - 1] = f[S - (w // 2 - 1):] if w > 2 else 0
    i8 = np.broadcast_to(np.arange(E_N, dtype=np.float32)[None], (P, E_N))
    return cp, np.concatenate([ct, ce], 1), cm, i8


JOBS = ([f"mr{i}" for i in range(4)] + ["mcol"] + [f"xT{k}" for k in range(KD)] + ["r"]
        + [f"u{i}" for i in range(4)] + [f"gk{i}" for i in range(4)]
        + ["q0", "q1", "k0", "k1"] + [f"yp{i}" for i in range(4)]
        + [f"v{i}" for i in range(4)] + [f"g{i}" for i in range(4)]
        + [f"att{d}{h}" for d in range(2) for h in range(HEADS)]
        + [f"kdt{d}{p}" for d in range(2) for p in range(2)]
        + [f"upd{d}{p}{par}" for d in range(2) for p in range(2) for par in range(2)]
        + [f"o{h}" for h in range(HEADS)] + [f"ss{h}" for h in range(HEADS)]
        + [f"m{a}{i}" for i in range(4, 12) for a in "rb"]
        + [f"wo{hf}{t}" for hf in range(2) for t in range(NT)]
        + [f"hT{t}{hf}" for t in range(NT) for hf in range(2)] + ["lg", "rk", "cnt"])
JOB = {n: i for i, n in enumerate(JOBS)}
assert len(JOB) == len(JOBS)
OUT_SCALAR = ([f"mr{i}" for i in range(4)] + [f"xT{k}" for k in range(0, KD, 2)] + ["r"]
              + [f"u{i}" for i in range(4)] + [f"gk{i}" for i in range(4)] + ["q0", "q1", "k0", "k1"]
              + [f"yp{i}" for i in range(4)] + [f"g{i}" for i in range(4)]
              + [f"kdt{d}{p}" for d in range(2) for p in range(2)] + [f"ss{h}" for h in range(HEADS)]
              + [f"mr{i}" for i in range(4, 12)] + [f"hT{t}{hf}" for t in range(NT) for hf in range(2)] + ["lg"])
OUT_VECTOR = (["mcol"] + [f"xT{k}" for k in range(1, KD, 2)] + [f"v{i}" for i in range(4)]
              + [f"att{d}{h}" for d in range(2) for h in range(HEADS)]
              + [f"upd{d}{p}{par}" for d in range(2) for p in range(2) for par in range(2)]
              + [f"o{h}" for h in range(HEADS)] + [f"mb{i}" for i in range(4, 12)]
              + [f"wo{hf}{t}" for hf in range(2) for t in range(NT)] + ["rk", "cnt"])
assert sorted(OUT_SCALAR + OUT_VECTOR) == sorted(JOBS)
STREAM = (["m0", "m1", "m2", "m3", "u", "qk", "v", "g"] + [f"m{i}" for i in range(4, 12)] + ["wo0", "wo1"])
SU = {n: i for i, n in enumerate(STREAM)}
PRE_UNITS = len(STREAM)
assert PRE_UNITS == 3 * PRE_SLOTS
LAST_USE_OF = dict(u="u3", qk="k1", v="v3", g="g3", wo0="wo03", wo1="wo13")
LAST_USE = [LAST_USE_OF.get(n, "mr" + n[1:]) for n in STREAM]


def build(nc, A, out, scratch):
    ctx = ExitStack()
    with ctx:
        def sb(name, shape, dt=F32):
            return ctx.enter_context(nc.sbuf_tensor(name, shape, dt))

        def sem(name):
            return ctx.enter_context(nc.semaphore(name))

        ring = sb("ring", [P, SLOTS, UNIT])
        x1 = sb("x1", [P, NT, D])
        big = sb("big", [P, UNIT])
        mid = sb("mid", [P, UNIT])
        low = sb("low", [P, UNIT])
        y_hi = sb("y_hi", [P, D], F32R)
        y_lo = sb("y_lo", [P, D], F32R)
        slot_tok = sb("slot_tok", [P, 2, S], F32R)
        keep = sb("keep", [P, 960])

        at = [0]

        def take(n):
            at[0] += n
            assert at[0] <= 960
            return keep[:, at[0] - n:at[0]]

        cp = take(CP_N)
        ident, iota, offs = cp[:, 0:128], cp[:, 128:192], cp[:, 192:200]
        cols = take(SC_N)
        col = {n: cols[:, a:b] for n, (a, b) in SC.items()}
        wrt = take(KD * E_N).rearrange("p (k e) -> p k e", k=KD)
        iota32 = take(E_N)
        rankm = take(NT * (E_N + 2)).rearrange("p (t e) -> p t e", t=NT)
        gwt = take(NT * (E_N + 2)).rearrange("p (t e) -> p t e", t=NT)
        gw_pair = take(NT * 2).rearrange("p (t e) -> p t e", t=NT)
        w_slot = take(2)
        count_f = take(PAIRS)
        count_i = take(PAIRS).bitcast(I32)
        modc = take(16)
        cs = take(KD)
        ssq = take(NT)
        rstd = take(NT)
        b_rt = take(E_N)
        rank_pair = take(NT * 2).rearrange("p (t e) -> p t e", t=NT)
        decay = take(4 * NCH).rearrange("p (a c) -> p a c", a=4)

        scr = ring[:, PRE_SLOTS:SLOTS, :].rearrange("p a n -> p (a n)")
        q_s = scr[:, 0:1024].rearrange("p (a t) -> p a t", a=2)
        k_s = scr[:, 1024:2048].rearrange("p (a t) -> p a t", a=2)
        v_s = scr[:, 2048:4096].rearrange("p (t c) -> p t c", t=NT)
        g_s = scr[:, 4096:6144].rearrange("p (h t) -> p h t", h=HEADS)
        up = scr[:, 4096:4096 + POOL_N]
        modr = scr[:, 4096:6144]
        base = 4096 + POOL_N
        ct = scr[:, base:base + CT_N + EDGE_N]
        reset, ones, sel, lower = ct[:, 0:512], ct[:, 512:640], ct[:, 640:768], ct[:, 768:896]
        edge = ct[:, CT_N:CT_N + EDGE_N]
        base += CT_N + EDGE_N
        ta, tb = scr[:, base:base + 528], scr[:, base + 528:base + 1056]
        base += 1056
        assert base <= 2 * UNIT
        att = scr[:, 0:2048].rearrange("p (h n) -> p h n", h=HEADS)
        sq, rst = ta[:, 0:512], tb[:, 0:512]
        bias_row = big[0:1, :]
        g1b, sc2b = scr[:, 2048:3072], scr[:, 3072:4096]
        sh2b, g2b = scr[:, 4096:5120], scr[:, 5120:6144]
        mrow = scr[:, 0:1024].rearrange("p (a n) -> p a n", a=2)
        rt = scr[:, 1280:2048]
        rt_s, rt_sel, rt_a, rt_tmp = (rt[:, i * 128:(i + 1) * 128].rearrange("p (t e) -> p t e", t=NT) for i in range(4))
        rt_srt = rt[:, 512:640].rearrange("p (t g e) -> p t g e", t=NT, g=G_N)
        rt_gs, rt_goh = (rt[:, 640 + i * 16:656 + i * 16].rearrange("p (t g) -> p t g", t=NT) for i in range(2))
        rt_in, rt_oh1, rt_oh2 = (scr[:, 1024 + i * 32:1056 + i * 32].rearrange("p (t e) -> p t e", t=NT) for i in range(3))
        rt_t12 = rt[:, 672:680].rearrange("p (t e) -> p t e", t=NT)
        rt_top, rt_m = rt[:, 680:684], rt[:, 684:688]

        h_t = big[:, :].rearrange("p (k t) -> p k t", k=KD)
        qe = big[:, 0:2048].rearrange("p (d a t) -> p d a t", d=2, a=2)
        ke = big[:, 2048:4096].rearrange("p (d a t) -> p d a t", d=2, a=2)
        acc = big[:, :].rearrange("p (t n) -> p t n", t=NT)
        xn = mid[:, :].rearrange("p (t n) -> p t n", t=NT)
        la = mid[:, 0:2048].rearrange("p (d a t) -> p d a t", d=2, a=2)
        bb = mid[:, 2048:4096].rearrange("p (d a t) -> p d a t", d=2, a=2)
        kd = la
        kdtok = bb.rearrange("p d a (t c) -> p d a t c", t=NT)
        st = [mid[:, 0:1792].rearrange("p (a n v) -> p a n v", a=2, n=7),
              big[:, 2048:3840].rearrange("p (a n v) -> p a n v", a=2, n=7)]
        h2 = mid[:, :].rearrange("p (t n) -> p t n", t=NT)
        cat = low[:, :].rearrange("p (k t) -> p k t", k=KD)
        wpool = low[:, 2048:2560].rearrange("p (g c) -> p g c", g=4)
        wr = low[:, 2560:2816].rearrange("p (k c) -> p k c", k=KD)
        masks = low[:, 2816:3072]
        wup = low[0:2 * RANK, 3072:3584].rearrange("p (d c) -> p d c", d=2)
        r_t = low[0:2 * RANK, 3584:4096]
        cb = scr[:, 1024:1280].rearrange("p (k m) -> p k m", k=KD)
        h2t = low[:, :].rearrange("p (k t) -> p k t", k=KD)
        onehot = low[:, 0:512].rearrange("p (t s) -> p t s", t=NT)
        xg = low[:, 512:2560].rearrange("p (b k s) -> p b k s", b=2, k=KD)
        sil = low[:, 2560:3072]
        hid = low[:, 3072:3584]
        hid_t = low[:, 3584:4096].rearrange("p (k s) -> p k s", k=KF)

        bank = [ctx.enter_context(nc.psum_tensor(f"bank{i}", [P, 512], F32)) for i in range(8)]

        def sems(names):
            return [sem(n) for n in names.split()]

        landed = [sem(f"landed{i}") for i in range(SLOTS)]
        x_in = [sem(f"x_in{t}") for t in range(NT)]
        cols_in, keep_in, tmp_in, small_in, bias_in = sems("cols_in keep_in tmp_in small_in bias_in")
        job_done, out_scalar, out_vector = sems("job_done out_scalar out_vector")
        scalar_chain, vector_chain, pool_chain = sems("scalar_chain vector_chain pool_chain")
        cs_ready, cb_ready, ssq_ready, std_ready, xn_ready = sems("cs_ready cb_ready ssq_ready std_ready xn_ready")
        pads_zero, pooled, gate_in, neg_abs, softplus, b_ready = sems("pads_zero pooled gate_in neg_abs softplus b_ready")
        exp_ready, qe_ready, kd_ready, att_zero = sems("exp_ready qe_ready kd_ready att_zero")
        sq_ready, cat_ready, x1_ready, h2_ready, chosen, routed = sems("sq_ready cat_ready x1_ready h2_ready chosen routed")
        g2_saved, moe_init = sems("g2_saved moe_init")
        rank_cols, p_ready, gath, xg_ready, pt_psum, pt_ready, w_ready = sems(
            "rank_cols onehot_ready gathered xg_ready pt_psum pt_ready w_ready")
        a_done, sil_ready, hid_ready, t_done, hidt_ready = sems(
            "up_done sil_ready hid_ready hid_transposed hidt_ready")
        y_done, yh_ready, yl_ready, c_done, acc_done = sems("down_done yh_ready yl_ready combined acc_done")
        extra, extra_scalar, extra_vector = sems("extra_step extra_scalar extra_vector")
        x1_half, tail_in, fin_mul, fin_sum, fin_ssq, fin_std, fin_rec, fin, stored = sems(
            "x1_half tail_in fin_mul fin_sum fin_ssq fin_std fin_rec fin stored")

        block = ctx.enter_context(nc.Block())

        w_mod, w_in, w_out = A["w_mod"][0], A["w_in"][0], A["w_out"][0]
        def rows(w):
            return w.rearrange("(k p) n -> p k n", p=P)

        def unit(slot, k):
            return ring[:, slot, :].rearrange("p (k n) -> p k n", k=k)

        def pre_source(n):
            name = STREAM[n]
            if name[0] == "m":
                i = int(name[1:])
                return rows(w_mod)[:, :, i * 512:(i + 1) * 512]
            if name[:2] == "wo":
                i = int(name[2:])
                return rows(w_out)[:, :, i * 512:(i + 1) * 512]
            i = dict(u=0, qk=1, v=2, g=3)[name]
            return rows(w_in)[:, :, i * 512:(i + 1) * 512]

        w1_r = A["w1"][0].rearrange("e (k p) n -> p e k n", p=P)
        w3_r = A["w3"][0].rearrange("e (k p) n -> p e k n", p=P)
        w2_r = A["w2"][0].rearrange("e (k p) n -> p e k n", p=P)

        def landed_at(n, it):
            slot = n % SLOTS
            return 16 * ((3 if slot < PRE_SLOTS else 0) + n // SLOTS + 1) + 16 * 3 * it

        @block.sync
        def _(sp):
            for n in range(PRE_UNITS):
                slot = n % PRE_SLOTS
                if n >= PRE_SLOTS:
                    sp.wait_ge(job_done, JOB[LAST_USE[n - PRE_SLOTS]] + 1)
                sp.dma_start(unit(slot, KD), pre_source(n)).then_inc(landed[slot], 16)

            def expert_unit(n, it):
                slot = n % SLOTS
                pair, k = n // UPP, n % UPP
                e = 2 * (PPI * it + pair) + k % 2
                w, kk = ((w1_r, KD), (w3_r, KD), (w2_r, KF))[k // 2]
                src = w[:, bass.ds(e, 1), :, :].rearrange("p e k n -> p (e k) n")
                sp.dma_start(unit(slot, kk), src).then_inc(landed[slot], 16)

            for n in range(SLOTS):
                if n < PRE_SLOTS:
                    sp.wait_ge(job_done, JOB[LAST_USE[PRE_UNITS - PRE_SLOTS + n]] + 1)
                elif n == PRE_SLOTS:
                    sp.wait_ge(routed, 1)
                    sp.wait_ge(job_done, len(JOBS))
                    sp.wait_ge(out_vector, len(OUT_VECTOR))
                    sp.wait_ge(g2_saved, 16)
                expert_unit(n, 0)
            per = UPP * PPI

            def slot_used_up(n, it):
                pair, k = (n - SLOTS) // UPP, (n - SLOTS) % UPP
                if k < 4:
                    sp.wait_ge(t_done, PPI * it + (pair + 1))
                else:
                    sp.wait_ge(y_done, 2 * PPI * it + (2 * pair + 2 + Y_AHEAD))

            with sp.Fori(0, ITERS - 1) as it:
                for n in range(SLOTS, SLOTS + per):
                    slot_used_up(n, it)
                    expert_unit(n, it)
            for n in range(SLOTS, per):
                slot_used_up(n, ITERS - 1)
                expert_unit(n, ITERS - 1)
            sp.wait_ge(gath, 2 * (PAIRS + 1))
            sp.wait_ge(pt_psum, PAIRS + 1)
            sp.dma_start(mid[:, 0:D], scratch.to_broadcast([P, D])).then_inc(tail_in, 16)
            sp.dma_start(mid[:, D:2 * D], A["final_g"].rearrange("(a n) -> a n", a=1).to_broadcast([P, D])).then_inc(tail_in, 16)
            out_r = out[0].rearrange("(t p) n -> p t n", p=P)
            for t in range(NT):
                sp.wait_ge(fin, t + 1)
                sp.dma_start(out_r[:, t, :], acc[:, t, :]).then_inc(stored, 16)
            sp.wait_ge(stored, 16 * NT)

        def full(eng, name):
            eng.wait_ge(job_done, JOB[name] + 1)
            return bank[JOB[name] % 8]

        def read_out(eng, name):
            if name in OUT_SCALAR:
                eng.wait_ge(out_scalar, OUT_SCALAR.index(name) + 1)
            else:
                eng.wait_ge(out_vector, OUT_VECTOR.index(name) + 1)

        @block.tensor
        def _(pe):
            mm = nc.tensor.matmul
            todo = iter(JOBS)

            def start(name):
                assert next(todo) == name, name
                j = JOB[name]
                if j >= 8:
                    read_out(pe, JOBS[j - 8])
                return bank[j % 8]

            def slot_in(name, k=KD):
                n = SU[name]
                pe.wait_ge(landed[n % PRE_SLOTS], 16 * (n // PRE_SLOTS + 1))
                return unit(n % PRE_SLOTS, k)

            def mod_rows(i):
                b = start(f"mr{i}")
                w = slot_in(f"m{i}")
                for k in range(KD):
                    j = k % 4
                    last = mm(b[32 * j:32 * j + 32, :], cb[:, k, :], w[:, k, :], start=k < 4, stop=k >= 4,
                              tile_position=(0, 32 * j), skip_group_check=True)
                last.then_inc(job_done, 1)

            pe.wait_ge(cb_ready, 1)
            for i in range(4):
                mod_rows(i)
            b = start("mcol")
            read_out(pe, "mr3")
            pe.wait_ge(tmp_in, 16)
            for i in range(16):
                last = mm(b[:, i:i + 1], modr[:, i * P:(i + 1) * P], sel[:, 0:1], start=True, stop=True)
            last.then_inc(job_done, 1)
            for k in range(KD):
                b = start(f"xT{k}")
                if k == 0:
                    pe.wait_ge(xn_ready, NT)
                    pe.wait_ge(keep_in, 64)
                for t in range(NT):
                    last = nc.tensor.transpose(b[:, t * P:(t + 1) * P], xn[:, t, k * P:(k + 1) * P], ident)
                last.then_inc(job_done, 1)
            b = start("r")
            pe.wait_ge(small_in, 16 * 4)
            for k in range(KD):
                read_out(pe, f"xT{k}")
                last = mm(b[0:2 * RANK, :], wr[:, k, :], h_t[:, k, :], start=k == 0, stop=k == KD - 1)
            last.then_inc(job_done, 1)

            def project_t(name, w, c0):
                b = start(name)
                for k in range(KD):
                    last = mm(b[:, :], w[:, k, c0:c0 + P], h_t[:, k, :], start=k == 0, stop=k == KD - 1)
                last.then_inc(job_done, 1)

            w = slot_in("u")
            for i in range(4):
                project_t(f"u{i}", w, i * P)
            read_out(pe, "r")
            for i in range(4):
                b = start(f"gk{i}")
                mm(b[:, :], wup[:, i // 2, (i % 2) * P:(i % 2 + 1) * P], r_t, start=True, stop=True).then_inc(job_done, 1)
            w = slot_in("qk")
            for i, name in enumerate(("q0", "q1", "k0", "k1")):
                project_t(name, w, i * P)
            for g in range(4):
                b = start(f"yp{g}")
                pe.wait_ge(pooled, g + 1)
                o, left, _ = POOL_AT[g]
                mm(b[:, :], wpool[:, g, :], up[:, o + left:o + left + S], start=True, stop=True).then_inc(job_done, 1)
            w = slot_in("v")
            for t in range(NT):
                b = start(f"v{t}")
                for k in range(KD):
                    last = mm(b[:, :], h_t[:, k, t * P:(t + 1) * P], w[:, k, :], start=k == 0, stop=k == KD - 1)
                last.then_inc(job_done, 1)
            w = slot_in("g")
            for i in range(4):
                project_t(f"g{i}", w, i * P)
            for d in range(2):
                for h in range(HEADS):
                    b = start(f"att{d}{h}")
                    pe.wait_ge(qe_ready, 4)
                    hp, pr = DK * (h % 2), h // 2
                    for t in range(NT):
                        c = slice(t * P, (t + 1) * P)
                        last = mm(b[:, c], ke[hp:hp + DK, d, pr, c], qe[hp:hp + DK, d, pr, c], start=True, stop=True)
                    last.then_inc(job_done, 1)
            for d in range(2):
                for pr in range(2):
                    b = start(f"kdt{d}{pr}")
                    pe.wait_ge(kd_ready, 4)
                    for t in range(NT):
                        c = slice(t * P, (t + 1) * P)
                        last = nc.tensor.transpose(b[:, c], kd[:, d, pr, c], ident)
                    last.then_inc(job_done, 1)
            read_out(pe, "v3")
            for d in range(2):
                for pr in range(2):
                    read_out(pe, f"kdt{d}{pr}")
                    for par in range(2):
                        b = start(f"upd{d}{pr}{par}")
                        r = slice(par * CHUNK, (par + 1) * CHUNK)
                        for t in range(NT):
                            for hh in range(2):
                                h = 2 * pr + hh
                                last = mm(b[hh * DK:(hh + 1) * DK, t * P:(t + 1) * P],
                                          kdtok[r, d, pr, t, hh * DK:(hh + 1) * DK],
                                          v_s[r, t, h * DV:(h + 1) * DV], start=True, stop=True)
                        last.then_inc(job_done, 1)
            for h in range(HEADS):
                b = start(f"o{h}")
                hp, pr = DK * (h % 2), h // 2
                read_out(pe, "att13")
                read_out(pe, "upd111")
                for t in range(NT):
                    mm(b[:, t * P:(t + 1) * P], v_s[:, t, h * DV:(h + 1) * DV], att[:, h, t * P:(t + 1) * P],
                       start=True, stop=False)
                    parts = []
                    for ch in (2 * t, 2 * t + 1):
                        if ch > 0:
                            parts.append((0, ch, ch - 1))
                        if ch < NCH - 1:
                            parts.append((1, ch, ch))
                    for n, (d, ch, si) in enumerate(parts):
                        c = slice(ch * CHUNK, (ch + 1) * CHUNK)
                        last = mm(b[:, c], st[d][hp:hp + DK, pr, si, :], qe[hp:hp + DK, d, pr, c],
                                  start=False, stop=n == len(parts) - 1)
                last.then_inc(job_done, 1)
            for h in range(HEADS):
                b = start(f"ss{h}")
                pe.wait_ge(sq_ready, h + 1)
                mm(b[:, :], ones, sq, start=True, stop=True).then_inc(job_done, 1)
            pe.wait_ge(cb_ready, 2)
            for i in range(4, 12):
                mod_rows(i)
                b = start(f"mb{i}")
                read_out(pe, f"mr{i}")
                pe.wait_ge(bias_in, 16)
                mm(b[:, :], sel, mrow[:, i % 2, :], start=True, stop=False)
                mm(b[:, :], ones[0:1, :], bias_row[:, (i - 4) * 512:(i - 3) * 512], start=False, stop=True).then_inc(job_done, 1)
            for hf in range(2):
                w = slot_in(f"wo{hf}")
                for t in range(NT):
                    b = start(f"wo{hf}{t}")
                    read_out(pe, "yp3")
                    pe.wait_ge(cat_ready, HEADS)
                    for k in range(KD):
                        last = mm(b[:, :], cat[:, k, t * P:(t + 1) * P], w[:, k, :], start=k == 0, stop=k == KD - 1)
                    last.then_inc(job_done, 1)
            for t in range(NT):
                for hf in range(2):
                    b = start(f"hT{t}{hf}")
                    pe.wait_ge(h2_ready, t + 1)
                    for j in range(4):
                        k = 4 * hf + j
                        last = nc.tensor.transpose(b[:, j * P:(j + 1) * P], h2[:, t, k * P:(k + 1) * P], ident)
                    last.then_inc(job_done, 1)
            b = start("lg")
            for t in range(NT):
                read_out(pe, f"hT{t}1")
                for k in range(KD):
                    last = mm(b[:, t * E_N:(t + 1) * E_N], h2t[:, k, t * P:(t + 1) * P], wrt[:, k, :],
                              start=k == 0, stop=k == KD - 1)
            last.then_inc(job_done, 1)
            b = start("rk")
            pe.wait_ge(chosen, 1)
            for t in range(NT):
                for u in range(t + 1):
                    last = mm(b[:, t * E_N:(t + 1) * E_N], lower if u == t else ones, rt_a[:, u, :],
                              start=u == 0, stop=u == t)
            last.then_inc(job_done, 1)
            b = start("cnt")
            for u in range(NT):
                last = mm(b[:, 0:E_N], ones, rt_a[:, u, :], start=u == 0, stop=u == NT - 1)
            last.then_inc(job_done, 1)
            pe.wait_ge(out_vector, len(OUT_VECTOR))
            pe.wait_ge(out_scalar, len(OUT_SCALAR))

            A1, A3, TB, Y0, Y1, G0, G1, CA = bank
            extra_n = pe.alloc_register("pe_extra_rounds")
            pe.reg_mov(extra_n, 0)

            def gather(buf_ready=None):
                for hf, g in ((0, G0), (1, G1)):
                    for j in range(4):
                        k = 4 * hf + j
                        for t in range(NT):
                            last = mm(g[:, j * P:(j + 1) * P], h2[:, t, k * P:(k + 1) * P], onehot[:, t, :],
                                      start=t == 0, stop=t == NT - 1)
                    if buf_ready is not None:
                        last.then_inc(buf_ready, 1)

            def slots_to_partitions():
                for t in range(NT):
                    nc.tensor.transpose(CA[:, t * P:(t + 1) * P], onehot[:, t, :], ident)
                for e in range(2):
                    for t in range(NT):
                        last = mm(A1[e * CAP:(e + 1) * CAP, 0:1], onehot[:, t, e * CAP:(e + 1) * CAP],
                                  gw_pair[:, t, e:e + 1], start=t == 0, stop=t == NT - 1)
                return last

            def up_products(n0, xb, done=None, wait=None):
                for w, bk in ((0, A1), (1, A3)):
                    if wait is not None:
                        for e in range(2):
                            n = n0 + 2 * w + e
                            pe.wait_ge(landed[n % SLOTS], wait(n))
                    for k in range(KD):
                        for e in range(2):
                            n = n0 + 2 * w + e
                            last = mm(bk[e * CAP:(e + 1) * CAP, :], xb[:, k, e * CAP:(e + 1) * CAP],
                                      unit(n % SLOTS, KD)[:, k, :], start=k == 0, stop=k == KD - 1)
                    if done is not None:
                        last.then_inc(done, 1)
                return last

            def down_products(n0, done=None):
                for hf, bk in ((0, Y0), (1, Y1)):
                    for k in range(KF):
                        for e in range(2):
                            n = n0 + 4 + e
                            last = mm(bk[e * CAP:(e + 1) * CAP, :], hid_t[:, k, e * CAP:(e + 1) * CAP],
                                      unit(n % SLOTS, KF)[:, k, hf * 512:(hf + 1) * 512],
                                      start=k == 0, stop=k == KF - 1)
                    if done is not None:
                        last.then_inc(done, 1)
                return last

            def combine_group(g, pt):
                t, hf = g // 2, g % 2
                bk = CA if g % 2 == 0 else TB
                c = slice(hf * 512, (hf + 1) * 512)
                mm(bk[:, :], slot_tok[:, pt, t * P:(t + 1) * P], y_hi[:, c], start=True, stop=False)
                return mm(bk[:, :], slot_tok[:, pt, t * P:(t + 1) * P], y_lo[:, c], start=False, stop=True)

            def combine(p, pt):
                for g in range(8):
                    if g == 0:
                        pe.wait_ge(yh_ready, 2 * p + 2)
                        pe.wait_ge(yl_ready, 2 * p + 2)
                        pe.wait_ge(pt_ready, p + 2)
                    elif g == 1:
                        pe.wait_ge(hidt_ready, p + 1)
                    else:
                        pe.wait_ge(acc_done, 8 * p + (g - 1))
                    combine_group(g, pt).then_inc(c_done, 1)

            def next_gather(q, first=False):
                pe.wait_ge(p_ready, q + 1)
                if not first:
                    pe.wait_ge(xg_ready, 2 * q)
                gather(gath)
                if not first:
                    pe.wait_ge(acc_done, 8 * q)
                    pe.wait_ge(sil_ready, q)
                slots_to_partitions().then_inc(pt_psum, 1)

            pe.wait_ge(moe_init, 2)
            next_gather(0, first=True)
            with pe.Fori(0, ITERS) as it:
                for j in range(PPI):
                    p = it * PPI + j
                    n0 = UPP * j
                    pe.wait_ge(xg_ready, 2 * p + 2)
                    pe.wait_ge(w_ready, p + 1)
                    pe.wait_ge(hid_ready, p + 1)
                    up_products(n0, xg[:, j % 2], a_done, lambda n, it=it: landed_at(n, it))
                    combine(p, (j + 1) % 2)
                    most = pe.value_load(count_i[0:1, bass.ds(p, 1)], min_val=0, max_val=S)
                    with pe.If(most > CAP):
                        with pe.Fori(1, ROUNDS) as r:
                            with pe.If(most > r * CAP):
                                b0 = pe.snap(extra_n) * EXTRA_STEPS
                                pe.wait_ge(hid_ready, p + 2)
                                pe.wait_ge(acc_done, 8 * p + 8)
                                for e in range(2):
                                    n = n0 + 4 + e
                                    pe.wait_ge(landed[n % SLOTS], landed_at(n, it))
                                pe.wait_ge(extra, b0 + 1)
                                gather()
                                slots_to_partitions().then_inc(extra, 1)
                                pe.wait_ge(extra, b0 + 3)
                                up_products(n0, xg[:, (j + 1) % 2]).then_inc(extra, 1)
                                pe.wait_ge(extra, b0 + 6)
                                for k in range(KF):
                                    last = nc.tensor.transpose(TB[:, k * P:(k + 1) * P],
                                                               onehot[:, k, :], ident)
                                last.then_inc(extra, 1)
                                pe.wait_ge(extra, b0 + 8)
                                down_products(n0).then_inc(extra, 1)
                                for g in range(8):
                                    pe.wait_ge(extra, b0 + 11 + 2 * g)
                                    combine_group(g, (j + 1) % 2).then_inc(extra, 1)
                                pe.wait_ge(extra, b0 + 27)
                                pe.reg_add(extra_n, extra_n, 1)
                    pe.wait_ge(hid_ready, p + 2)
                    pe.wait_ge(acc_done, 8 * p + 8)
                    for k in range(KF):
                        last = nc.tensor.transpose(TB[:, k * P:(k + 1) * P], hid[:, k * P:(k + 1) * P], ident)
                    last.then_inc(t_done, 1)
                    next_gather(p + 1)
                    pe.wait_ge(hidt_ready, p + 2)
                    pe.wait_ge(yl_ready, 2 * p + 2)
                    pe.wait_ge(yh_ready, 2 * p + 2)
                    for e in range(2):
                        n = n0 + 4 + e
                        pe.wait_ge(landed[n % SLOTS], landed_at(n, it))
                    down_products(n0, y_done)
            combine(PAIRS, (PAIRS + 1) % 2)

        @block.scalar
        def _(act):
            a = nc.scalar.activation
            n_chain = [0]

            def link(ins):
                n_chain[0] += 1
                ins.then_inc(scalar_chain, 1)
                act.wait_ge(scalar_chain, n_chain[0])

            x_r = A["x"][0].rearrange("(t p) n -> p t n", p=P)
            act.dma_start(cols, A["cols"]).then_inc(cols_in, 16)
            for t in range(NT):
                act.dma_start(x1[:, t, :], x_r[:, t, :]).then_inc(x_in[t], 16)
            act.dma_start(cp, A["const_keep"]).then_inc(keep_in, 16)
            act.dma_start(ct, A["const_tmp"]).then_inc(tmp_in, 16)
            act.dma_start(wrt.rearrange("p k e -> p (k e)"), A["wrt"]).then_inc(keep_in, 16)
            act.dma_start(iota32, A["iota32"]).then_inc(keep_in, 16)
            act.dma_start(b_rt, A["b_router"].rearrange("(a n) -> a n", a=1).to_broadcast([P, E_N])).then_inc(keep_in, 16)

            act.wait_ge(cols_in, 16)
            a(cs, col["c"], ACT.Silu).then_inc(cs_ready, 1)
            for t in range(NT):
                act.wait_ge(x_in[t], 16)
                a(xn[:, t, :], x1[:, t, :], ACT.Square, accum_out=ssq[:, t:t + 1]).then_inc(ssq_ready, 1)
            act.wait_ge(ssq_ready, NT)
            a(rstd, ssq, ACT.Sqrt, bias=col["eps"], scale=1.0 / D).then_inc(std_ready, 1)
            act.dma_start(wr.rearrange("p k c -> p (k c)"), A["wr"]).then_inc(small_in, 16)
            act.dma_start(wpool.rearrange("p k c -> p (k c)"), A["wpool"]).then_inc(small_in, 16)
            act.dma_start(masks, A["masks"]).then_inc(small_in, 16)
            act.dma_start(wup.rearrange("p d c -> p (d c)"), A["wup"]).then_inc(small_in, 16)
            for i in range(4):
                b = full(act, f"mr{i}")
                nc.scalar.copy(modr[:, i * 512:(i + 1) * 512], b[:, :]).then_inc(out_scalar, 1)
            read_out(act, "mcol")
            for k in range(0, KD, 2):
                b = full(act, f"xT{k}")
                a(h_t[:, k, :], b[:, :], ACT.Identity, bias=modc[:, k:k + 1], scale=modc[:, 8 + k:9 + k]).then_inc(out_scalar, 1)
            b = full(act, "r")
            nc.scalar.copy(r_t, b[0:2 * RANK, :]).then_inc(out_scalar, 1)
            act.wait_ge(pads_zero, 1)
            for g in range(4):
                b = full(act, f"u{g}")
                o, left, _ = POOL_AT[g]
                nc.scalar.copy(up[:, o + left:o + left + S], b[:, :]).then_inc(out_scalar, 1)
            for i in range(4):
                b = full(act, f"gk{i}")
                a(la[:, i // 2, i % 2, :], b[:, :], ACT.Identity, bias=col["bgk"][:, i:i + 1]).then_inc(out_scalar, 1)
            for i, name in enumerate(("q0", "q1", "k0", "k1")):
                b = full(act, name)
                dst = (q_s, q_s, k_s, k_s)[i][:, i % 2, :]
                a(dst, b[:, :], ACT.Copy, scale=DK ** -0.5 if i < 2 else 1.0).then_inc(out_scalar, 1)
            for i in range(4):
                act.wait_ge(neg_abs, i + 1)
                link(a(bb[:, i // 2, i % 2, :], bb[:, i // 2, i % 2, :], ACT.Exp))
                a(bb[:, i // 2, i % 2, :], bb[:, i // 2, i % 2, :], ACT.Ln, bias=1.0).then_inc(softplus, 1)
            for g in range(4):
                b = full(act, f"yp{g}")
                a(cat[:, g, :], b[:, :], ACT.Copy, scale=col["pscale"][:, g:g + 1]).then_inc(out_scalar, 1)
            act.wait_ge(b_ready, 4)
            act.wait_ge(job_done, JOB["g3"] + 1)
            for i in range(4):
                d, pr = i // 2, i % 2
                a(qe[:, d, pr, :], bb[:, d, pr, :], ACT.Exp, scale=1.0 / GATE_NORM).then_inc(exp_ready, 1)
                a(ke[:, d, pr, :], bb[:, d, pr, :], ACT.Exp, scale=-1.0 / GATE_NORM).then_inc(exp_ready, 1)
                whole = bb[:, d, pr, :].rearrange("p (c n) -> p c n", n=CHUNK)[:, :, (CHUNK - 1) if d == 0 else 0]
                a(decay[:, i, :], whole, ACT.Exp, scale=1.0 / GATE_NORM).then_inc(exp_ready, 1)
            act.wait_ge(pooled, 4)
            act.wait_ge(job_done, JOB["yp3"] + 1)
            for h in range(HEADS):
                b = full(act, f"g{h}")
                a(g_s[:, h, :], b[:, :], ACT.Silu).then_inc(out_scalar, 1)
            act.wait_ge(kd_ready, 4)
            for i in range(4):
                b = full(act, f"kdt{i // 2}{i % 2}")
                nc.scalar.copy(kdtok[:, i // 2, i % 2, :, :].rearrange("p t c -> p (t c)"), b[:, :]).then_inc(out_scalar, 1)
            for h in range(HEADS):
                b = full(act, f"o{h}")
                if h:
                    act.wait_ge(job_done, JOB[f"ss{h - 1}"] + 1)
                a(sq, b[:, :], ACT.Square).then_inc(sq_ready, 1)
                b2 = full(act, f"ss{h}")
                if h:
                    read_out(act, f"o{h - 1}")
                a(rst, b2[:, :], ACT.Sqrt, bias=col["eps"], scale=1.0 / DV).then_inc(out_scalar, 1)
            for i in range(4, 12):
                b = full(act, f"mr{i}")
                if i >= 6:
                    act.wait_ge(job_done, JOB[f"mb{i - 2}"] + 1)
                nc.scalar.copy(mrow[:, i % 2, :], b[:, :]).then_inc(out_scalar, 1)
            for t in range(NT):
                act.wait_ge(x1_ready, t + 1)
                a(h2[:, t, :], x1[:, t, :], ACT.Square, accum_out=ssq[:, t:t + 1]).then_inc(ssq_ready, 1)
                act.wait_ge(ssq_ready, NT + t + 1)
                a(rstd[:, t:t + 1], ssq[:, t:t + 1], ACT.Sqrt, bias=col["eps"], scale=1.0 / D).then_inc(std_ready, 1)
            for t in range(NT):
                for hf in range(2):
                    b = full(act, f"hT{t}{hf}")
                    dst = h2t[:, 4 * hf:4 * hf + 4, t * P:(t + 1) * P]
                    nc.scalar.copy(dst, b[:, :].rearrange("p (k t) -> p k t", k=4)).then_inc(out_scalar, 1)
            b = full(act, "lg")
            a(rt_s.rearrange("p t e -> p (t e)"), b[:, 0:NT * E_N], ACT.Sigmoid).then_inc(out_scalar, 1)

            A1, A3, TB, Y0, Y1, G0, G1, CA = bank
            extra_n = act.alloc_register("act_extra_rounds")
            act.reg_mov(extra_n, 0)

            def take_gathered(buf, gate, done, first_wait=None):
                for hf, g in ((0, G0), (1, G1)):
                    if gate is not None:
                        act.wait_ge(gath, gate + hf)
                    nc.scalar.copy(xg[:, buf, 4 * hf:4 * hf + 4, :].rearrange("p k s -> p (k s)"), g[:, :]).then_inc(done, 1)

            def gathered(q, buf, first=False):
                if not first:
                    act.wait_ge(a_done, 2 * q)
                take_gathered(buf, 2 * q + 1, xg_ready)
                act.wait_ge(pt_psum, q + 1)
                if not first:
                    act.wait_ge(c_done, 8 * q)
                nc.scalar.copy(slot_tok[:, buf, :], CA[:, :]).then_inc(pt_ready, 1)
                if not first:
                    act.wait_ge(yl_ready, 2 * q)
                nc.scalar.copy(w_slot[:, buf:buf + 1], A1[:, 0:1]).then_inc(w_ready, 1)

            def take_down(buf, done, gate=None):
                for hf, bk in ((0, Y0), (1, Y1)):
                    if gate is not None:
                        act.wait_ge(y_done, gate + hf)
                    a(y_hi[:, hf * 512:(hf + 1) * 512], bk[:, :], ACT.Copy, scale=w_slot[:, buf:buf + 1]).then_inc(done, 1)

            act.wait_ge(moe_init, 2)
            gathered(0, 0, first=True)
            with act.Fori(0, ITERS) as it:
                for j in range(PPI):
                    p = it * PPI + j
                    act.wait_ge(a_done, 2 * p + 1 + A_AHEAD)
                    act.wait_ge(hid_ready, p + 1)
                    a(sil, A1[:, :], ACT.Silu).then_inc(sil_ready, 1)
                    most = act.value_load(count_i[0:1, bass.ds(p, 1)], min_val=0, max_val=S)
                    with act.If(most > CAP):
                        with act.Fori(1, ROUNDS) as r:
                            with act.If(most > r * CAP):
                                done = act.snap(extra_n)
                                b0 = done * EXTRA_STEPS
                                nb = (j + 1) % 2
                                act.wait_ge(extra, b0 + 2)
                                take_gathered(nb, None, extra_scalar)
                                nc.scalar.copy(slot_tok[:, nb, :], CA[:, :]).then_inc(extra_scalar, 1)
                                nc.scalar.copy(w_slot[:, nb:nb + 1], A1[:, 0:1]).then_inc(extra, 1)
                                act.wait_ge(extra, b0 + 4)
                                a(sil, A1[:, :], ACT.Silu).then_inc(extra, 1)
                                act.wait_ge(extra, b0 + 7)
                                nc.scalar.copy(hid_t.rearrange("p k s -> p (k s)"), TB[:, :]).then_inc(extra, 1)
                                act.wait_ge(extra, b0 + 9)
                                a(y_hi[:, 0:512], Y0[:, :], ACT.Copy, scale=w_slot[:, nb:nb + 1]).then_inc(extra_scalar, 1)
                                a(y_hi[:, 512:1024], Y1[:, :], ACT.Copy, scale=w_slot[:, nb:nb + 1]).then_inc(extra, 1)
                                act.reg_add(extra_n, extra_n, 1)
                    act.wait_ge(t_done, p + 1)
                    act.wait_ge(y_done, 2 * p + Y_AHEAD)
                    nc.scalar.copy(hid_t.rearrange("p k s -> p (k s)"), TB[:, :]).then_inc(hidt_ready, 1)
                    gathered(p + 1, (j + 1) % 2)
                    act.wait_ge(c_done, 8 * p + 8)
                    act.wait_ge(w_ready, p + 1)
                    take_down(j % 2, yh_ready, 2 * p + 1 + Y_AHEAD)
            for t in range(NT):
                act.wait_ge(fin_sum, t + 1)
                a(x1[:, t, :], acc[:, t, :], ACT.Square, accum_out=ssq[:, t:t + 1]).then_inc(fin_ssq, 1)
                act.wait_ge(fin_ssq, t + 1)
                a(rstd[:, t:t + 1], ssq[:, t:t + 1], ACT.Sqrt, bias=col["eps"], scale=1.0 / D).then_inc(fin_std, 1)

        @block.vector
        def _(dve):
            v = nc.vector
            n_chain = [0]

            def link(ins):
                n_chain[0] += 1
                ins.then_inc(vector_chain, 1)
                dve.wait_ge(vector_chain, n_chain[0])

            dve.wait_ge(cs_ready, 1)
            v.tensor_copy(cb, cs.unsqueeze(2).to_broadcast([P, KD, 32])).then_inc(cb_ready, 1)
            dve.wait_ge(std_ready, 1)
            link(v.reciprocal(rstd, rstd))
            for t in range(NT):
                v.tensor_scalar(xn[:, t, :], x1[:, t, :], rstd[:, t:t + 1], None, ALU.mult).then_inc(xn_ready, 1)
            b = full(dve, "mcol")
            dve.wait_ge(cols_in, 16)
            link(v.tensor_tensor(modc, b[:, 0:16], col["bmod"], ALU.add))
            v.tensor_scalar(modc[:, 8:16], modc[:, 8:16], 1.0, None, ALU.add).then_inc(out_vector, 1)
            read_out(dve, "mcol")
            for k in range(1, KD, 2):
                b = full(dve, f"xT{k}")
                v.tensor_scalar(h_t[:, k, :], b[:, :], modc[:, 8 + k:9 + k], modc[:, k:k + 1], ALU.mult, ALU.add).then_inc(out_vector, 1)
            for i in range(4):
                read_out(dve, f"gk{i}")
                y, t = la[:, i // 2, i % 2, :], bb[:, i // 2, i % 2, :]
                v.scalar_tensor_tensor(t, y, -1.0, y, ALU.mult, ALU.min).then_inc(neg_abs, 1)
            dve.wait_ge(tmp_in, 16)
            for i in range(4):
                dve.wait_ge(softplus, i + 1)
                y, t = la[:, i // 2, i % 2, :], bb[:, i // 2, i % 2, :]
                link(v.scalar_tensor_tensor(y, y, 0.0, t, ALU.min, ALU.subtract))
                if i // 2 == 0:
                    ins = v.tensor_tensor_scan(t, reset, y, 0.0, ALU.mult, ALU.add)
                else:
                    ins = v.tensor_tensor_scan(t[:, ::-1], reset, y[:, ::-1], 0.0, ALU.mult, ALU.add)
                ins.then_inc(b_ready, 1)
            for t in range(NT):
                b = full(dve, f"v{t}")
                v.tensor_copy(v_s[:, t, :], b[:, :]).then_inc(out_vector, 1)
            read_out(dve, "k1")
            for i in range(4):
                d, pr = i // 2, i % 2
                dve.wait_ge(exp_ready, 3 * i + 3)
                v.tensor_tensor(qe[:, d, pr, :], qe[:, d, pr, :], q_s[:, pr, :], ALU.mult)
                v.tensor_tensor(ke[:, d, pr, :], ke[:, d, pr, :], k_s[:, pr, :], ALU.mult).then_inc(qe_ready, 1)
                dve.wait_ge(qe_ready, i + 1)
                v.tensor_tensor(kd[:, d, pr, :].rearrange("p (c n) -> p c n", n=CHUNK),
                                ke[:, d, pr, :].rearrange("p (c n) -> p c n", n=CHUNK),
                                decay[:, i, :].unsqueeze(2).to_broadcast([P, NCH, CHUNK]), ALU.mult).then_inc(kd_ready, 1)
            dve.wait_ge(att_zero, 1)
            dve.wait_ge(small_in, 64)
            for d in range(2):
                for h in range(HEADS):
                    b = full(dve, f"att{d}{h}")
                    if d:
                        read_out(dve, f"att0{h}")
                    m = masks[:, d * P:(d + 1) * P].bitcast(I32).unsqueeze(1).to_broadcast([P, NT, P])
                    v.copy_predicated(att[:, h, :].rearrange("p (t i) -> p t i", t=NT), m,
                                      b[:, :].rearrange("p (t i) -> p t i", t=NT)).then_inc(out_vector, 1)
            for d in range(2):
                for pr in range(2):
                    full(dve, f"upd{d}{pr}0")
                    full(dve, f"upd{d}{pr}1")

                    def upd(n):
                        bk = bank[JOB[f"upd{d}{pr}{n % 2}"] % 8]
                        return bk[:, (n // 2) * P:(n // 2 + 1) * P]
                    order = list(range(NCH - 1)) if d == 0 else list(range(NCH - 1, 0, -1))
                    for i, n in enumerate(order):
                        s_out = st[d][:, pr, n if d == 0 else n - 1, :]
                        if i == 0:
                            ins = v.tensor_copy(s_out, upd(n))
                        else:
                            s_in = st[d][:, pr, n - 1 if d == 0 else n, :]
                            ins = v.scalar_tensor_tensor(s_out, s_in, decay[:, 2 * d + pr, n:n + 1], upd(n), ALU.mult, ALU.add)
                        if i < NCH - 2:
                            link(ins)
                        else:
                            ins.then_inc(out_vector, 2)
            for h in range(HEADS):
                b = full(dve, f"o{h}")
                read_out(dve, f"ss{h}")
                link(v.reciprocal(rst, rst))
                v.scalar_tensor_tensor(cat[:, 4 + h, :], b[:, :], col["ng"], rst, ALU.mult, ALU.mult).then_inc(out_vector, 1)
                read_out(dve, f"o{h}")
                v.tensor_tensor(cat[:, 4 + h, :], cat[:, 4 + h, :], g_s[:, h, :], ALU.mult).then_inc(cat_ready, 1)
            v.tensor_copy(cb, cs.unsqueeze(2).to_broadcast([P, KD, 32])).then_inc(cb_ready, 1)
            dve.wait_ge(cat_ready, HEADS)
            for i in range(4, 12):
                b = full(dve, f"mb{i}")
                dst = (g1b, sh2b, sc2b, g2b)[(i - 4) // 2][:, (i % 2) * 512:(i % 2 + 1) * 512]
                v.tensor_scalar(dst, b[:, :], 1.0 if i in (8, 9) else 0.0, None, ALU.add).then_inc(out_vector, 1)
            read_out(dve, "mb11")
            for hf in range(2):
                for t in range(NT):
                    b = full(dve, f"wo{hf}{t}")
                    c = slice(hf * 512, (hf + 1) * 512)
                    tmp = sq if t % 2 == 0 else rst
                    v.tensor_tensor(tmp, b[:, :], g1b[:, c], ALU.mult).then_inc(out_vector, 1)
                    read_out(dve, f"wo{hf}{t}")
                    ins = v.tensor_tensor(x1[:, t, c], x1[:, t, c], tmp, ALU.add)
                    if hf == 1:
                        ins.then_inc(x1_ready, 1)
                    else:
                        ins.then_inc(x1_half, 1)
                        dve.wait_ge(x1_half, t + 1)
            for t in range(NT):
                dve.wait_ge(std_ready, 2 + t)
                link(v.reciprocal(rstd[:, t:t + 1], rstd[:, t:t + 1]))
                link(v.scalar_tensor_tensor(h2[:, t, :], x1[:, t, :], rstd[:, t:t + 1], sc2b, ALU.mult, ALU.mult))
                v.tensor_tensor(h2[:, t, :], h2[:, t, :], sh2b, ALU.add).then_inc(h2_ready, 1)

            dve.wait_ge(keep_in, 64)
            read_out(dve, "lg")
            gview = lambda z: z.rearrange("p t (g e) -> p t g e", g=G_N)
            big4 = [P, NT, G_N, EPG]
            iota_g = iota32[:, 0:G_N].unsqueeze(1).to_broadcast([P, NT, G_N])
            iota_e = iota32[:, 0:EPG].unsqueeze(1).to_broadcast([P, NT, EPG])
            link(v.tensor_tensor(rt_sel, rt_s, b_rt.unsqueeze(1).to_broadcast([P, NT, E_N]), ALU.add))
            for t in range(NT):
                for g in range(G_N):
                    ins = v.max(rt_srt[:, t, g, :], rt_sel[:, t, g * EPG:(g + 1) * EPG])
            link(ins)
            link(v.tensor_tensor(rt_gs, rt_srt[:, :, :, 0], rt_srt[:, :, :, 1], ALU.add))

            def first_of(onehot_out, values, target, n, iota_n, taken=None):
                link(v.tensor_tensor(onehot_out, values, target.unsqueeze(2).to_broadcast([P, NT, n]), ALU.is_equal))
                link(v.scalar_tensor_tensor(onehot_out, onehot_out, -100.0, iota_n, ALU.mult, ALU.add))
                if taken is not None:
                    link(v.scalar_tensor_tensor(onehot_out, taken, 1000.0, onehot_out, ALU.mult, ALU.add))
                link(v.tensor_reduce(rt_m, onehot_out, AX_X, ALU.min))
                link(v.tensor_tensor(onehot_out, onehot_out, rt_m.unsqueeze(2).to_broadcast([P, NT, n]), ALU.is_equal))

            link(v.tensor_reduce(rt_top, rt_gs, AX_X, ALU.max))
            first_of(rt_goh, rt_gs, rt_top, G_N, iota_g)
            goh4 = rt_goh.unsqueeze(3).to_broadcast(big4)
            link(v.tensor_tensor(gview(rt_tmp), gview(rt_sel), goh4, ALU.mult))
            link(v.tensor_reduce(rt_in, gview(rt_tmp).rearrange("p t g e -> p t e g"), AX_X, ALU.add))
            link(v.tensor_tensor(rt_srt, rt_srt, goh4, ALU.mult))
            link(v.tensor_reduce(rt_t12, rt_srt[:, :, :, 0:2].rearrange("p t g e -> p t e g"), AX_X, ALU.add))
            first_of(rt_oh1, rt_in, rt_t12[:, :, 0], EPG, iota_e)
            first_of(rt_oh2, rt_in, rt_t12[:, :, 1], EPG, iota_e, taken=rt_oh1)
            link(v.tensor_tensor(rt_oh1, rt_oh1, rt_oh2, ALU.add))
            v.tensor_tensor(gview(rt_a), goh4, rt_oh1.unsqueeze(2).to_broadcast(big4), ALU.mult).then_inc(chosen, 1)
            dve.wait_ge(chosen, 1)
            link(v.tensor_tensor(gwt[:, :, 0:E_N], rt_a, rt_s, ALU.mult))
            link(v.tensor_reduce(rt_m, gwt[:, :, 0:E_N], AX_X, ALU.add))
            link(v.reciprocal(rt_m, rt_m))
            link(v.tensor_tensor(gwt[:, :, 0:E_N], gwt[:, :, 0:E_N], rt_m.unsqueeze(2).to_broadcast([P, NT, E_N]), ALU.mult))
            b = full(dve, "rk")
            v.scalar_tensor_tensor(rankm[:, :, 0:E_N], b[:, 0:NT * E_N].rearrange("p (t e) -> p t e", t=NT), 1.0, rt_a,
                                   ALU.add, ALU.mult).then_inc(out_vector, 1)
            read_out(dve, "rk")
            link(v.tensor_scalar(rankm[:, :, 0:E_N], rankm[:, :, 0:E_N], -1.0, None, ALU.add))
            link(v.memset(rankm[:, :, E_N:E_N + 2], -1.0))
            link(v.memset(gwt[:, :, E_N:E_N + 2], 0.0))
            b = full(dve, "cnt")
            v.tensor_reduce(count_f, b[:, 0:E_N].rearrange("p (a e) -> p a e", e=2), AX_X, ALU.max).then_inc(out_vector, 1)
            read_out(dve, "cnt")
            v.tensor_copy(count_i, count_f).then_inc(routed, 1)

            A1, A3, TB, Y0, Y1, G0, G1, CA = bank
            extra_n = dve.alloc_register("dve_extra_rounds")
            dve.reg_mov(extra_n, 0)
            iota8 = iota.unsqueeze(1).to_broadcast([P, NT * 2, CAP])

            def one_hot(q, off, cols_ready, cols_count, done):
                v.tensor_scalar(rank_pair, rankm[:, :, bass.ds(2 * q, 2)], off, None, ALU.add).then_inc(cols_ready, 1)
                v.tensor_copy(gw_pair, gwt[:, :, bass.ds(2 * q, 2)])
                dve.wait_ge(cols_ready, cols_count)
                v.tensor_tensor(onehot.rearrange("p t (e s) -> p (t e) s", e=2),
                                rank_pair.rearrange("p t e -> p (t e)").unsqueeze(2).to_broadcast([P, NT * 2, CAP]),
                                iota8, ALU.is_equal).then_inc(done, 1)

            def low_parts(buf, done, gate_h=None, gate_y=None):
                for hf, bk in ((0, Y0), (1, Y1)):
                    c = slice(hf * 512, (hf + 1) * 512)
                    if gate_h is not None:
                        dve.wait_ge(yh_ready, gate_h + hf)
                    ins = v.scalar_tensor_tensor(y_lo[:, c], bk[:, :], w_slot[:, buf:buf + 1], y_hi[:, c].bitcast(F32),
                                                 ALU.mult, ALU.subtract)
                    if gate_h is not None or hf:
                        ins.then_inc(done, 1)

            def add_group(g):
                t, hf = g // 2, g % 2
                bk = CA if g % 2 == 0 else TB
                c = slice(hf * 512, (hf + 1) * 512)
                return v.tensor_tensor(acc[:, t, c], acc[:, t, c], bk[:, :], ALU.add)

            def add_up(p):
                for g in range(8):
                    dve.wait_ge(c_done, 8 * p + g + 1)
                    add_group(g).then_inc(acc_done, 1)

            for s_, n_ in ((a_done, A_AHEAD), (y_done, Y_AHEAD), (hid_ready, 1), (hidt_ready, 1), (pt_ready, 1),
                           (yh_ready, 2), (yl_ready, 2)):
                dve.sem_inc(s_, n_)
            dve.wait_ge(routed, 1)
            dve.wait_ge(job_done, len(JOBS))
            dve.wait_ge(out_scalar, len(OUT_SCALAR))
            dve.sem_inc(moe_init, 1)
            dve.wait_ge(moe_init, 2)
            one_hot(0, 0.0, rank_cols, 1, p_ready)
            with dve.Fori(0, ITERS) as it:
                for j in range(PPI):
                    p = it * PPI + j
                    dve.wait_ge(a_done, 2 * p + 2 + A_AHEAD)
                    dve.wait_ge(sil_ready, p + 1)
                    v.tensor_tensor(hid, sil, A3[:, :], ALU.mult).then_inc(hid_ready, 1)
                    add_up(p)
                    most = dve.value_load(count_i[0:1, bass.ds(p, 1)], min_val=0, max_val=S)
                    with dve.If(most > CAP):
                        with dve.Fori(1, ROUNDS) as r:
                            with dve.If(most > r * CAP):
                                done = dve.snap(extra_n)
                                b0 = done * EXTRA_STEPS
                                dve.wait_ge(pt_psum, p + 1)
                                nb = (j + 1) % 2
                                one_hot(p, offs[:, bass.ds(r, 1)], extra_vector, done + 1, extra)
                                dve.wait_ge(extra, b0 + 5)
                                v.tensor_tensor(onehot.rearrange("p t s -> p (t s)"), sil, A3[:, :], ALU.mult).then_inc(extra, 1)
                                dve.wait_ge(extra, b0 + 10)
                                low_parts(nb, extra)
                                for g in range(8):
                                    dve.wait_ge(extra, b0 + 12 + 2 * g)
                                    add_group(g).then_inc(extra, 1)
                                dve.wait_ge(extra, b0 + 27)
                                dve.reg_add(extra_n, extra_n, 1)
                    dve.wait_ge(pt_psum, p + 1)
                    one_hot(p + 1, 0.0, rank_cols, p + 2, p_ready)
                    dve.wait_ge(w_ready, p + 1)
                    low_parts(j % 2, yl_ready, 2 * p + 3)
            add_up(PAIRS)
            dve.wait_ge(tail_in, 32)
            dve.wait_ge(acc_done, 8 * PAIRS + 8)
            for t in range(NT):
                v.tensor_tensor(acc[:, t, :], acc[:, t, :], mid[:, 0:D], ALU.mult).then_inc(fin_mul, 1)
                dve.wait_ge(fin_mul, t + 1)
                v.tensor_tensor(acc[:, t, :], acc[:, t, :], x1[:, t, :], ALU.add).then_inc(fin_sum, 1)
            for t in range(NT):
                dve.wait_ge(fin_std, t + 1)
                v.reciprocal(rstd[:, t:t + 1], rstd[:, t:t + 1]).then_inc(fin_rec, 1)
                dve.wait_ge(fin_rec, t + 1)
                v.scalar_tensor_tensor(acc[:, t, :], acc[:, t, :], rstd[:, t:t + 1], mid[:, D:2 * D],
                                       ALU.mult, ALU.mult).then_inc(fin, 1)

        @block.gpsimd
        def _(pool):
            g_ = nc.gpsimd
            n_chain = [0]

            def link(ins):
                n_chain[0] += 1
                ins.then_inc(pool_chain, 1)
                pool.wait_ge(pool_chain, n_chain[0])

            g_.memset(y_hi[:, :].bitcast(F32), 0.0)
            g_.memset(y_lo[:, :].bitcast(F32), 0.0)
            g_.memset(slot_tok[:, 1, :].bitcast(F32), 0.0)
            pool.wait_ge(job_done, JOB["mcol"] + 1)
            g_.memset(up, 0.0).then_inc(pads_zero, 1)
            pool.wait_ge(tmp_in, 16)
            for g, w in enumerate(WINDOWS):
                o, left, ed = POOL_AT[g]
                read_out(pool, f"u{g}")
                src, n, m = up[:, o:o + S + w - 1], S + w - 1, 1
                dst = (ta, tb)
                i = 0
                while m < w:
                    n -= m
                    to = dst[i % 2][:, 0:n]
                    link(g_.tensor_tensor(to, src[:, 0:n], src[:, m:m + n], ALU.add))
                    src, m, i = to, 2 * m, i + 1
                link(g_.tensor_tensor(src[:, 0:left], src[:, 0:left], edge[:, ed:ed + left], ALU.mult))
                if left > 1:
                    link(g_.tensor_tensor(src[:, S - left + 1:S], src[:, S - left + 1:S], edge[:, ed + left:ed + w - 1], ALU.mult))
                u = up[:, o + left:o + left + S]
                link(g_.tensor_scalar(src[:, 0:S], src[:, 0:S], 1.0 / w, None, ALU.mult))
                g_.tensor_tensor(u, src[:, 0:S], u, ALU.subtract).then_inc(pooled, 1)
                pool.wait_ge(pooled, g + 1)
            pool.wait_ge(qe_ready, 4)
            g_.memset(scr[:, 0:2048], 0.0).then_inc(att_zero, 1)
            pool.wait_ge(job_done, JOB["o3"] + 1)
            pool.dma_start(bias_row, A["b_mod"][:, 2 * D:6 * D]).then_inc(bias_in, 16)
            read_out(pool, "mb11")
            pool.dma_start(scratch, g2b[0:1, :]).then_inc(g2_saved, 16)
            g_.memset(big[:, :], 0.0).then_inc(moe_init, 1)


def kernel(**inputs):
    import numpy as _np
    import concourse.bacc as _bacc
    from concourse import mybir as _mybir
    from concourse.bass_utils import run_bass_kernel_spmd as _run

    f32 = _np.float32
    z = {k: _np.asarray(v) for k, v in inputs.items()}
    cp, ct, cm, i32 = constants()

    def columns(v):
        return v.reshape(-1, P).T

    arrays = {n: z[n] for n in ("x", "w_mod", "w_in", "w_out", "w1", "w3", "w2", "b_mod", "b_router", "final_g")}
    arrays["cols"] = _np.concatenate([columns(z["c"][0]), columns(z["b_mod"][0, :2 * D]), columns(z["pool_scale"][0]),
                                      columns(z["b_gk"][0].reshape(-1)), columns(z["gla_norm_g"][0]),
                                      _np.full((P, 1), EPS, f32)], 1)
    arrays["wr"] = z["w_in"][0][:, 2048:].reshape(KD, P, 2 * RANK).transpose(1, 0, 2).reshape(P, -1)
    arrays["wrt"] = z["w_router"].reshape(KD, P, E_N).transpose(1, 0, 2).reshape(P, -1)
    arrays["wpool"] = z["w_pool"][0].transpose(1, 0, 2).reshape(P, -1)
    wup = _np.zeros((2 * RANK, 2, HEADS * DK), f32)
    wup[:RANK, 0], wup[RANK:, 1] = z["w_gk_up"][0, 0], z["w_gk_up"][0, 1]
    arrays["wup"] = wup.reshape(2 * RANK, -1)
    arrays.update(const_keep=cp, const_tmp=ct, masks=cm, iota32=i32)

    nc = _bacc.Bacc("TRN2", target_bir_lowering=False, num_devices=1)
    A = {}
    for n in arrays:
        arrays[n] = _np.ascontiguousarray(arrays[n])
        A[n] = nc.dram_tensor(f"in_{n}", arrays[n].shape, _mybir.dt.from_np(arrays[n].dtype), kind="ExternalInput").ap()
    out = nc.dram_tensor("out_0", (1, S, D), F32, kind="ExternalOutput").ap()
    scratch = nc.dram_tensor("g2_row", (1, D), F32, kind="Internal").ap()
    build(nc, A, out, scratch)
    r = _run(nc, [{f"in_{n}": a for n, a in arrays.items()}], core_ids=[0])
    return r.results[0]["out_0"]
```

```python
from contextlib import ExitStack

import numpy as np

import concourse.bass as bass
from concourse import mybir

F32 = mybir.dt.float32
F32R = mybir.dt.float32r
I32 = mybir.dt.int32
ALU = mybir.AluOpType
ACT = mybir.ActivationFunctionType
AX_X = mybir.AxisListType.X

P = 128
D = 1024
S = 512
KD = D // P
NT = S // P
DG = 512
WINDOWS = (2, 4, 8, 16)
HEADS, DK, DV = 4, 64, 128
RANK = 16
CHUNK = 64
NCH = S // CHUNK
GATE_NORM = 16.0
E_N, G_N, EPG = 32, 4, 8
DFF = 512
KF = DFF // P
EPS = 1e-6
CAP = 64
PAIRS = E_N // 2
ROUNDS = S // CAP
UNIT = 4096
SLOTS = 8
PRE_SLOTS = 4
UPP = 6
PPI = 4
ITERS = PAIRS // PPI
EXTRA_STEPS = 14
A_AHEAD = Y_AHEAD = 2

SC = dict(c=(0, 8), bmod=(8, 24), pscale=(24, 28), bgk=(28, 32), ng=(32, 33), eps=(33, 34))
SC_N = 34
CP = dict(ident=(0, 128), iota=(128, 192), off=(192, 200))
CP_N = 200
CT = dict(reset=(0, 512), ones=(512, 640), sel=(640, 768), lower=(768, 896))
CT_N = 896
CM_N = 256
CE_N = 2 * 26


def pool_offsets():
    out, at, ed = [], 0, 0
    for w in WINDOWS:
        out.append((at, w // 2, ed))
        at += S + w - 1
        ed += w - 1
    return out, at, ed


POOL_AT, POOL_N, EDGE_N = pool_offsets()


def constants():
    r = np.arange(P)
    cp = np.zeros((P, CP_N), np.float32)
    cp[:, 0:128] = np.eye(P)
    cp[:, 128:192] = np.arange(CAP)[None]
    cp[:, 192:200] = -CAP * np.arange(ROUNDS)[None]
    ct = np.zeros((P, CT_N), np.float32)
    ct[:, 0:512] = (np.arange(S) % CHUNK != 0)[None]
    ct[:, 512:640] = 1.0
    ct[0::32, 640:768] = 1.0
    ct[:, 768:896] = r[:, None] < r[None, :]
    cm = np.zeros((P, CM_N), np.float32)
    same = r[:, None] // CHUNK == r[None, :] // CHUNK
    cm[:, 0:128] = same & (r[:, None] <= r[None, :])
    cm[:, 128:256] = same & (r[:, None] > r[None, :])
    ce = np.zeros((P, EDGE_N), np.float32)
    t = np.arange(S)
    for w, (_, _, ed) in zip(WINDOWS, POOL_AT):
        cnt = np.minimum(t - w // 2 + w - 1, S - 1) - np.maximum(t - w // 2, 0) + 1
        f = (w / cnt).astype(np.float32)
        ce[:, ed:ed + w // 2] = f[:w // 2]
        ce[:, ed + w // 2:ed + w - 1] = f[S - (w // 2 - 1):] if w > 2 else 0
    i8 = np.broadcast_to(np.arange(E_N, dtype=np.float32)[None], (P, E_N))
    return cp, np.concatenate([ct, ce], 1), cm, i8


JOBS = ([f"mr{i}" for i in range(4)] + ["mcol"] + [f"xT{k}" for k in range(KD)] + ["r"]
        + [f"u{i}" for i in range(4)] + [f"gk{i}" for i in range(4)]
        + ["q0", "q1", "k0", "k1"] + [f"yp{i}" for i in range(4)]
        + [f"v{i}" for i in range(4)] + [f"g{i}" for i in range(4)]
        + [f"m{a}{i + j}" for i in (4, 6) for a in "rb" for j in range(2)]
        + [f"att{d}{h}" for d in range(2) for h in range(HEADS)]
        + [f"kdt{d}{p}" for d in range(2) for p in range(2)]
        + [f"m{a}{8 + j}" for a in "rb" for j in range(2)]
        + [f"upd{d}{p}{par}" for d in range(2) for p in range(2) for par in range(2)]
        + [f"m{a}{10 + j}" for a in "rb" for j in range(2)]
        + [f"o{h}" for h in range(HEADS)] + [f"ss{h}" for h in range(HEADS)]
        + [f"wo{hf}{t}" for hf in range(2) for t in range(NT)]
        + [f"hT{t}{hf}" for t in range(NT) for hf in range(2)] + ["lg", "rk", "cnt"])
JOB = {n: i for i, n in enumerate(JOBS)}
assert len(JOB) == len(JOBS)
STREAM = (["m0", "m1", "m2", "m3", "u", "qk", "v", "g"] + [f"m{i}" for i in range(4, 12)] + ["wo0", "wo1"])
SU = {n: i for i, n in enumerate(STREAM)}
PRE_UNITS = len(STREAM)
SPLIT = ["u", "qk", "v", "g", "wo0", "wo1"]
DEPTH = 4
LAST_JOB = ["u3", "k1", "v3", "g3", "wo03", "wo13"]
OUT_SCALAR = ([f"mr{i}" for i in range(4)] + [f"xT{k}" for k in range(KD)] + ["r"]
              + [f"u{i}" for i in range(4)] + [f"gk{i}" for i in range(4)] + ["q0", "q1", "k0", "k1"]
              + [f"yp{i}" for i in range(4)] + [f"g{i}" for i in range(4)]
              + [f"mr{i}" for i in range(4, 8)]
              + [f"kdt{d}{p}" for d in range(2) for p in range(2)]
              + [f"mr{i}" for i in range(8, 12)] + [f"ss{h}" for h in range(HEADS)]
              + [f"hT{t}{hf}" for t in range(NT) for hf in range(2)] + ["lg"])
OUT_VECTOR = (["mcol"] + [f"v{i}" for i in range(4)] + [f"mb{i}" for i in range(4, 8)]
              + [f"att{d}{h}" for d in range(2) for h in range(HEADS)] + ["mb8", "mb9"]
              + [f"upd{d}{p}{par}" for d in range(2) for p in range(2) for par in range(2)]
              + ["mb10", "mb11"] + [f"o{h}" for h in range(HEADS)]
              + [f"wo{hf}{t}" for hf in range(2) for t in range(NT)] + ["rk", "cnt"])
assert sorted(OUT_SCALAR + OUT_VECTOR) == sorted(JOBS)
PRE_USES = [len(range(i, PRE_UNITS, PRE_SLOTS)) if i < PRE_SLOTS else 0 for i in range(SLOTS)]


def build(nc, A, out, g2_row, x1_row):
    ctx = ExitStack()
    with ctx:
        def sb(name, shape, dt=F32):
            return ctx.enter_context(nc.sbuf_tensor(name, shape, dt))

        def sem(name):
            return ctx.enter_context(nc.semaphore(name))

        first = (nc.sbuf_base + 63) // 64 * 64
        total = SLOTS * UNIT + 4 * UNIT + 3 * D + 960

        def place(name, at, shape, dt=F32):
            n = 1
            for d_ in shape[1:]:
                n *= d_
            assert at + n <= total
            return nc.alloc_sbuf_tensor_at(name, shape, dt, offset=first + 4 * at)

        assert first + 4 * total <= nc.sbuf_usable_end
        X1, BIG, MID, LOW = (SLOTS * UNIT + i * UNIT for i in range(4))
        YA = SLOTS * UNIT + 4 * UNIT
        ring = place("ring", 0, [P, SLOTS, UNIT])
        x1 = place("x1", X1, [P, NT, D])
        mid = place("mid", MID, [P, UNIT])
        low = place("low", LOW, [P, UNIT])
        big = place("big", BIG, [P, UNIT])
        keep = place("keep", YA + 3 * D, [P, 960])
        h_hi = place("h_hi", BIG, [P, KD, S], F32R)
        h_lo = place("h_lo", 5 * UNIT, [P, KD, S], F32R)
        cat_hi = place("cat_hi", BIG, [P, KD, S], F32R)
        cat_lo = place("cat_lo", 6 * UNIT, [P, KD, S], F32R)
        h2_hi = place("h2_hi", BIG, [P, NT, D], F32R)
        h2_lo = place("h2_lo", X1, [P, NT, D], F32R)
        w_hi = place("w_hi", 4 * UNIT, [P, DEPTH, 512], F32R)
        w_lo = place("w_lo", 4 * UNIT + DEPTH * 512, [P, DEPTH, 512], F32R)
        wr_hi = place("wr_hi", LOW, [P, KD, P], F32R)
        wr_lo = place("wr_lo", LOW + KD * P, [P, KD, P], F32R)
        spread = place("spread", YA, [P, 3 * D])
        h_tmp = spread[:, 0:D].rearrange("p (a t) -> p a t", a=2)
        wr_raw = spread[:, D:2 * D]
        g1b, sc2b, sh2b = (spread[:, i * D:(i + 1) * D] for i in range(3))
        y_hi = place("y_hi", YA, [P, D], F32R)
        extra_rows = place("extra_rows", YA, [P, D])
        y_lo = place("y_lo", YA + D, [P, D], F32R)
        slot_tok = place("slot_tok", YA + 2 * D, [P, 2, S], F32R)
        onehot_t = place("onehot", LOW, [P, NT, P], F32R)
        after = place("after", 4 * UNIT, [P, 2 * UNIT])
        mrow = after[:, 0:1024].rearrange("p (a n) -> p a n", a=2)
        g2row = after[0:1, 1024:2048]
        bias_row = after[0:1, UNIT:2 * UNIT]

        at = [0]

        def take(n):
            at[0] += n
            assert at[0] <= 960
            return keep[:, at[0] - n:at[0]]

        cp = take(CP_N)
        ident, iota, offs = cp[:, 0:128], cp[:, 128:192], cp[:, 192:200]
        cols = take(SC_N)
        col = {n: cols[:, a:b] for n, (a, b) in SC.items()}
        wrt = take(KD * E_N).rearrange("p (k e) -> p k e", k=KD)
        iota32 = take(E_N)
        rankm = take(NT * (E_N + 2)).rearrange("p (t e) -> p t e", t=NT)
        gwt = take(NT * (E_N + 2)).rearrange("p (t e) -> p t e", t=NT)
        gw_pair = take(NT * 2).rearrange("p (t e) -> p t e", t=NT)
        w_slot = take(2)
        count_f = take(PAIRS)
        count_i = take(PAIRS).bitcast(I32)
        modc = take(16)
        cs = take(KD)
        ssq = take(NT)
        rstd = take(NT)
        b_rt = take(E_N)
        rank_pair = take(NT * 2).rearrange("p (t e) -> p t e", t=NT)
        decay = take(4 * NCH).rearrange("p (a c) -> p a c", a=4)

        scr = ring[:, 6:SLOTS, :].rearrange("p a n -> p (a n)")
        q_s = scr[:, 0:1024].rearrange("p (a t) -> p a t", a=2)
        k_s = scr[:, 1024:2048].rearrange("p (a t) -> p a t", a=2)
        v_s = scr[:, 2048:4096].rearrange("p (t c) -> p t c", t=NT)
        g_s = scr[:, 4096:6144].rearrange("p (h t) -> p h t", h=HEADS)
        up = scr[:, 4096:4096 + POOL_N]
        modr = scr[:, 4096:6144]
        base = 4096 + POOL_N
        ct = scr[:, base:base + CT_N + EDGE_N]
        reset, ones, sel, lower = ct[:, 0:512], ct[:, 512:640], ct[:, 640:768], ct[:, 768:896]
        edge = ct[:, CT_N:CT_N + EDGE_N]
        base += CT_N + EDGE_N
        ta, tb = scr[:, base:base + 528], scr[:, base + 528:base + 1056]
        base += 1056
        assert base <= 2 * UNIT
        att = scr[:, 0:2048].rearrange("p (h n) -> p h n", h=HEADS)
        tmp_x = (ta[:, 0:512], tb[:, 0:512])
        rt = scr[:, 1280:2048]
        rt_s, rt_sel, rt_a, rt_tmp = (rt[:, i * 128:(i + 1) * 128].rearrange("p (t e) -> p t e", t=NT) for i in range(4))
        rt_srt = rt[:, 512:640].rearrange("p (t g e) -> p t g e", t=NT, g=G_N)
        rt_gs, rt_goh = (rt[:, 640 + i * 16:656 + i * 16].rearrange("p (t g) -> p t g", t=NT) for i in range(2))
        rt_in, rt_oh1, rt_oh2 = (scr[:, 1024 + i * 32:1056 + i * 32].rearrange("p (t e) -> p t e", t=NT) for i in range(3))
        rt_t12 = rt[:, 672:680].rearrange("p (t e) -> p t e", t=NT)
        rt_top, rt_m = rt[:, 680:684], rt[:, 684:688]

        qe = big[:, 0:2048].rearrange("p (d a t) -> p d a t", d=2, a=2)
        ke = big[:, 2048:4096].rearrange("p (d a t) -> p d a t", d=2, a=2)
        acc = mid[:, :].rearrange("p (t n) -> p t n", t=NT)
        xn = mid[:, :].rearrange("p (t n) -> p t n", t=NT)
        la = mid[:, 0:2048].rearrange("p (d a t) -> p d a t", d=2, a=2)
        bb = mid[:, 2048:4096].rearrange("p (d a t) -> p d a t", d=2, a=2)
        kd = la
        kdtok = bb.rearrange("p d a (t c) -> p d a t c", t=NT)
        st = [mid[:, 0:1792].rearrange("p (a n v) -> p a n v", a=2, n=7),
              big[:, 2048:3840].rearrange("p (a n v) -> p a n v", a=2, n=7)]
        h2 = mid[:, :].rearrange("p (t n) -> p t n", t=NT)
        cat = low[:, :].rearrange("p (k t) -> p k t", k=KD)
        wpool = low[:, 2048:2560].rearrange("p (g c) -> p g c", g=4)
        cb = low[:, 2560:2816].rearrange("p (k m) -> p k m", k=KD)
        masks = low[:, 2816:3072]
        wup = low[0:2 * RANK, 3072:3584].rearrange("p (d c) -> p d c", d=2)
        r_t = low[0:2 * RANK, 3584:4096]
        rst = mid[:, 0:2048].rearrange("p (h t) -> p h t", h=HEADS)
        h2t = low[:, :].rearrange("p (k t) -> p k t", k=KD)
        onehot = onehot_t[:, :, :].bitcast(F32)
        xg = low[:, 512:2560].rearrange("p (b k s) -> p b k s", b=2, k=KD)
        sil = low[:, 2560:3072]
        hid = low[:, 3072:3584]
        xg_rows = low[:, 2560:3584]
        hid_t = low[:, 3584:4096].rearrange("p (k s) -> p k s", k=KF)
        hid_x = low[:, 0:512]

        bank = [ctx.enter_context(nc.psum_tensor(f"bank{i}", [P, 512], F32)) for i in range(8)]

        def sems(names):
            return [sem(n) for n in names.split()]

        landed = [sem(f"landed{i}") for i in range(SLOTS)]
        x_in = [sem(f"x_in{t}") for t in range(NT)]
        cols_in, keep_in, tmp_in, small_in, wr_in, bias_in = sems("cols_in keep_in tmp_in small_in wr_in bias_in")
        job_done, out_scalar, out_vector = sems("job_done out_scalar out_vector")
        vector_chain, pool_chain = sems("vector_chain pool_chain")
        cs_ready, cb_ready, ssq_ready, std_ready, xn_ready = sems("cs_ready cb_ready ssq_ready std_ready xn_ready")
        h_parts, wr_parts, w_hi_ready, w_lo_ready, chunk_used = sems("h_parts wr_parts w_hi_ready w_lo_ready chunk_used")
        cat_hi_ready, cat_lo_ready, h2_hi_ready, h2_lo_ready, x1_saved = sems(
            "cat_hi_ready cat_lo_ready h2_hi_ready h2_lo_ready x1_saved")
        pads_zero, pooled, neg_abs, gate_exp, softplus, b_ready = sems("pads_zero pooled neg_abs gate_exp softplus b_ready")
        exp_ready, qe_ready, kd_ready, att_zero = sems("exp_ready qe_ready kd_ready att_zero")
        sq_ready, cat_ready, x1_ready, h2_ready, chosen, routed = sems("sq_ready cat_ready x1_ready h2_ready chosen routed")
        g2_saved, moe_init = sems("g2_saved moe_init")
        rank_cols, p_ready, gath, rows_ready, turned, xg_ready, pt_psum, pt_ready, w_ready = sems(
            "rank_cols onehot_ready gathered rows_ready turned xg_ready pt_psum pt_ready w_ready")
        a_done, sil_ready, hid_ready, t_done, hidt_ready = sems(
            "up_done sil_ready hid_ready hid_transposed hidt_ready")
        y_done, yh_ready, yl_ready, c_done, acc_done = sems("down_done yh_ready yl_ready combined acc_done")
        extra, extra_vector, extra_c = sems("extra_step extra_vector extra_combined")
        x1_half, tail_in, fin_mul, fin_sum, fin_ssq, fin_std, fin_rec, fin, stored = sems(
            "x1_half tail_in fin_mul fin_sum fin_ssq fin_std fin_rec fin stored")

        block = ctx.enter_context(nc.Block())

        w_mod, w_in, w_out = A["w_mod"][0], A["w_in"][0], A["w_out"][0]
        def rows(w):
            return w.rearrange("(k p) n -> p k n", p=P)

        def unit(slot, k):
            return ring[:, slot, :].rearrange("p (k n) -> p k n", k=k)

        def pre_source(n):
            name = STREAM[n]
            if name[0] == "m":
                i = int(name[1:])
                return rows(w_mod)[:, :, i * 512:(i + 1) * 512]
            if name[:2] == "wo":
                i = int(name[2:])
                return rows(w_out)[:, :, i * 512:(i + 1) * 512]
            i = dict(u=0, qk=1, v=2, g=3)[name]
            return rows(w_in)[:, :, i * 512:(i + 1) * 512]

        s0 = (UPP * (PAIRS - 1)) % SLOTS
        assert s0 + 3 < SLOTS
        tail_x = ring[:, s0, :].rearrange("p (t n) -> p t n", t=NT)
        tail_g2, tail_fg = ring[:, s0 + 1, 0:D], ring[:, s0 + 1, D:2 * D]

        w1_r = A["w1"][0].rearrange("e (k p) n -> p e k n", p=P)
        w3_r = A["w3"][0].rearrange("e (k p) n -> p e k n", p=P)
        w2_r = A["w2"][0].rearrange("e (k p) n -> p e k n", p=P)

        def landed_at(n, it):
            slot = n % SLOTS
            return 16 * (PRE_USES[slot] + n // SLOTS + 1) + 16 * 3 * it

        def used_up(eng, n):
            name = STREAM[n]
            if name in SPLIT:
                count = KD * (SPLIT.index(name) + 1)
                eng.wait_ge(w_hi_ready, count)
                eng.wait_ge(w_lo_ready, count)
            else:
                eng.wait_ge(job_done, JOB["mr" + name[1:]] + 1)

        @block.sync
        def _(sp):
            x_r = A["x"][0].rearrange("(t p) n -> p t n", p=P)
            sp.dma_start(cols, A["cols"]).then_inc(cols_in, 16)
            for t in range(NT):
                sp.dma_start(x1[:, t, :], x_r[:, t, :]).then_inc(x_in[t], 16)
            for n in range(PRE_UNITS):
                slot = n % PRE_SLOTS
                if n >= PRE_SLOTS:
                    used_up(sp, n - PRE_SLOTS)
                sp.dma_start(unit(slot, KD), pre_source(n)).then_inc(landed[slot], 16)

            def expert_unit(n, it):
                slot = n % SLOTS
                pair, k = n // UPP, n % UPP
                e = 2 * (PPI * it + pair) + k % 2
                w, kk = ((w1_r, KD), (w3_r, KD), (w2_r, KF))[k // 2]
                src = w[:, bass.ds(e, 1), :, :].rearrange("p e k n -> p (e k) n")
                sp.dma_start(unit(slot, kk), src).then_inc(landed[slot], 16)

            for n in range(SLOTS):
                if n < PRE_SLOTS:
                    used_up(sp, [m for m in range(PRE_UNITS) if m % PRE_SLOTS == n][-1])
                elif n == PRE_SLOTS:
                    sp.wait_ge(job_done, JOB["wo13"] + 1)
                    sp.wait_ge(g2_saved, 16)
                elif n == 6:
                    sp.wait_ge(routed, 1)
                    sp.wait_ge(job_done, len(JOBS))
                    sp.wait_ge(out_vector, len(OUT_VECTOR))
                expert_unit(n, 0)
            per = UPP * PPI

            def slot_used_up(n, it):
                pair, k = (n - SLOTS) // UPP, (n - SLOTS) % UPP
                if k < 4:
                    sp.wait_ge(t_done, PPI * it + (pair + 1))
                else:
                    sp.wait_ge(y_done, 2 * PPI * it + (2 * pair + 2 + Y_AHEAD))

            with sp.Fori(0, ITERS - 1) as it:
                for n in range(SLOTS, SLOTS + per):
                    slot_used_up(n, it)
                    expert_unit(n, it)
            for n in range(SLOTS, per):
                slot_used_up(n, ITERS - 1)
                expert_unit(n, ITERS - 1)
            sp.wait_ge(x1_saved, 16)
            sp.wait_ge(t_done, PAIRS)
            sp.dma_start(tail_x, x1_row.rearrange("(t p) n -> p t n", p=P)).then_inc(tail_in, 16)
            sp.dma_start(tail_g2, g2_row.to_broadcast([P, D])).then_inc(tail_in, 16)
            sp.dma_start(tail_fg, A["final_g"].rearrange("(a n) -> a n", a=1).to_broadcast([P, D])).then_inc(tail_in, 16)
            out_r = out[0].rearrange("(t p) n -> p t n", p=P)
            for t in range(NT):
                sp.wait_ge(fin, t + 1)
                sp.dma_start(out_r[:, t, :], acc[:, t, :]).then_inc(stored, 16)
            sp.wait_ge(stored, 16 * NT)

        def full(eng, name):
            eng.wait_ge(job_done, JOB[name] + 1)
            return bank[JOB[name] % 8]

        def read_out(eng, name):
            if name in OUT_SCALAR:
                eng.wait_ge(out_scalar, OUT_SCALAR.index(name) + 1)
            else:
                eng.wait_ge(out_vector, OUT_VECTOR.index(name) + 1)

        @block.tensor
        def _(pe):
            mm = nc.tensor.matmul
            todo = iter(JOBS)

            def start(name):
                assert next(todo) == name, name
                j = JOB[name]
                if j >= 8:
                    read_out(pe, JOBS[j - 8])
                return bank[j % 8]

            def slot_in(name, k=KD):
                n = SU[name]
                pe.wait_ge(landed[n % PRE_SLOTS], 16 * (n // PRE_SLOTS + 1))
                return unit(n % PRE_SLOTS, k)

            def mod_rows(i):
                b = start(f"mr{i}")
                w = slot_in(f"m{i}")
                for k in range(KD):
                    j = k % 4
                    last = mm(b[32 * j:32 * j + 32, :], cb[:, k, :], w[:, k, :], start=k < 4, stop=k >= 4,
                              tile_position=(0, 32 * j), skip_group_check=True)
                last.then_inc(job_done, 1)

            pe.wait_ge(cb_ready, 1)
            for i in range(4):
                mod_rows(i)
            b = start("mcol")
            read_out(pe, "mr3")
            pe.wait_ge(tmp_in, 16)
            for i in range(16):
                last = mm(b[:, i:i + 1], modr[:, i * P:(i + 1) * P], sel[:, 0:1], start=True, stop=True)
            last.then_inc(job_done, 1)
            for k in range(KD):
                b = start(f"xT{k}")
                if k == 0:
                    pe.wait_ge(xn_ready, NT)
                    pe.wait_ge(keep_in, 64)
                for t in range(NT):
                    last = nc.tensor.transpose(b[:, t * P:(t + 1) * P], xn[:, t, k * P:(k + 1) * P], ident)
                last.then_inc(job_done, 1)
            def three(out_, hi, lo, w_h, w_l, k, stop, stationary_w):
                for n, (x_, y_) in enumerate(((hi, w_h), (hi, w_l), (lo, w_h))):
                    lhs, rhs = (y_, x_) if stationary_w else (x_, y_)
                    last = mm(out_, lhs, rhs, start=k == 0 and n == 0, stop=stop and n == 2)
                return last

            b = start("r")
            for k in range(KD):
                pe.wait_ge(h_parts, k + 1)
                if k == 0:
                    pe.wait_ge(wr_parts, 1)
                last = three(b[:, :], h_hi[:, k, :], h_lo[:, k, :], wr_hi[:, k, :], wr_lo[:, k, :], k, k == KD - 1, True)
            last.then_inc(job_done, 1)

            def product(unit_name, names, a_hi, a_lo, stationary_w, ready=None):
                banks = [start(n) for n in names]
                for k in range(KD):
                    c = KD * SPLIT.index(unit_name) + k
                    pe.wait_ge(w_hi_ready, c + 1)
                    pe.wait_ge(w_lo_ready, c + 1)
                    if ready is not None:
                        ready(k)
                    for i, b in enumerate(banks):
                        s_ = slice(i * P, (i + 1) * P)
                        if stationary_w:
                            last = three(b[:, :], a_hi[:, k, :], a_lo[:, k, :], w_hi[:, c % DEPTH, s_], w_lo[:, c % DEPTH, s_],
                                         k, k == KD - 1, True)
                        else:
                            last = three(b[:, :], a_hi[:, k, s_], a_lo[:, k, s_], w_hi[:, c % DEPTH, :], w_lo[:, c % DEPTH, :],
                                         k, k == KD - 1, False)
                        if k == KD - 1:
                            last.then_inc(job_done, 1)
                    if k < KD - 1:
                        last.then_inc(chunk_used, 1)

            product("u", [f"u{i}" for i in range(4)], h_hi, h_lo, True)
            read_out(pe, "r")
            pe.wait_ge(small_in, 48)
            for i in range(4):
                b = start(f"gk{i}")
                mm(b[:, :], wup[:, i // 2, (i % 2) * P:(i % 2 + 1) * P], r_t, start=True, stop=True).then_inc(job_done, 1)
            product("qk", ["q0", "q1", "k0", "k1"], h_hi, h_lo, True)
            for g in range(4):
                b = start(f"yp{g}")
                pe.wait_ge(pooled, g + 1)
                o, left, _ = POOL_AT[g]
                mm(b[:, :], wpool[:, g, :], up[:, o + left:o + left + S], start=True, stop=True).then_inc(job_done, 1)
            product("v", [f"v{i}" for i in range(4)], h_hi, h_lo, False)
            product("g", [f"g{i}" for i in range(4)], h_hi, h_lo, True)

            def mod_pair(i):
                for j in (i, i + 1):
                    mod_rows(j)
                for j in (i, i + 1):
                    b = start(f"mb{j}")
                    read_out(pe, f"mr{j}")
                    pe.wait_ge(bias_in, 16)
                    mm(b[:, :], sel, mrow[:, j % 2, :], start=True, stop=False)
                    mm(b[:, :], ones[0:1, :], bias_row[:, (j - 4) * 512:(j - 3) * 512], start=False, stop=True).then_inc(job_done, 1)

            mod_pair(4)
            mod_pair(6)
            for d in range(2):
                for pr in range(2):
                    b = [start(f"att{d}{2 * pr + hh}") for hh in range(2)]
                    pe.wait_ge(qe_ready, 2 * d + pr + 1)
                    for t in range(NT):
                        c = slice(t * P, (t + 1) * P)
                        for hh in range(2):
                            r = slice(hh * DK, (hh + 1) * DK)
                            last = mm(b[hh][:, c], ke[r, d, pr, c], qe[r, d, pr, c], start=True, stop=True)
                            if t == NT - 1:
                                last.then_inc(job_done, 1)
            for d in range(2):
                for pr in range(2):
                    b = start(f"kdt{d}{pr}")
                    pe.wait_ge(kd_ready, 2 * d + pr + 1)
                    for t in range(NT):
                        c = slice(t * P, (t + 1) * P)
                        last = nc.tensor.transpose(b[:, c], kd[:, d, pr, c], ident)
                    last.then_inc(job_done, 1)
            mod_pair(8)
            read_out(pe, "v3")
            for d in range(2):
                for pr in range(2):
                    read_out(pe, f"kdt{d}{pr}")
                    b = [start(f"upd{d}{pr}{par}") for par in range(2)]
                    for t in range(NT):
                        for hh in range(2):
                            for par in range(2):
                                r = slice(par * CHUNK, (par + 1) * CHUNK)
                                h = 2 * pr + hh
                                last = mm(b[par][hh * DK:(hh + 1) * DK, t * P:(t + 1) * P],
                                          kdtok[r, d, pr, t, hh * DK:(hh + 1) * DK],
                                          v_s[r, t, h * DV:(h + 1) * DV], start=True, stop=True)
                                if t == NT - 1 and hh == 1:
                                    last.then_inc(job_done, 1)
            mod_pair(10)
            for pr in range(2):
                b = [start(f"o{2 * pr + hh}") for hh in range(2)]
                read_out(pe, "att13")
                read_out(pe, f"upd1{pr}1")
                for t in range(NT):
                    for hh in range(2):
                        h = 2 * pr + hh
                        mm(b[hh][:, t * P:(t + 1) * P], v_s[:, t, h * DV:(h + 1) * DV], att[:, h, t * P:(t + 1) * P],
                           start=True, stop=False)
                    parts = []
                    for ch in (2 * t, 2 * t + 1):
                        if ch > 0:
                            parts.append((0, ch, ch - 1))
                        if ch < NCH - 1:
                            parts.append((1, ch, ch))
                    for n, (d, ch, si) in enumerate(parts):
                        c = slice(ch * CHUNK, (ch + 1) * CHUNK)
                        for hh in range(2):
                            r = slice(hh * DK, (hh + 1) * DK)
                            last = mm(b[hh][:, c], st[d][r, pr, si, :], qe[r, d, pr, c], start=False, stop=n == len(parts) - 1)
                            if t == NT - 1 and n == len(parts) - 1:
                                last.then_inc(job_done, 1)
            for h in range(HEADS):
                b = start(f"ss{h}")
                pe.wait_ge(sq_ready, h + 1)
                mm(b[:, :], ones, cat[:, 4 + h, :], start=True, stop=True).then_inc(job_done, 1)

            def cat_parts(k):
                pe.wait_ge(cat_hi_ready, k + 1)
                pe.wait_ge(cat_lo_ready, k + 1)

            for hf in range(2):
                product(f"wo{hf}", [f"wo{hf}{t}" for t in range(NT)], cat_hi, cat_lo, False, cat_parts)
            for t in range(NT):
                for hf in range(2):
                    b = start(f"hT{t}{hf}")
                    pe.wait_ge(h2_ready, t + 1)
                    for j in range(4):
                        k = 4 * hf + j
                        last = nc.tensor.transpose(b[:, j * P:(j + 1) * P], h2[:, t, k * P:(k + 1) * P], ident)
                    last.then_inc(job_done, 1)
            b = start("lg")
            for t in range(NT):
                read_out(pe, f"hT{t}1")
                for k in range(KD):
                    last = mm(b[:, t * E_N:(t + 1) * E_N], h2t[:, k, t * P:(t + 1) * P], wrt[:, k, :],
                              start=k == 0, stop=k == KD - 1)
            last.then_inc(job_done, 1)
            b = start("rk")
            pe.wait_ge(chosen, 1)
            for t in range(NT):
                for u in range(t + 1):
                    last = mm(b[:, t * E_N:(t + 1) * E_N], lower if u == t else ones, rt_a[:, u, :],
                              start=u == 0, stop=u == t)
            last.then_inc(job_done, 1)
            b = start("cnt")
            for u in range(NT):
                last = mm(b[:, 0:E_N], ones, rt_a[:, u, :], start=u == 0, stop=u == NT - 1)
            last.then_inc(job_done, 1)
            pe.wait_ge(out_vector, len(OUT_VECTOR))
            pe.wait_ge(out_scalar, len(OUT_SCALAR))

            A1, A3, TB, Y0, Y1, G0, G1, CA = bank
            SUM_BANKS = (TB, CA, Y0, Y1)
            extra_n = pe.alloc_register("pe_extra_rounds")
            pe.reg_mov(extra_n, 0)

            def gather(done=None):
                for hf, g in ((0, G0), (1, G1)):
                    c = slice(hf * 512, (hf + 1) * 512)
                    for t in range(NT):
                        mm(g[:, :], onehot_t[:, t, :], h2_hi[:, t, c], start=t == 0, stop=False)
                        last = mm(g[:, :], onehot_t[:, t, :], h2_lo[:, t, c], start=False, stop=t == NT - 1)
                    if done is not None:
                        last.then_inc(done, 1)
                return last

            def turn_rows(rows_, done=None):
                for k in range(KD):
                    g = (G0, G1)[k // 4]
                    last = nc.tensor.transpose(g[:, (k % 4) * P:(k % 4 + 1) * P], rows_[:, k * P:(k + 1) * P], ident)
                    if done is not None and k % 4 == 3:
                        last.then_inc(done, 1)
                return last

            def slots_to_partitions():
                for t in range(NT):
                    nc.tensor.transpose(CA[:, t * P:(t + 1) * P], onehot[:, t, :], ident)
                for e in range(2):
                    for t in range(NT):
                        last = mm(A1[e * CAP:(e + 1) * CAP, 0:1], onehot[:, t, e * CAP:(e + 1) * CAP],
                                  gw_pair[:, t, e:e + 1], start=t == 0, stop=t == NT - 1)
                return last

            def up_products(n0, xb, done=None, wait=None):
                for w, bk in ((0, A1), (1, A3)):
                    if wait is not None:
                        for e in range(2):
                            n = n0 + 2 * w + e
                            pe.wait_ge(landed[n % SLOTS], wait(n))
                    for k in range(KD):
                        for e in range(2):
                            n = n0 + 2 * w + e
                            last = mm(bk[e * CAP:(e + 1) * CAP, :], xb[:, k, e * CAP:(e + 1) * CAP],
                                      unit(n % SLOTS, KD)[:, k, :], start=k == 0, stop=k == KD - 1)
                    if done is not None:
                        last.then_inc(done, 1)
                return last

            def down_half(n0, hf):
                bk = (Y0, Y1)[hf]
                for k in range(KF):
                    for e in range(2):
                        n = n0 + 4 + e
                        last = mm(bk[e * CAP:(e + 1) * CAP, :], hid_t[:, k, e * CAP:(e + 1) * CAP],
                                  unit(n % SLOTS, KF)[:, k, hf * 512:(hf + 1) * 512],
                                  start=k == 0, stop=k == KF - 1)
                return last

            def combine_group(g, pt, bk):
                t, hf = g // 2, g % 2
                c = slice(hf * 512, (hf + 1) * 512)
                mm(bk[:, :], slot_tok[:, pt, t * P:(t + 1) * P], y_hi[:, c], start=True, stop=False)
                return mm(bk[:, :], slot_tok[:, pt, t * P:(t + 1) * P], y_lo[:, c], start=False, stop=True)

            def combine(p, pt):
                for g in range(8):
                    if g == 0:
                        pe.wait_ge(yh_ready, 2 * p + 2)
                        pe.wait_ge(yl_ready, 2 * p + 2)
                        pe.wait_ge(pt_ready, p + 2)
                        pe.wait_ge(hidt_ready, p + 1)
                    elif g >= 4:
                        pe.wait_ge(acc_done, 8 * p + (g - 3))
                    combine_group(g, pt, SUM_BANKS[g % 4]).then_inc(c_done, 1)

            def next_gather(q, first=False):
                pe.wait_ge(p_ready, q + 1)
                if not first:
                    pe.wait_ge(xg_ready, 2 * q)
                gather(gath)
                if not first:
                    pe.wait_ge(acc_done, 8 * q)
                    pe.wait_ge(sil_ready, q)
                slots_to_partitions().then_inc(pt_psum, 1)

            def next_turn(q):
                pe.wait_ge(rows_ready, 2 * q + 2)
                turn_rows(xg_rows, turned)

            pe.wait_ge(moe_init, 3)
            next_gather(0, first=True)
            next_turn(0)
            with pe.Fori(0, ITERS) as it:
                for j in range(PPI):
                    p = it * PPI + j
                    n0 = UPP * j
                    pe.wait_ge(xg_ready, 2 * p + 2)
                    pe.wait_ge(w_ready, p + 1)
                    pe.wait_ge(hid_ready, p + 1)
                    up_products(n0, xg[:, j % 2], a_done, lambda n, it=it: landed_at(n, it))
                    combine(p, (j + 1) % 2)
                    most = pe.value_load(count_i[0:1, bass.ds(p, 1)], min_val=0, max_val=S)
                    with pe.If(most > CAP):
                        with pe.Fori(1, ROUNDS) as r:
                            with pe.If(most > r * CAP):
                                done = pe.snap(extra_n)
                                b0 = done * EXTRA_STEPS
                                pe.wait_ge(hid_ready, p + 2)
                                pe.wait_ge(acc_done, 8 * p + 8)
                                for e in range(2):
                                    n = n0 + 4 + e
                                    pe.wait_ge(landed[n % SLOTS], landed_at(n, it))
                                pe.wait_ge(extra, b0 + 1)
                                gather()
                                slots_to_partitions().then_inc(extra, 1)
                                pe.wait_ge(extra, b0 + 3)
                                turn_rows(extra_rows).then_inc(extra, 1)
                                pe.wait_ge(extra, b0 + 5)
                                up_products(n0, xg[:, (j + 1) % 2]).then_inc(extra, 1)
                                pe.wait_ge(extra, b0 + 8)
                                for k in range(KF):
                                    last = nc.tensor.transpose(TB[:, k * P:(k + 1) * P], hid_x[:, k * P:(k + 1) * P], ident)
                                last.then_inc(extra, 1)
                                pe.wait_ge(extra, b0 + 10)
                                down_half(n0, 0)
                                down_half(n0, 1).then_inc(extra, 1)
                                pe.wait_ge(extra, b0 + 13)
                                for g in range(8):
                                    last = combine_group(g, (j + 1) % 2, bank[g])
                                    if g % 2:
                                        last.then_inc(extra_c, 1)
                                pe.wait_ge(extra, b0 + EXTRA_STEPS)
                                pe.reg_add(extra_n, extra_n, 1)
                    pe.wait_ge(hid_ready, p + 2)
                    pe.wait_ge(acc_done, 8 * p + 5)
                    for k in range(KF):
                        last = nc.tensor.transpose(TB[:, k * P:(k + 1) * P], hid[:, k * P:(k + 1) * P], ident)
                    last.then_inc(t_done, 1)
                    next_gather(p + 1)
                    pe.wait_ge(hidt_ready, p + 2)
                    for e in range(2):
                        n = n0 + 4 + e
                        pe.wait_ge(landed[n % SLOTS], landed_at(n, it))
                    down_half(n0, 0).then_inc(y_done, 1)
                    next_turn(p + 1)
                    down_half(n0, 1).then_inc(y_done, 1)
            combine(PAIRS, (PAIRS + 1) % 2)

        def part_free(eng, c):
            if c >= DEPTH:
                u, k = divmod(c - DEPTH, KD)
                if k < KD - 1:
                    eng.wait_ge(chunk_used, (KD - 1) * u + k + 1)
                else:
                    eng.wait_ge(job_done, JOB[LAST_JOB[u]] + 1)

        def raw_chunk(c):
            slot = SU[SPLIT[c // KD]] % PRE_SLOTS
            return unit(slot, KD)[:, c % KD, :]

        @block.scalar
        def _(act):
            a = nc.scalar.activation

            act.dma_start(wr_raw, A["wr"]).then_inc(wr_in, 16)
            act.dma_start(cp, A["const_keep"]).then_inc(keep_in, 16)
            act.dma_start(ct, A["const_tmp"]).then_inc(tmp_in, 16)
            act.dma_start(wpool.rearrange("p k c -> p (k c)"), A["wpool"]).then_inc(small_in, 16)
            act.dma_start(masks, A["masks"]).then_inc(small_in, 16)
            act.dma_start(wup.rearrange("p d c -> p (d c)"), A["wup"]).then_inc(small_in, 16)
            act.dma_start(wrt.rearrange("p k e -> p (k e)"), A["wrt"]).then_inc(keep_in, 16)
            act.dma_start(iota32, A["iota32"]).then_inc(keep_in, 16)
            act.dma_start(b_rt, A["b_router"].rearrange("(a n) -> a n", a=1).to_broadcast([P, E_N])).then_inc(keep_in, 16)

            act.wait_ge(cols_in, 16)
            a(cs, col["c"], ACT.Silu).then_inc(cs_ready, 1)
            for t in range(NT):
                act.wait_ge(x_in[t], 16)
                a(xn[:, t, :], x1[:, t, :], ACT.Square, accum_out=ssq[:, t:t + 1]).then_inc(ssq_ready, 1)
            act.wait_ge(ssq_ready, NT)
            a(rstd, ssq, ACT.Sqrt, bias=col["eps"], scale=1.0 / D).then_inc(std_ready, 1)
            for i in range(4):
                b = full(act, f"mr{i}")
                nc.scalar.copy(modr[:, i * 512:(i + 1) * 512], b[:, :]).then_inc(out_scalar, 1)
            read_out(act, "mcol")
            for k in range(KD):
                b = full(act, f"xT{k}")
                if k >= 2:
                    act.wait_ge(h_parts, k - 1)
                a(h_tmp[:, k % 2, :], b[:, :], ACT.Identity, bias=modc[:, k:k + 1], scale=modc[:, 8 + k:9 + k]).then_inc(out_scalar, 1)

            def high_parts(c0, c1):
                for c in range(c0, c1):
                    n = SU[SPLIT[c // KD]]
                    if c % KD == 0 or c == c0:
                        act.wait_ge(landed[n % PRE_SLOTS], 16 * (n // PRE_SLOTS + 1))
                    part_free(act, c)
                    nc.scalar.copy(w_hi[:, c % DEPTH, :], raw_chunk(c)).then_inc(w_hi_ready, 1)

            high_parts(0, 4)
            b = full(act, "r")
            nc.scalar.copy(r_t, b[0:2 * RANK, :]).then_inc(out_scalar, 1)
            high_parts(4, 12)
            act.wait_ge(pads_zero, 1)
            for g in range(4):
                b = full(act, f"u{g}")
                o, left, _ = POOL_AT[g]
                nc.scalar.copy(up[:, o + left:o + left + S], b[:, :]).then_inc(out_scalar, 1)
            for i in range(4):
                b = full(act, f"gk{i}")
                a(la[:, i // 2, i % 2, :], b[:, :], ACT.Identity, bias=col["bgk"][:, i:i + 1]).then_inc(out_scalar, 1)
            high_parts(12, 16)
            for i in range(4):
                act.wait_ge(neg_abs, i + 1)
                a(bb[:, i // 2, i % 2, :], bb[:, i // 2, i % 2, :], ACT.Exp).then_inc(gate_exp, 1)
            for i in range(4):
                act.wait_ge(gate_exp, i + 1)
                a(bb[:, i // 2, i % 2, :], bb[:, i // 2, i % 2, :], ACT.Ln, bias=1.0).then_inc(softplus, 1)
            high_parts(16, 20)
            for i, name in enumerate(("q0", "q1", "k0", "k1")):
                b = full(act, name)
                dst = (q_s, q_s, k_s, k_s)[i][:, i % 2, :]
                a(dst, b[:, :], ACT.Copy, scale=DK ** -0.5 if i < 2 else 1.0).then_inc(out_scalar, 1)
            high_parts(20, 22)
            for g in range(4):
                b = full(act, f"yp{g}")
                a(cat[:, g, :], b[:, :], ACT.Copy, scale=col["pscale"][:, g:g + 1]).then_inc(out_scalar, 1)
            high_parts(22, 32)
            for h in range(HEADS):
                b = full(act, f"g{h}")
                a(g_s[:, h, :], b[:, :], ACT.Silu).then_inc(out_scalar, 1)
            act.wait_ge(b_ready, 4)

            def decays(i):
                d, pr = i // 2, i % 2
                a(qe[:, d, pr, :], bb[:, d, pr, :], ACT.Exp, scale=1.0 / GATE_NORM).then_inc(exp_ready, 1)
                a(ke[:, d, pr, :], bb[:, d, pr, :], ACT.Exp, scale=-1.0 / GATE_NORM).then_inc(exp_ready, 1)
                whole = bb[:, d, pr, :].rearrange("p (c n) -> p c n", n=CHUNK)[:, :, (CHUNK - 1) if d == 0 else 0]
                a(decay[:, i, :], whole, ACT.Exp, scale=1.0 / GATE_NORM).then_inc(exp_ready, 1)

            def mod_part(i):
                b = full(act, f"mr{i}")
                if i >= 6:
                    act.wait_ge(job_done, JOB[f"mb{i - 2}"] + 1)
                nc.scalar.copy(mrow[:, i % 2, :], b[:, :]).then_inc(out_scalar, 1)

            for i in range(4):
                decays(i)
            for i in range(4, 8):
                mod_part(i)
            for i in range(4):
                b = full(act, f"kdt{i // 2}{i % 2}")
                if i == 0:
                    act.wait_ge(kd_ready, 4)
                nc.scalar.copy(kdtok[:, i // 2, i % 2, :, :].rearrange("p t c -> p (t c)"), b[:, :]).then_inc(out_scalar, 1)
            for i in range(8, 12):
                mod_part(i)
            for h in range(HEADS):
                b = full(act, f"o{h}")
                a(cat[:, 4 + h, :], b[:, :], ACT.Square).then_inc(sq_ready, 1)
            for h in range(HEADS):
                b = full(act, f"ss{h}")
                a(rst[:, h, :], b[:, :], ACT.Sqrt, bias=col["eps"], scale=1.0 / DV).then_inc(out_scalar, 1)

            def high_cat(k):
                nc.scalar.copy(cat_hi[:, k, :], cat[:, k, :]).then_inc(cat_hi_ready, 1)

            read_out(act, "yp3")
            for k in range(4):
                high_cat(k)
            act.wait_ge(job_done, JOB["mb11"] + 1)
            act.wait_ge(g2_saved, 16)
            high_parts(32, 36)
            for k in range(4, KD):
                act.wait_ge(cat_ready, k - 3)
                high_cat(k)
            high_parts(36, 48)
            for t in range(NT):
                act.wait_ge(x1_ready, t + 1)
                a(h2[:, t, :], x1[:, t, :], ACT.Square, accum_out=ssq[:, t:t + 1]).then_inc(ssq_ready, 1)
                act.wait_ge(ssq_ready, NT + t + 1)
                a(rstd[:, t:t + 1], ssq[:, t:t + 1], ACT.Sqrt, bias=col["eps"], scale=1.0 / D).then_inc(std_ready, 1)
            act.wait_ge(job_done, JOB["wo13"] + 1)
            for t in range(NT):
                for hf in range(2):
                    b = full(act, f"hT{t}{hf}")
                    dst = h2t[:, 4 * hf:4 * hf + 4, t * P:(t + 1) * P]
                    nc.scalar.copy(dst, b[:, :].rearrange("p (k t) -> p k t", k=4)).then_inc(out_scalar, 1)
                if t < NT - 1:
                    nc.scalar.copy(h2_hi[:, t, :], h2[:, t, :]).then_inc(h2_hi_ready, 1)
            b = full(act, "lg")
            a(rt_s.rearrange("p t e -> p (t e)"), b[:, 0:NT * E_N], ACT.Sigmoid).then_inc(out_scalar, 1)
            nc.scalar.copy(h2_hi[:, NT - 1, :], h2[:, NT - 1, :]).then_inc(h2_hi_ready, 1)

            A1, A3, TB, Y0, Y1, G0, G1, CA = bank
            extra_n = act.alloc_register("act_extra_rounds")
            act.reg_mov(extra_n, 0)

            def take_rows(to, done, gate=None):
                for hf, g in ((0, G0), (1, G1)):
                    if gate is not None:
                        act.wait_ge(gath, gate + hf)
                    ins = nc.scalar.copy(to[:, hf * 512:(hf + 1) * 512], g[:, :])
                    if done is not None:
                        ins.then_inc(done, 1)

            def take_turned(buf, hf):
                return nc.scalar.copy(xg[:, buf, 4 * hf:4 * hf + 4, :].rearrange("p k s -> p (k s)"), (G0, G1)[hf][:, :])

            def gathered(q, buf, first=False):
                take_rows(xg_rows, rows_ready, 2 * q + 1)
                act.wait_ge(pt_psum, q + 1)
                if not first:
                    act.wait_ge(c_done, 8 * q)
                nc.scalar.copy(slot_tok[:, buf, :], CA[:, :]).then_inc(pt_ready, 1)
                if not first:
                    act.wait_ge(yl_ready, 2 * q)
                nc.scalar.copy(w_slot[:, buf:buf + 1], A1[:, 0:1]).then_inc(w_ready, 1)

            def turned_rows(q, buf, first=False):
                if not first:
                    act.wait_ge(a_done, 2 * q)
                for hf in range(2):
                    act.wait_ge(turned, 2 * q + hf + 1)
                    take_turned(buf, hf).then_inc(xg_ready, 1)

            def take_down(buf, hf):
                return a(y_hi[:, hf * 512:(hf + 1) * 512], (Y0, Y1)[hf][:, :], ACT.Copy, scale=w_slot[:, buf:buf + 1])

            act.wait_ge(moe_init, 3)
            gathered(0, 0, first=True)
            turned_rows(0, 0, first=True)
            with act.Fori(0, ITERS) as it:
                for j in range(PPI):
                    p = it * PPI + j
                    act.wait_ge(a_done, 2 * p + 1 + A_AHEAD)
                    act.wait_ge(hid_ready, p + 1)
                    a(sil, A1[:, :], ACT.Silu).then_inc(sil_ready, 1)
                    most = act.value_load(count_i[0:1, bass.ds(p, 1)], min_val=0, max_val=S)
                    with act.If(most > CAP):
                        with act.Fori(1, ROUNDS) as r:
                            with act.If(most > r * CAP):
                                done = act.snap(extra_n)
                                b0 = done * EXTRA_STEPS
                                nb = (j + 1) % 2
                                act.wait_ge(extra, b0 + 2)
                                take_rows(extra_rows, None)
                                nc.scalar.copy(slot_tok[:, nb, :], CA[:, :])
                                nc.scalar.copy(w_slot[:, nb:nb + 1], A1[:, 0:1]).then_inc(extra, 1)
                                act.wait_ge(extra, b0 + 4)
                                take_turned(nb, 0)
                                take_turned(nb, 1).then_inc(extra, 1)
                                act.wait_ge(extra, b0 + 6)
                                a(sil, A1[:, :], ACT.Silu).then_inc(extra, 1)
                                act.wait_ge(extra, b0 + 9)
                                nc.scalar.copy(hid_t.rearrange("p k s -> p (k s)"), TB[:, :]).then_inc(extra, 1)
                                act.wait_ge(extra, b0 + 11)
                                take_down(nb, 0)
                                take_down(nb, 1).then_inc(extra, 1)
                                act.reg_add(extra_n, extra_n, 1)
                    act.wait_ge(t_done, p + 1)
                    act.wait_ge(y_done, 2 * p + Y_AHEAD)
                    nc.scalar.copy(hid_t.rearrange("p k s -> p (k s)"), TB[:, :]).then_inc(hidt_ready, 1)
                    gathered(p + 1, (j + 1) % 2)
                    act.wait_ge(y_done, 2 * p + 1 + Y_AHEAD)
                    take_down(j % 2, 0).then_inc(yh_ready, 1)
                    turned_rows(p + 1, (j + 1) % 2)
                    act.wait_ge(y_done, 2 * p + 2 + Y_AHEAD)
                    take_down(j % 2, 1).then_inc(yh_ready, 1)
            for t in range(NT):
                act.wait_ge(fin_sum, t + 1)
                a(x1[:, t, :], acc[:, t, :], ACT.Square, accum_out=ssq[:, t:t + 1]).then_inc(fin_ssq, 1)
                act.wait_ge(fin_ssq, t + 1)
                a(rstd[:, t:t + 1], ssq[:, t:t + 1], ACT.Sqrt, bias=col["eps"], scale=1.0 / D).then_inc(fin_std, 1)

        @block.vector
        def _(dve):
            v = nc.vector
            n_chain = [0]

            def link(ins):
                n_chain[0] += 1
                ins.then_inc(vector_chain, 1)
                dve.wait_ge(vector_chain, n_chain[0])

            dve.wait_ge(cs_ready, 1)
            v.tensor_copy(cb, cs.unsqueeze(2).to_broadcast([P, KD, 32])).then_inc(cb_ready, 1)
            dve.wait_ge(std_ready, 1)
            link(v.reciprocal(rstd, rstd))
            for t in range(NT):
                v.tensor_scalar(xn[:, t, :], x1[:, t, :], rstd[:, t:t + 1], None, ALU.mult).then_inc(xn_ready, 1)
            dve.wait_ge(wr_in, 16)
            link(v.tensor_copy(wr_hi[:, :, :].rearrange("p k c -> p (k c)"), wr_raw))
            v.tensor_tensor(wr_lo[:, :, :].rearrange("p k c -> p (k c)"), wr_raw,
                            wr_hi[:, :, :].rearrange("p k c -> p (k c)").bitcast(F32), ALU.subtract).then_inc(wr_parts, 1)
            b = full(dve, "mcol")
            link(v.tensor_tensor(modc, b[:, 0:16], col["bmod"], ALU.add))
            v.tensor_scalar(modc[:, 8:16], modc[:, 8:16], 1.0, None, ALU.add).then_inc(out_vector, 1)
            for k in range(KD):
                read_out(dve, f"xT{k}")
                link(v.tensor_copy(h_hi[:, k, :], h_tmp[:, k % 2, :]))
                v.tensor_tensor(h_lo[:, k, :], h_tmp[:, k % 2, :], h_hi[:, k, :].bitcast(F32), ALU.subtract).then_inc(h_parts, 1)

            def low_weights(c0, c1):
                for c in range(c0, c1):
                    dve.wait_ge(w_hi_ready, c + 1)
                    v.tensor_tensor(w_lo[:, c % DEPTH, :], raw_chunk(c), w_hi[:, c % DEPTH, :].bitcast(F32),
                                    ALU.subtract).then_inc(w_lo_ready, 1)

            low_weights(0, 12)
            for i in range(4):
                read_out(dve, f"gk{i}")
                y, t = la[:, i // 2, i % 2, :], bb[:, i // 2, i % 2, :]
                v.scalar_tensor_tensor(t, y, -1.0, y, ALU.mult, ALU.min).then_inc(neg_abs, 1)
            low_weights(12, 16)
            dve.wait_ge(tmp_in, 16)
            for i in range(4):
                dve.wait_ge(softplus, i + 1)
                y, t = la[:, i // 2, i % 2, :], bb[:, i // 2, i % 2, :]
                link(v.scalar_tensor_tensor(y, y, 0.0, t, ALU.min, ALU.subtract))
                if i // 2 == 0:
                    ins = v.tensor_tensor_scan(t, reset, y, 0.0, ALU.mult, ALU.add)
                else:
                    ins = v.tensor_tensor_scan(t[:, ::-1], reset, y[:, ::-1], 0.0, ALU.mult, ALU.add)
                ins.then_inc(b_ready, 1)
            low_weights(16, 28)
            for t in range(NT):
                b = full(dve, f"v{t}")
                v.tensor_copy(v_s[:, t, :], b[:, :]).then_inc(out_vector, 1)
            low_weights(28, 32)
            read_out(dve, "k1")

            def decayed(i):
                d, pr = i // 2, i % 2
                dve.wait_ge(exp_ready, 3 * i + 3)
                v.tensor_tensor(qe[:, d, pr, :], qe[:, d, pr, :], q_s[:, pr, :], ALU.mult)
                v.tensor_tensor(ke[:, d, pr, :], ke[:, d, pr, :], k_s[:, pr, :], ALU.mult).then_inc(qe_ready, 1)
                dve.wait_ge(qe_ready, i + 1)
                v.tensor_tensor(kd[:, d, pr, :].rearrange("p (c n) -> p c n", n=CHUNK),
                                ke[:, d, pr, :].rearrange("p (c n) -> p c n", n=CHUNK),
                                decay[:, i, :].unsqueeze(2).to_broadcast([P, NCH, CHUNK]), ALU.mult).then_inc(kd_ready, 1)

            def mod_row(i):
                b = full(dve, f"mb{i}")
                c = slice((i % 2) * 512, (i % 2 + 1) * 512)
                if i < 10:
                    v.tensor_scalar((g1b, sh2b, sc2b)[(i - 4) // 2][:, c], b[:, :], 1.0 if i in (8, 9) else 0.0, None,
                                    ALU.add).then_inc(out_vector, 1)
                else:
                    v.tensor_copy(g2row[:, c], b[0:1, :]).then_inc(out_vector, 1)

            for i in range(4):
                decayed(i)
            dve.wait_ge(h_parts, KD)
            dve.wait_ge(wr_parts, 1)
            for i in range(4, 8):
                mod_row(i)
            dve.wait_ge(att_zero, 1)
            dve.wait_ge(small_in, 48)
            for d in range(2):
                for h in range(HEADS):
                    b = full(dve, f"att{d}{h}")
                    if d:
                        read_out(dve, f"att0{h}")
                    m = masks[:, d * P:(d + 1) * P].bitcast(I32).unsqueeze(1).to_broadcast([P, NT, P])
                    v.copy_predicated(att[:, h, :].rearrange("p (t i) -> p t i", t=NT), m,
                                      b[:, :].rearrange("p (t i) -> p t i", t=NT)).then_inc(out_vector, 1)
            mod_row(8)
            mod_row(9)
            for d in range(2):
                for pr in range(2):
                    full(dve, f"upd{d}{pr}0")
                    full(dve, f"upd{d}{pr}1")

                    def upd(n):
                        bk = bank[JOB[f"upd{d}{pr}{n % 2}"] % 8]
                        return bk[:, (n // 2) * P:(n // 2 + 1) * P]
                    order = list(range(NCH - 1)) if d == 0 else list(range(NCH - 1, 0, -1))
                    for i, n in enumerate(order):
                        s_out = st[d][:, pr, n if d == 0 else n - 1, :]
                        if i == 0:
                            ins = v.tensor_copy(s_out, upd(n))
                        else:
                            s_in = st[d][:, pr, n - 1 if d == 0 else n, :]
                            ins = v.scalar_tensor_tensor(s_out, s_in, decay[:, 2 * d + pr, n:n + 1], upd(n), ALU.mult, ALU.add)
                        if i < NCH - 2:
                            link(ins)
                        else:
                            ins.then_inc(out_vector, 2)
            mod_row(10)
            mod_row(11)
            def low_cat(k):
                dve.wait_ge(cat_hi_ready, k + 1)
                v.tensor_tensor(cat_lo[:, k, :], cat[:, k, :], cat_hi[:, k, :].bitcast(F32), ALU.subtract).then_inc(cat_lo_ready, 1)

            for h in range(HEADS):
                b = full(dve, f"o{h}")
                read_out(dve, f"ss{h}")
                link(v.reciprocal(rst[:, h, :], rst[:, h, :]))
                v.scalar_tensor_tensor(cat[:, 4 + h, :], b[:, :], col["ng"], rst[:, h, :], ALU.mult, ALU.mult).then_inc(out_vector, 1)
            for k in range(4):
                low_cat(k)
            low_weights(32, 34)
            for h in range(HEADS):
                read_out(dve, f"o{h}")
                v.tensor_tensor(cat[:, 4 + h, :], cat[:, 4 + h, :], g_s[:, h, :], ALU.mult).then_inc(cat_ready, 1)
            low_weights(34, 36)
            for k in range(4, KD):
                low_cat(k)
            low_weights(36, 44)

            def residual(hf, t):
                b = full(dve, f"wo{hf}{t}")
                c = slice(hf * 512, (hf + 1) * 512)
                v.tensor_tensor(tmp_x[t % 2], b[:, :], g1b[:, c], ALU.mult).then_inc(out_vector, 1)
                read_out(dve, f"wo{hf}{t}")
                return v.tensor_tensor(x1[:, t, c], x1[:, t, c], tmp_x[t % 2], ALU.add)

            for t in range(NT):
                residual(0, t).then_inc(x1_half, 1)
                dve.wait_ge(x1_half, t + 1)
            low_weights(44, 48)
            for t in range(NT):
                residual(1, t).then_inc(x1_ready, 1)
                dve.wait_ge(x1_ready, t + 1)
            for t in range(NT):
                dve.wait_ge(std_ready, 2 + t)
                link(v.reciprocal(rstd[:, t:t + 1], rstd[:, t:t + 1]))
                link(v.scalar_tensor_tensor(h2[:, t, :], x1[:, t, :], rstd[:, t:t + 1], sc2b, ALU.mult, ALU.mult))
                v.tensor_tensor(h2[:, t, :], h2[:, t, :], sh2b, ALU.add).then_inc(h2_ready, 1)

            dve.wait_ge(keep_in, 64)
            read_out(dve, "lg")
            gview = lambda z: z.rearrange("p t (g e) -> p t g e", g=G_N)
            big4 = [P, NT, G_N, EPG]
            iota_g = iota32[:, 0:G_N].unsqueeze(1).to_broadcast([P, NT, G_N])
            iota_e = iota32[:, 0:EPG].unsqueeze(1).to_broadcast([P, NT, EPG])
            link(v.tensor_tensor(rt_sel, rt_s, b_rt.unsqueeze(1).to_broadcast([P, NT, E_N]), ALU.add))
            for t in range(NT):
                for g in range(G_N):
                    ins = v.max(rt_srt[:, t, g, :], rt_sel[:, t, g * EPG:(g + 1) * EPG])
            link(ins)
            link(v.tensor_tensor(rt_gs, rt_srt[:, :, :, 0], rt_srt[:, :, :, 1], ALU.add))

            def first_of(onehot_out, values, target, n, iota_n, taken=None):
                link(v.tensor_tensor(onehot_out, values, target.unsqueeze(2).to_broadcast([P, NT, n]), ALU.is_equal))
                link(v.scalar_tensor_tensor(onehot_out, onehot_out, -100.0, iota_n, ALU.mult, ALU.add))
                if taken is not None:
                    link(v.scalar_tensor_tensor(onehot_out, taken, 1000.0, onehot_out, ALU.mult, ALU.add))
                link(v.tensor_reduce(rt_m, onehot_out, AX_X, ALU.min))
                link(v.tensor_tensor(onehot_out, onehot_out, rt_m.unsqueeze(2).to_broadcast([P, NT, n]), ALU.is_equal))

            link(v.tensor_reduce(rt_top, rt_gs, AX_X, ALU.max))
            first_of(rt_goh, rt_gs, rt_top, G_N, iota_g)
            goh4 = rt_goh.unsqueeze(3).to_broadcast(big4)
            link(v.tensor_tensor(gview(rt_tmp), gview(rt_sel), goh4, ALU.mult))
            link(v.tensor_reduce(rt_in, gview(rt_tmp).rearrange("p t g e -> p t e g"), AX_X, ALU.add))
            link(v.tensor_tensor(rt_srt, rt_srt, goh4, ALU.mult))
            link(v.tensor_reduce(rt_t12, rt_srt[:, :, :, 0:2].rearrange("p t g e -> p t e g"), AX_X, ALU.add))
            first_of(rt_oh1, rt_in, rt_t12[:, :, 0], EPG, iota_e)
            first_of(rt_oh2, rt_in, rt_t12[:, :, 1], EPG, iota_e, taken=rt_oh1)
            link(v.tensor_tensor(rt_oh1, rt_oh1, rt_oh2, ALU.add))
            v.tensor_tensor(gview(rt_a), goh4, rt_oh1.unsqueeze(2).to_broadcast(big4), ALU.mult).then_inc(chosen, 1)
            dve.wait_ge(chosen, 1)
            link(v.tensor_tensor(gwt[:, :, 0:E_N], rt_a, rt_s, ALU.mult))
            link(v.tensor_reduce(rt_m, gwt[:, :, 0:E_N], AX_X, ALU.add))
            link(v.reciprocal(rt_m, rt_m))
            link(v.tensor_tensor(gwt[:, :, 0:E_N], gwt[:, :, 0:E_N], rt_m.unsqueeze(2).to_broadcast([P, NT, E_N]), ALU.mult))
            b = full(dve, "rk")
            v.scalar_tensor_tensor(rankm[:, :, 0:E_N], b[:, 0:NT * E_N].rearrange("p (t e) -> p t e", t=NT), 1.0, rt_a,
                                   ALU.add, ALU.mult).then_inc(out_vector, 1)
            read_out(dve, "rk")
            link(v.tensor_scalar(rankm[:, :, 0:E_N], rankm[:, :, 0:E_N], -1.0, None, ALU.add))
            link(v.memset(rankm[:, :, E_N:E_N + 2], -1.0))
            link(v.memset(gwt[:, :, E_N:E_N + 2], 0.0))
            b = full(dve, "cnt")
            v.tensor_reduce(count_f, b[:, 0:E_N].rearrange("p (a e) -> p a e", e=2), AX_X, ALU.max).then_inc(out_vector, 1)
            read_out(dve, "cnt")
            v.tensor_copy(count_i, count_f).then_inc(routed, 1)

            A1, A3, TB, Y0, Y1, G0, G1, CA = bank
            SUM_BANKS = (TB, CA, Y0, Y1)
            extra_n = dve.alloc_register("dve_extra_rounds")
            dve.reg_mov(extra_n, 0)
            iota8 = iota.unsqueeze(1).to_broadcast([P, NT * 2, CAP])

            def one_hot(q, off, cols_ready, cols_count):
                v.tensor_scalar(rank_pair, rankm[:, :, bass.ds(2 * q, 2)], off, None, ALU.add).then_inc(cols_ready, 1)
                v.tensor_copy(gw_pair, gwt[:, :, bass.ds(2 * q, 2)])
                dve.wait_ge(cols_ready, cols_count)
                return v.tensor_tensor(onehot_t[:, :, :].rearrange("p t (e s) -> p (t e) s", e=2),
                                       rank_pair.rearrange("p t e -> p (t e)").unsqueeze(2).to_broadcast([P, NT * 2, CAP]),
                                       iota8, ALU.is_equal)

            def low_part(buf, hf):
                c = slice(hf * 512, (hf + 1) * 512)
                return v.scalar_tensor_tensor(y_lo[:, c], (Y0, Y1)[hf][:, :], w_slot[:, buf:buf + 1], y_hi[:, c].bitcast(F32),
                                              ALU.mult, ALU.subtract)

            def add_group(g, bk):
                t, hf = g // 2, g % 2
                c = slice(hf * 512, (hf + 1) * 512)
                return v.tensor_tensor(acc[:, t, c], acc[:, t, c], bk[:, :], ALU.add)

            def add_up(p):
                for g in range(8):
                    dve.wait_ge(c_done, 8 * p + g + 1)
                    add_group(g, SUM_BANKS[g % 4]).then_inc(acc_done, 1)

            for s_, n_ in ((a_done, A_AHEAD), (y_done, Y_AHEAD), (hid_ready, 1), (hidt_ready, 1), (pt_ready, 1),
                           (yh_ready, 2), (yl_ready, 2)):
                dve.sem_inc(s_, n_)
            dve.wait_ge(routed, 1)
            dve.wait_ge(job_done, len(JOBS))
            dve.wait_ge(out_scalar, len(OUT_SCALAR))
            dve.sem_inc(moe_init, 1)
            one_hot(0, 0.0, rank_cols, 1).then_inc(p_ready, 1)
            dve.wait_ge(moe_init, 3)
            with dve.Fori(0, ITERS) as it:
                for j in range(PPI):
                    p = it * PPI + j
                    dve.wait_ge(a_done, 2 * p + 2 + A_AHEAD)
                    dve.wait_ge(sil_ready, p + 1)
                    v.tensor_tensor(hid, sil, A3[:, :], ALU.mult).then_inc(hid_ready, 1)
                    dve.wait_ge(pt_psum, p + 1)
                    one_hot(p + 1, 0.0, rank_cols, p + 2).then_inc(p_ready, 1)
                    add_up(p)
                    most = dve.value_load(count_i[0:1, bass.ds(p, 1)], min_val=0, max_val=S)
                    with dve.If(most > CAP):
                        with dve.Fori(1, ROUNDS) as r:
                            with dve.If(most > r * CAP):
                                done = dve.snap(extra_n)
                                b0 = done * EXTRA_STEPS
                                nb = (j + 1) % 2
                                dve.wait_ge(p_ready, p + 2)
                                one_hot(p, offs[:, bass.ds(r, 1)], extra_vector, 2 * done + 1).then_inc(extra, 1)
                                dve.wait_ge(extra, b0 + 7)
                                v.tensor_tensor(hid_x, sil, A3[:, :], ALU.mult).then_inc(extra, 1)
                                dve.wait_ge(extra, b0 + 12)
                                low_part(nb, 0)
                                low_part(nb, 1).then_inc(extra, 1)
                                for g in range(8):
                                    if g % 2 == 0:
                                        dve.wait_ge(extra_c, done * 4 + (g // 2 + 1))
                                    add_group(g, bank[g])
                                one_hot(p + 1, 0.0, extra_vector, 2 * done + 2).then_inc(extra, 1)
                                dve.wait_ge(extra, b0 + EXTRA_STEPS)
                                dve.reg_add(extra_n, extra_n, 1)
                    for hf in range(2):
                        dve.wait_ge(yh_ready, 2 * p + 3 + hf)
                        low_part(j % 2, hf).then_inc(yl_ready, 1)
            add_up(PAIRS)
            dve.wait_ge(tail_in, 48)
            dve.wait_ge(acc_done, 8 * PAIRS + 8)
            for t in range(NT):
                v.tensor_tensor(acc[:, t, :], acc[:, t, :], tail_g2, ALU.mult).then_inc(fin_mul, 1)
                dve.wait_ge(fin_mul, t + 1)
                v.tensor_tensor(acc[:, t, :], acc[:, t, :], tail_x[:, t, :], ALU.add).then_inc(fin_sum, 1)
            for t in range(NT):
                dve.wait_ge(fin_std, t + 1)
                v.reciprocal(rstd[:, t:t + 1], rstd[:, t:t + 1]).then_inc(fin_rec, 1)
                dve.wait_ge(fin_rec, t + 1)
                v.scalar_tensor_tensor(acc[:, t, :], acc[:, t, :], rstd[:, t:t + 1], tail_fg,
                                       ALU.mult, ALU.mult).then_inc(fin, 1)

        @block.gpsimd
        def _(pool):
            g_ = nc.gpsimd
            n_chain = [0]

            def link(ins):
                n_chain[0] += 1
                ins.then_inc(pool_chain, 1)
                pool.wait_ge(pool_chain, n_chain[0])

            pool.wait_ge(job_done, JOB["mcol"] + 1)
            g_.memset(up, 0.0).then_inc(pads_zero, 1)
            pool.wait_ge(tmp_in, 16)
            for g, w in enumerate(WINDOWS):
                o, left, ed = POOL_AT[g]
                read_out(pool, f"u{g}")
                src, n, m = up[:, o:o + S + w - 1], S + w - 1, 1
                dst = (ta, tb)
                i = 0
                while m < w:
                    n -= m
                    to = dst[i % 2][:, 0:n]
                    link(g_.tensor_tensor(to, src[:, 0:n], src[:, m:m + n], ALU.add))
                    src, m, i = to, 2 * m, i + 1
                link(g_.tensor_tensor(src[:, 0:left], src[:, 0:left], edge[:, ed:ed + left], ALU.mult))
                if left > 1:
                    link(g_.tensor_tensor(src[:, S - left + 1:S], src[:, S - left + 1:S], edge[:, ed + left:ed + w - 1], ALU.mult))
                u = up[:, o + left:o + left + S]
                link(g_.tensor_scalar(src[:, 0:S], src[:, 0:S], 1.0 / w, None, ALU.mult))
                g_.tensor_tensor(u, src[:, 0:S], u, ALU.subtract).then_inc(pooled, 1)
                pool.wait_ge(pooled, g + 1)
            pool.wait_ge(job_done, JOB["g3"] + 1)
            pool.dma_start(bias_row, A["b_mod"][:, 2 * D:6 * D]).then_inc(bias_in, 16)
            pool.wait_ge(qe_ready, 4)
            g_.memset(scr[:, 0:2048], 0.0).then_inc(att_zero, 1)
            read_out(pool, "mb11")
            pool.dma_start(g2_row, g2row).then_inc(g2_saved, 16)
            pool.wait_ge(x1_ready, NT)
            pool.dma_start(x1_row.rearrange("(t p) n -> p t n", p=P), x1[:, :, :]).then_inc(x1_saved, 16)
            pool.wait_ge(h2_ready, NT)
            g_.memset(y_hi[:, :].bitcast(F32), 0.0)
            g_.memset(y_lo[:, :].bitcast(F32), 0.0)
            g_.memset(slot_tok[:, 1, :].bitcast(F32), 0.0)
            pool.wait_ge(x1_saved, 16)
            for t in range(NT):
                pool.wait_ge(h2_hi_ready, t + 1)
                g_.tensor_tensor(h2_lo[:, t, :], h2[:, t, :], h2_hi[:, t, :].bitcast(F32), ALU.subtract).then_inc(h2_lo_ready, 1)
            pool.wait_ge(h2_lo_ready, NT)
            pool.wait_ge(job_done, JOB["hT31"] + 1)
            g_.memset(mid[:, :], 0.0).then_inc(moe_init, 2)


def kernel(**inputs):
    import numpy as _np
    import concourse.bacc as _bacc
    from concourse import mybir as _mybir
    from concourse.bass_utils import run_bass_kernel_spmd as _run

    f32 = _np.float32
    z = {k: _np.asarray(v) for k, v in inputs.items()}
    cp, ct, cm, i32 = constants()

    def columns(v):
        return v.reshape(-1, P).T

    arrays = {n: z[n] for n in ("x", "w_mod", "w_in", "w_out", "w1", "w3", "w2", "b_mod", "b_router", "final_g")}
    arrays["cols"] = _np.concatenate([columns(z["c"][0]), columns(z["b_mod"][0, :2 * D]), columns(z["pool_scale"][0]),
                                      columns(z["b_gk"][0].reshape(-1)), columns(z["gla_norm_g"][0]),
                                      _np.full((P, 1), EPS, f32)], 1)
    wr = _np.zeros((P, KD, P), f32)
    wr[:, :, :2 * RANK] = z["w_in"][0][:, 2048:].reshape(KD, P, 2 * RANK).transpose(1, 0, 2)
    arrays["wr"] = wr.reshape(P, -1)
    arrays["wrt"] = z["w_router"].reshape(KD, P, E_N).transpose(1, 0, 2).reshape(P, -1)
    arrays["wpool"] = z["w_pool"][0].transpose(1, 0, 2).reshape(P, -1)
    wup = _np.zeros((2 * RANK, 2, HEADS * DK), f32)
    wup[:RANK, 0], wup[RANK:, 1] = z["w_gk_up"][0, 0], z["w_gk_up"][0, 1]
    arrays["wup"] = wup.reshape(2 * RANK, -1)
    arrays.update(const_keep=cp, const_tmp=ct, masks=cm, iota32=i32)

    nc = _bacc.Bacc("TRN2", target_bir_lowering=False, num_devices=1)
    A = {}
    for n in arrays:
        arrays[n] = _np.ascontiguousarray(arrays[n])
        A[n] = nc.dram_tensor(f"in_{n}", arrays[n].shape, _mybir.dt.from_np(arrays[n].dtype), kind="ExternalInput").ap()
    out = nc.dram_tensor("out_0", (1, S, D), F32, kind="ExternalOutput").ap()
    g2_row = nc.dram_tensor("g2_row", (1, D), F32, kind="Internal").ap()
    x1_row = nc.dram_tensor("x1_rows", (S, D), F32, kind="Internal").ap()
    build(nc, A, out, g2_row, x1_row)
    r = _run(nc, [{f"in_{n}": a for n, a in arrays.items()}], core_ids=[0])
    return r.results[0]["out_0"]
```

```python
from contextlib import ExitStack

import numpy as np

import concourse.bass as bass
from concourse import mybir

F32 = mybir.dt.float32
F32R = mybir.dt.float32r
BF16 = mybir.dt.bfloat16
I32 = mybir.dt.int32
ALU = mybir.AluOpType
ACT = mybir.ActivationFunctionType
AX_X = mybir.AxisListType.X

P = 128
D = 1024
S = 512
KD = D // P
NT = S // P
WINDOWS = (2, 4, 8, 16)
HEADS, DK, DV = 4, 64, 128
RANK = 16
CHUNK = 64
NCH = S // CHUNK
GATE_NORM = 16.0
E_N, G_N, EPG = 32, 4, 8
DFF = 512
KF = DFF // P
EPS = 1e-6
CAP = 64
PAIRS = E_N // 2
ROUNDS = S // CAP
UNIT = 4096
SLOTS = 8
PRE_SLOTS = 4
UPP = 6
PPI = 4
ITERS = PAIRS // PPI
EXTRA_STEPS = 10
HALVES_FIRST = (0, 2, 4, 6, 1, 3, 5, 7)
EXTRA_UP = 6
EXTRA_AHEAD = EXTRA_STEPS - EXTRA_UP + 1
A_AHEAD = Y_AHEAD = 2

SC = dict(c=(0, 8), bmod=(8, 24), pscale=(24, 28), bgk=(28, 32), ng=(32, 33), eps=(33, 34))
SC_N = 34
CP = dict(ident=(0, 128), iota=(128, 192), off=(192, 200))
CP_N = 200
CT = dict(reset=(0, 512), ones=(512, 640), sel=(640, 768), lower=(768, 896), fold=(896, 928))
CT_N = 928
CM_N = 256


def pool_offsets():
    out, at, ed = [], 0, 0
    for w in WINDOWS:
        out.append((at, w // 2, ed))
        at += S + w - 1
        ed += w - 1
    return out, at, ed


POOL_AT, POOL_N, EDGE_N = pool_offsets()


def constants():
    r = np.arange(P)
    cp = np.zeros((P, CP_N), np.float32)
    cp[:, 0:128] = np.eye(P)
    cp[:, 128:192] = 1 + np.arange(CAP)[None]
    cp[:, 192:200] = -CAP * np.arange(ROUNDS)[None]
    ct = np.zeros((P, CT_N), np.float32)
    ct[:, 0:512] = (np.arange(S) % CHUNK != 0)[None]
    ct[:, 512:640] = 1.0
    ct[0::32, 640:768] = 1.0
    ct[:, 768:896] = r[:, None] < r[None, :]
    ct[:, 896:928] = r[:, None] % E_N == np.arange(E_N)[None]
    cm = np.zeros((P, CM_N), np.float32)
    same = r[:, None] // CHUNK == r[None, :] // CHUNK
    cm[:, 0:128] = same & (r[:, None] <= r[None, :])
    cm[:, 128:256] = same & (r[:, None] > r[None, :])
    ce = np.zeros((P, EDGE_N), np.float32)
    t = np.arange(S)
    for w, (_, _, ed) in zip(WINDOWS, POOL_AT):
        cnt = np.minimum(t - w // 2 + w - 1, S - 1) - np.maximum(t - w // 2, 0) + 1
        f = (w / cnt).astype(np.float32)
        ce[:, ed:ed + w // 2] = f[:w // 2]
        ce[:, ed + w // 2:ed + w - 1] = f[S - (w // 2 - 1):] if w > 2 else 0
    i8 = np.broadcast_to(np.arange(E_N, dtype=np.float32)[None], (P, E_N))
    return cp, np.concatenate([ct, ce], 1), cm, i8


JOBS = ([f"mr{i}" for i in range(4)] + ["mcol"] + [f"xT{k}" for k in range(KD)]
        + [f"u{i}" for i in range(4)] + ["r", "q0", "q1", "k0", "k1"] + [f"gk{i}" for i in range(4)]
        + [f"v{i}" for i in range(4)] + [f"yp{i}" for i in range(4)] + [f"g{i}" for i in range(4)]
        + [f"m{a}{i + j}" for i in (4, 6) for a in "rb" for j in range(2)]
        + [f"att{d}{h}" for d in range(2) for h in range(HEADS)]
        + [f"kdt{d}{p}" for d in range(2) for p in range(2)]
        + [f"m{a}{8 + j}" for a in "rb" for j in range(2)]
        + [f"upd{d}{p}{par}" for d in range(2) for p in range(2) for par in range(2)]
        + [f"m{a}{10 + j}" for a in "rb" for j in range(2)]
        + [f"o{h}" for h in range(HEADS)] + [f"rb{h}" for h in range(HEADS)]
        + [f"wo{hf}{t}" for hf in range(2) for t in range(NT)]
        + [f"hT{t}{hf}" for t in range(NT) for hf in range(2)] + ["lg", "rk", "cnt"])
JOB = {n: i for i, n in enumerate(JOBS)}
assert len(JOB) == len(JOBS)
STREAM = (["m0", "m1", "m2", "m3", "u", "qk", "v", "g"] + [f"m{i}" for i in range(4, 12)] + ["wo0", "wo1"])
SU = {n: i for i, n in enumerate(STREAM)}
PRE_UNITS = len(STREAM)
SPLIT = ["u", "qk", "v", "g", "wo0", "wo1"]
DEPTH = 4
POOL_T = 2
LAST_JOB = ["u3", "k1", "v3", "g3", "wo03", "wo13"]
OUT_SCALAR = ([f"mr{i}" for i in range(4)] + [f"xT{k}" for k in range(KD)]
              + [f"u{i}" for i in range(4)] + ["r", "q0", "q1", "k0", "k1"] + [f"gk{i}" for i in range(4)]
              + [f"yp{i}" for i in range(4)] + [f"g{i}" for i in range(4)]
              + [f"mr{i}" for i in range(4, 8)]
              + [f"kdt{d}{p}" for d in range(2) for p in range(2)]
              + [f"mr{i}" for i in range(8, 12)] + [f"o{h}" for h in range(HEADS)]
              + [f"hT{t}{hf}" for t in range(NT) for hf in range(2)] + ["lg"])
OUT_VECTOR = (["mcol"] + [f"v{i}" for i in range(4)] + [f"mb{i}" for i in range(4, 8)]
              + [f"att{d}{h}" for d in range(2) for h in range(HEADS)] + ["mb8", "mb9"]
              + [f"upd{d}{p}{par}" for d in range(2) for p in range(2) for par in range(2)]
              + ["mb10", "mb11"] + [f"rb{h}" for h in range(HEADS)]
              + [f"wo{hf}{t}" for hf in range(2) for t in range(NT)] + ["rk", "cnt"])
assert sorted(OUT_SCALAR + OUT_VECTOR) == sorted(JOBS)
PRE_USES = [len(range(i, PRE_UNITS, PRE_SLOTS)) if i < PRE_SLOTS else 0 for i in range(SLOTS)]


def build(nc, A, out, g2_row, x1_row):
    ctx = ExitStack()
    with ctx:
        def sb(name, shape, dt=F32):
            return ctx.enter_context(nc.sbuf_tensor(name, shape, dt))

        def sem(name):
            return ctx.enter_context(nc.semaphore(name))

        first = (nc.sbuf_base + 63) // 64 * 64
        total = SLOTS * UNIT + 4 * UNIT + 3 * D + 960

        def place(name, at, shape, dt=F32):
            n = 1
            for d_ in shape[1:]:
                n *= d_
            assert at + n <= total or dt == BF16
            return nc.alloc_sbuf_tensor_at(name, shape, dt, offset=first + 4 * at)

        assert first + 4 * total <= nc.sbuf_usable_end
        X1, BIG, MID, LOW = (SLOTS * UNIT + i * UNIT for i in range(4))
        YA = SLOTS * UNIT + 4 * UNIT
        ring = place("ring", 0, [P, SLOTS, UNIT])
        x1 = place("x1", X1, [P, NT, D])
        mid = place("mid", MID, [P, UNIT])
        low = place("low", LOW, [P, UNIT])
        big = place("big", BIG, [P, UNIT])
        keep = place("keep", YA + 3 * D, [P, 960])
        h_hi = place("h_hi", BIG, [P, KD, S], F32R)
        h_lo = place("h_lo", 5 * UNIT, [P, KD, S], F32R)
        cat_hi = [place("pool_hi", MID + 2048, [P, 4, S], F32R), place("gla_hi", BIG, [P, 4, S], F32R)]
        cat_lo = [place("pool_lo", 5 * UNIT, [P, 4, S], F32R), place("gla_lo", 6 * UNIT, [P, 4, S], F32R)]
        h2_hi = place("h2_hi", BIG, [P, NT, D], F32R)
        h2_lo = place("h2_lo", X1, [P, NT, D], F32R)
        w_hi = place("w_hi", 4 * UNIT, [P, DEPTH, 512], F32R)
        w_lo = place("w_lo", 4 * UNIT + DEPTH * 512, [P, DEPTH, 512], F32R)
        wr_hi = place("wr_hi", LOW, [P, KD, P], F32R)
        wr_lo = place("wr_lo", LOW + KD * P, [P, KD, P], F32R)
        spread = place("spread", YA, [P, 3 * D])
        h_tmp = spread[:, 0:D].rearrange("p (a t) -> p a t", a=2)
        wr_raw = spread[:, D:2 * D]
        g1b, sc2b, sh2b = (spread[:, i * D:(i + 1) * D] for i in range(3))
        y_hi = place("y_hi", YA, [P, D], F32R)
        extra_rows = place("extra_rows", YA, [P, D])
        y_lo = place("y_lo", YA + D, [P, D], F32R)
        slot_tok = place("slot_tok", YA + 2 * D, [P, 2, S], F32R)
        onehot_t = place("onehot", LOW, [P, NT, P], F32R)
        after = place("after", 4 * UNIT, [P, 2 * UNIT])
        mrow = after[:, 0:1024].rearrange("p (a n) -> p a n", a=2)
        g2row = after[0:1, 1024:2048]
        bias_b = after[:, UNIT:2 * UNIT]
        sq = after[:, UNIT + 2048:2 * UNIT].rearrange("p (h t) -> p h t", h=HEADS)

        at = [0]

        def take(n):
            at[0] += n
            assert at[0] <= 960
            return keep[:, at[0] - n:at[0]]

        cp = take(CP_N)
        ident, iota, offs = cp[:, 0:128], cp[:, 128:192], cp[:, 192:200]
        cols = take(SC_N)
        col = {n: cols[:, a:b] for n, (a, b) in SC.items()}
        wrt = take(KD * E_N).rearrange("p (k e) -> p k e", k=KD)
        iota32 = take(E_N)
        rankm = take(NT * (E_N + 2)).rearrange("p (t e) -> p t e", t=NT)
        gwt = take(NT * (E_N + 2)).rearrange("p (t e) -> p t e", t=NT)
        gw_pair = take(NT * 2).rearrange("p (t e) -> p t e", t=NT)
        w_slot = take(2)
        count_f = take(PAIRS)
        count_i = take(PAIRS).bitcast(I32)
        modc = take(16)
        cs = take(KD)
        ssq = take(NT)
        table_in = take(1)
        rstd = take(NT)
        b_rt = take(E_N)
        rank_pair = take(NT * 2).rearrange("p (t e) -> p t e", t=NT)
        decay = take(4 * NCH).rearrange("p (a c) -> p a c", a=4)

        scr = ring[:, 6:SLOTS, :].rearrange("p a n -> p (a n)")
        q_s = scr[:, 0:1024].rearrange("p (a t) -> p a t", a=2)
        k_s = scr[:, 1024:2048].rearrange("p (a t) -> p a t", a=2)
        v_s = scr[:, 2048:4096].rearrange("p (t c) -> p t c", t=NT)
        g_s = scr[:, 4096:6144].rearrange("p (h t) -> p h t", h=HEADS)
        up = scr[:, 4096:4096 + POOL_N]
        modr = scr[:, 4096:6144]
        base = 4096 + POOL_N
        ct = scr[:, base:base + CT_N + EDGE_N]
        reset, ones, sel, lower, fold = (ct[:, a:b] for a, b in CT.values())
        edge = ct[:, CT_N:CT_N + EDGE_N]
        base += CT_N + EDGE_N
        ta, tb = spread[:, 2 * D:2 * D + 528], scr[:, base:base + 528]
        rst = logits_t = tb[:, 0:512]
        base += 528
        base = (base + 15) // 16 * 16
        flags = place("flags", 6 * UNIT + base, [P, 3, P], BF16)
        lower_b, ones_b = flags[:, 0, :], flags[:, 1, :]
        chosen_b = flags[:, 2, :].rearrange("p (t e) -> p t e", t=NT)
        base += 192
        assert base <= 2 * UNIT
        att = scr[:, 0:2048].rearrange("p (h n) -> p h n", h=HEADS)
        rt = scr[:, 1280:2048]
        rt_s, rt_sel, rt_a, rt_tmp = (rt[:, i * 128:(i + 1) * 128].rearrange("p (t e) -> p t e", t=NT) for i in range(4))
        rt_srt = rt[:, 512:640].rearrange("p (t g e) -> p t g e", t=NT, g=G_N)
        rt_gs, rt_goh = (rt[:, 640 + i * 16:656 + i * 16].rearrange("p (t g) -> p t g", t=NT) for i in range(2))
        rt_in, rt_oh1, rt_oh2 = (scr[:, 1024 + i * 32:1056 + i * 32].rearrange("p (t e) -> p t e", t=NT) for i in range(3))
        rt_t12 = rt[:, 672:680].rearrange("p (t e) -> p t e", t=NT)
        rt_top, rt_m = rt[:, 680:684], rt[:, 684:688]

        qe = big[:, 0:2048].rearrange("p (d a t) -> p d a t", d=2, a=2)
        ke = big[:, 2048:4096].rearrange("p (d a t) -> p d a t", d=2, a=2)
        acc = mid[:, :].rearrange("p (t n) -> p t n", t=NT)
        xn = mid[:, :].rearrange("p (t n) -> p t n", t=NT)
        la = mid[:, 0:2048].rearrange("p (d a t) -> p d a t", d=2, a=2)
        bb = mid[:, 2048:4096].rearrange("p (d a t) -> p d a t", d=2, a=2)
        kd = la
        kdtok = bb.rearrange("p d a (t c) -> p d a t c", t=NT)
        st = [mid[:, 0:1792].rearrange("p (a n v) -> p a n v", a=2, n=7),
              big[:, 2048:3840].rearrange("p (a n v) -> p a n v", a=2, n=7)]
        h2 = mid[:, :].rearrange("p (t n) -> p t n", t=NT)
        cat = low[:, :].rearrange("p (k t) -> p k t", k=KD)
        wpool = low[:, 2048:2560].rearrange("p (g c) -> p g c", g=4)
        cb = low[:, 2560:2816].rearrange("p (k m) -> p k m", k=KD)
        masks = low[:, 2816:3072]
        wup = low[0:2 * RANK, 3072:3584].rearrange("p (d c) -> p d c", d=2)
        r_t = low[0:2 * RANK, 3584:4096]
        h2t = low[:, :].rearrange("p (k t) -> p k t", k=KD)
        onehot = onehot_t[:, :, :].bitcast(F32)
        xg = low[:, 512:2560].rearrange("p (b k s) -> p b k s", b=2, k=KD)
        sil = low[:, 2560:3072]
        hid = low[:, 3072:3584]
        xg_rows = low[:, 2560:3584]
        hid_t = low[:, 3584:4096].rearrange("p (k s) -> p k s", k=KF)
        y_end = low[:, 512:512 + D]
        hid_x = low[:, 0:512]

        bank = [ctx.enter_context(nc.psum_tensor(f"bank{i}", [P, 512], F32)) for i in range(8)]

        def sems(names):
            return [sem(n) for n in names.split()]

        landed = [sem(f"landed{i}") for i in range(SLOTS)]
        x_in = [sem(f"x_in{t}") for t in range(NT)]
        cols_in, ident_in, keep_in, tmp_in, small_in, wr_in, bias_in = sems(
            "cols_in ident_in keep_in tmp_in small_in wr_in bias_in")
        job_done, out_scalar, out_vector = sems("job_done out_scalar out_vector")
        vector_chain, pool_chain = sems("vector_chain pool_chain")
        cs_ready, cb_ready, ssq_ready, std_ready, xn_ready = sems("cs_ready cb_ready ssq_ready std_ready xn_ready")
        h_parts, wr_parts, w_hi_ready, w_lo_ready, chunk_used = sems("h_parts wr_parts w_hi_ready w_lo_ready chunk_used")
        cat_hi_ready, cat_lo_ready, h2_hi_ready, h2_lo_ready, x1_saved = sems(
            "cat_hi_ready cat_lo_ready h2_hi_ready h2_lo_ready x1_saved")
        pads_zero, pooled, neg_abs, gate_exp, softplus, b_ready = sems("pads_zero pooled neg_abs gate_exp softplus b_ready")
        exp_ready, qe_ready, kd_ready, att_zero = sems("exp_ready qe_ready kd_ready att_zero")
        ss_done, ss_root, rst_ready, cat_ready, scaled, h2_scaled, h2_first, h2_ready, lgt_done, lgt_out, chosen, routed = sems(
            "ss_done ss_root rst_ready cat_ready scaled h2_scaled h2_first h2_ready lgt_done lgt_out chosen routed")
        g2_saved, moe_init, first_weights, sum_zero = sems("g2_saved moe_init first_weights sum_zero")
        rank_cols, p_ready, gath, rows_ready, turned, xg_ready, pt_psum, pt_ready, w_ready = sems(
            "rank_cols onehot_ready gathered rows_ready turned xg_ready pt_psum pt_ready w_ready")
        a_done, sil_ready, hid_ready, t_done, hidt_ready = sems(
            "up_done sil_ready hid_ready hid_transposed hidt_ready")
        y_done, yh_ready, yl_ready, c_done, acc_done = sems("down_done yh_ready yl_ready combined acc_done")
        extra_a1, extra_sil = sems("extra_a1 extra_silu")
        extra, extra_vector, extra_down, extra_hi, extra_lo, extra_c = sems(
            "extra_step extra_vector extra_down extra_hi extra_lo extra_combined")
        fin_add, end_pool, fin_table = sems("fin_add end_pool fin_table")
        end_ready, tail_in, fin_mul, fin_ssq, fin_std, fin_rec, fin, stored = sems(
            "end_ready tail_in fin_mul fin_ssq fin_std fin_rec fin stored")

        block = ctx.enter_context(nc.Block())

        w_mod, w_in, w_out = A["w_mod"][0], A["w_in"][0], A["w_out"][0]
        def rows(w):
            return w.rearrange("(k p) n -> p k n", p=P)

        def unit(slot, k):
            return ring[:, slot, :].rearrange("p (k n) -> p k n", k=k)

        def pre_source(n):
            name = STREAM[n]
            if name[0] == "m":
                i = int(name[1:])
                return rows(w_mod)[:, :, i * 512:(i + 1) * 512]
            if name[:2] == "wo":
                i = int(name[2:])
                return rows(w_out)[:, :, i * 512:(i + 1) * 512]
            i = dict(u=0, qk=1, v=2, g=3)[name]
            return rows(w_in)[:, :, i * 512:(i + 1) * 512]

        s0 = (UPP * (PAIRS - 1) - 2) % SLOTS
        assert s0 + 1 < SLOTS
        tail_x = ring[:, s0, :].rearrange("p (t n) -> p t n", t=NT)
        tail_g2, tail_fg = ring[:, s0 + 1, 0:D], ring[:, s0 + 1, D:2 * D]

        w1_r = A["w1"][0].rearrange("e (k p) n -> p e k n", p=P)
        w3_r = A["w3"][0].rearrange("e (k p) n -> p e k n", p=P)
        w2_r = A["w2"][0].rearrange("e (k p) n -> p e k n", p=P)

        def landed_at(n, it):
            slot = n % SLOTS
            return 16 * (PRE_USES[slot] + n // SLOTS + 1) + 16 * 3 * it

        def full(eng, name):
            eng.wait_ge(job_done, JOB[name] + 1)
            return bank[JOB[name] % 8]

        def read_out(eng, name):
            if name in OUT_SCALAR:
                eng.wait_ge(out_scalar, OUT_SCALAR.index(name) + 1)
            else:
                eng.wait_ge(out_vector, OUT_VECTOR.index(name) + 1)

        def further_rounds(eng, p, extra_round):
            most = eng.value_load(count_i[0:1, bass.ds(p, 1)], min_val=0, max_val=S)
            with eng.If(most > CAP):
                extra_round(1)
                with eng.If(most > 2 * CAP):
                    with eng.Fori(2, ROUNDS) as r:
                        with eng.If(most > r * CAP):
                            extra_round(r)

        def used_up(eng, n):
            name = STREAM[n]
            if name in SPLIT:
                count = KD * (SPLIT.index(name) + 1)
                eng.wait_ge(w_hi_ready, count)
                eng.wait_ge(w_lo_ready, count)
            else:
                eng.wait_ge(job_done, JOB["mr" + name[1:]] + 1)

        @block.sync
        def _(sp):
            x_r = A["x"][0].rearrange("(t p) n -> p t n", p=P)
            sp.dma_start(cols, A["cols"]).then_inc(cols_in, 16)
            for t in range(NT):
                sp.dma_start(x1[:, t, :], x_r[:, t, :]).then_inc(x_in[t], 16)
            for n in range(PRE_UNITS):
                slot = n % PRE_SLOTS
                if n >= PRE_SLOTS:
                    used_up(sp, n - PRE_SLOTS)
                sp.dma_start(unit(slot, KD), pre_source(n)).then_inc(landed[slot], 16)

            def expert_unit(n, it):
                slot = n % SLOTS
                pair, k = n // UPP, n % UPP
                e = 2 * (PPI * it + pair) + k % 2
                w, kk = ((w1_r, KD), (w3_r, KD), (w2_r, KF))[k // 2]
                src = w[:, bass.ds(e, 1), :, :].rearrange("p e k n -> p (e k) n")
                sp.dma_start(unit(slot, kk), src).then_inc(landed[slot], 16)

            sp.wait_ge(g2_saved, 16)
            for n in (2, 3, 0, 1, 4, 5, 6, 7):
                if n < PRE_SLOTS:
                    used_up(sp, [m for m in range(PRE_UNITS) if m % PRE_SLOTS == n][-1])
                elif n == PRE_SLOTS:
                    read_out(sp, "wo13")
                    sp.dma_start(x1_row.rearrange("(t p) n -> p t n", p=P), x1[:, :, :]).then_inc(x1_saved, 16)
                    sp.wait_ge(job_done, JOB["wo13"] + 1)
                elif n == 6:
                    sp.wait_ge(routed, 1)
                    sp.wait_ge(job_done, len(JOBS))
                    sp.wait_ge(out_vector, len(OUT_VECTOR))
                expert_unit(n, 0)
            per = UPP * PPI
            extra_n = sp.alloc_register("sp_extra_rounds")
            sp.reg_mov(extra_n, 1)

            def slot_used_up(n, it):
                pair, k = (n - SLOTS) // UPP, (n - SLOTS) % UPP
                p = PPI * it + pair
                if k == 0:
                    further_rounds(sp, p, lambda r: sp.reg_add(extra_n, extra_n, 1))
                if k < 4:
                    if k % 2 == 0:
                        rounds = sp.snap(extra_n)
                    sp.wait_ge(a_done, 2 * p + (1 + k // 2 + A_AHEAD))
                    if k == 0:
                        sp.wait_ge(extra_a1, rounds)
                    elif k == 2:
                        sp.wait_ge(extra, rounds * EXTRA_STEPS - (EXTRA_STEPS - 1))
                else:
                    sp.wait_ge(y_done, 2 * p + (2 + Y_AHEAD))

            with sp.Fori(0, ITERS - 1) as it:
                for n in range(SLOTS, SLOTS + per):
                    slot_used_up(n, it)
                    expert_unit(n, it)
            for n in range(SLOTS, per):
                slot_used_up(n, ITERS - 1)
                expert_unit(n, ITERS - 1)
            sp.wait_ge(x1_saved, 16)
            sp.wait_ge(y_done, 2 * (PAIRS - 1) + Y_AHEAD)
            sp.dma_start(tail_g2, g2_row.to_broadcast([P, D])).then_inc(tail_in, 16)
            sp.dma_start(tail_x, x1_row.rearrange("(t p) n -> p t n", p=P)).then_inc(tail_in, 16)
            sp.dma_start(tail_fg, A["final_g"].rearrange("(a n) -> a n", a=1).to_broadcast([P, D])).then_inc(tail_in, 16)
            out_r = out[0].rearrange("(t p) n -> p t n", p=P)
            for t in range(NT):
                sp.wait_ge(fin, t + 1)
                sp.dma_start(out_r[:, t, :], acc[:, t, :]).then_inc(stored, 16)
            sp.wait_ge(stored, 16 * NT)

        def h2_tile(eng, t):
            if t < POOL_T:
                eng.wait_ge(h2_first, t + 1)
            else:
                eng.wait_ge(h2_ready, t + 1 - POOL_T)

        def partial_bank(t):
            return bank[JOB[f"hT{t // 2}{t % 2}"] % 8]

        @block.tensor
        def _(pe):
            mm = nc.tensor.matmul
            todo = iter(JOBS)

            def start(name):
                assert next(todo) == name, name
                j = JOB[name]
                if j >= 8:
                    read_out(pe, JOBS[j - 8])
                return bank[j % 8]

            def slot_in(name, k=KD):
                n = SU[name]
                pe.wait_ge(landed[n % PRE_SLOTS], 16 * (n // PRE_SLOTS + 1))
                return unit(n % PRE_SLOTS, k)

            def mod_rows(i):
                b = start(f"mr{i}")
                w = slot_in(f"m{i}")
                for k in range(KD):
                    j = k % 4
                    last = mm(b[32 * j:32 * j + 32, :], cb[:, k, :], w[:, k, :], start=k < 4, stop=k >= 4,
                              tile_position=(0, 32 * j), skip_group_check=True)
                last.then_inc(job_done, 1)

            pe.wait_ge(cb_ready, 1)

            columns = bank[JOB["mcol"] % 8]
            assert JOB["mcol"] < 8

            def mod_columns(i0, i1):
                read_out(pe, f"mr{i1 // 4 - 1}")
                for i in range(i0, i1):
                    last = mm(columns[:, i:i + 1], modr[:, i * P:(i + 1) * P], sel[:, 0:1], start=True, stop=True)
                return last

            def x_transposed(k):
                b = start(f"xT{k}")
                for t in range(NT):
                    last = nc.tensor.transpose(b[:, t * P:(t + 1) * P], xn[:, t, k * P:(k + 1) * P], ident)
                last.then_inc(job_done, 1)

            mod_rows(0)
            mod_rows(1)
            pe.wait_ge(tmp_in, 16)
            mod_columns(0, 8)
            mod_rows(2)
            mod_columns(8, 12)
            mod_rows(3)
            start("mcol")
            mod_columns(12, 16).then_inc(job_done, 1)
            pe.wait_ge(xn_ready, NT)
            pe.wait_ge(ident_in, 16)
            for k in range(KD):
                x_transposed(k)

            def three(out_, hi, lo, w_h, w_l, k, stop, stationary_w):
                for n, (x_, y_) in enumerate(((hi, w_h), (hi, w_l), (lo, w_h))):
                    lhs, rhs = (y_, x_) if stationary_w else (x_, y_)
                    last = mm(out_, lhs, rhs, start=k == 0 and n == 0, stop=stop and n == 2)
                return last

            def low_rank():
                b = start("r")
                pe.wait_ge(wr_parts, 1)
                for k in range(KD):
                    last = three(b[:, :], h_hi[:, k, :], h_lo[:, k, :], wr_hi[:, k, :], wr_lo[:, k, :], k, k == KD - 1, True)
                last.then_inc(job_done, 1)

            def product(unit_name, names, a_hi, a_lo, stationary_w, ready=None):
                banks = []
                for k in range(KD):
                    c = KD * SPLIT.index(unit_name) + k
                    pe.wait_ge(w_hi_ready, c + 1)
                    pe.wait_ge(w_lo_ready, c + 1)
                    if ready is not None:
                        ready(k)
                    for i in range(4):
                        if k == 0:
                            banks.append(start(names[i]))
                        b = banks[i]
                        s_ = slice(i * P, (i + 1) * P)
                        if stationary_w:
                            last = three(b[:, :], a_hi[:, k, :], a_lo[:, k, :], w_hi[:, c % DEPTH, s_], w_lo[:, c % DEPTH, s_],
                                         k, k == KD - 1, True)
                        else:
                            ah, al = (a_hi[:, k], a_lo[:, k]) if unit_name[0] != "w" else (a_hi[k // 4][:, k % 4], a_lo[k // 4][:, k % 4])
                            last = three(b[:, :], ah[:, s_], al[:, s_], w_hi[:, c % DEPTH, :], w_lo[:, c % DEPTH, :],
                                         k, k == KD - 1, False)
                        if k == KD - 1:
                            last.then_inc(job_done, 1)
                    if k < KD - 1:
                        last.then_inc(chunk_used, 1)

            product("u", [f"u{i}" for i in range(4)], h_hi, h_lo, True, lambda k: pe.wait_ge(h_parts, k + 1))
            low_rank()
            product("qk", ["q0", "q1", "k0", "k1"], h_hi, h_lo, True)
            read_out(pe, "r")
            pe.wait_ge(small_in, 48)
            for i in range(4):
                b = start(f"gk{i}")
                mm(b[:, :], wup[:, i // 2, (i % 2) * P:(i % 2 + 1) * P], r_t, start=True, stop=True).then_inc(job_done, 1)
            product("v", [f"v{i}" for i in range(4)], h_hi, h_lo, False)
            for g in range(4):
                b = start(f"yp{g}")
                pe.wait_ge(pooled, g + 1)
                o, left, _ = POOL_AT[g]
                mm(b[:, :], wpool[:, g, :], up[:, o + left:o + left + S], start=True, stop=True).then_inc(job_done, 1)
            product("g", [f"g{i}" for i in range(4)], h_hi, h_lo, True)

            def mod_pair(i):
                for j in (i, i + 1):
                    mod_rows(j)
                for j in (i, i + 1):
                    b = start(f"mb{j}")
                    read_out(pe, f"mr{j}")
                    mm(b[:, :], sel, mrow[:, j % 2, :], start=True, stop=True).then_inc(job_done, 1)

            mod_pair(4)
            mod_pair(6)
            for d in range(2):
                for pr in range(2):
                    b = [start(f"att{d}{2 * pr + hh}") for hh in range(2)]
                    pe.wait_ge(qe_ready, 2 * d + pr + 1)
                    for t in range(NT):
                        c = slice(t * P, (t + 1) * P)
                        for hh in range(2):
                            r = slice(hh * DK, (hh + 1) * DK)
                            last = mm(b[hh][:, c], ke[r, d, pr, c], qe[r, d, pr, c], start=True, stop=True)
                            if t == NT - 1:
                                last.then_inc(job_done, 1)
            for d in range(2):
                for pr in range(2):
                    b = start(f"kdt{d}{pr}")
                    pe.wait_ge(kd_ready, 2 * d + pr + 1)
                    for t in range(NT):
                        c = slice(t * P, (t + 1) * P)
                        last = nc.tensor.transpose(b[:, c], kd[:, d, pr, c], ident)
                    last.then_inc(job_done, 1)
            mod_pair(8)
            read_out(pe, "v3")
            for d in range(2):
                for pr in range(2):
                    read_out(pe, f"kdt{d}{pr}")
                    b = [start(f"upd{d}{pr}{par}") for par in range(2)]
                    for t in range(NT):
                        for hh in range(2):
                            for par in range(2):
                                r = slice(par * CHUNK, (par + 1) * CHUNK)
                                h = 2 * pr + hh
                                last = mm(b[par][hh * DK:(hh + 1) * DK, t * P:(t + 1) * P],
                                          kdtok[r, d, pr, t, hh * DK:(hh + 1) * DK],
                                          v_s[r, t, h * DV:(h + 1) * DV], start=True, stop=True)
                                if t == NT - 1 and hh == 1:
                                    last.then_inc(job_done, 1)
            mod_pair(10)
            for pr in range(2):
                b = [start(f"o{2 * pr + hh}") for hh in range(2)]
                read_out(pe, "att13")
                read_out(pe, f"upd1{pr}1")
                for t in range(NT):
                    for hh in range(2):
                        h = 2 * pr + hh
                        mm(b[hh][:, t * P:(t + 1) * P], v_s[:, t, h * DV:(h + 1) * DV], att[:, h, t * P:(t + 1) * P],
                           start=True, stop=False)
                    parts = []
                    for ch in (2 * t, 2 * t + 1):
                        if ch > 0:
                            parts.append((0, ch, ch - 1))
                        if ch < NCH - 1:
                            parts.append((1, ch, ch))
                    for n, (d, ch, si) in enumerate(parts):
                        c = slice(ch * CHUNK, (ch + 1) * CHUNK)
                        for hh in range(2):
                            r = slice(hh * DK, (hh + 1) * DK)
                            last = mm(b[hh][:, c], st[d][r, pr, si, :], qe[r, d, pr, c], start=False, stop=n == len(parts) - 1)
                            if t == NT - 1 and n == len(parts) - 1:
                                last.then_inc(job_done, 1)
            squares = bank[JOB["rb3"] % 8]

            def sums_of_squares():
                read_out(pe, "mb11")
                for h in range(HEADS):
                    read_out(pe, f"o{h}")
                    last = mm(squares[32 * h:32 * h + 32, :], ones[:, 0:32], sq[:, h, :], start=True, stop=True,
                              tile_position=(0, 32 * h), skip_group_check=True)
                last.then_inc(ss_done, 1)

            def norms_spread():
                pe.wait_ge(rst_ready, 1)
                for h in range(HEADS):
                    b = norm_banks[h]
                    r_ = slice(32 * h, 32 * h + 32)
                    mm(b[:, :], sel[r_, :], rst[r_, :], start=True, stop=True, tile_position=(32 * h, 0)).then_inc(job_done, 1)

            def cat_parts(k):
                pe.wait_ge(cat_hi_ready, k + 1)
                pe.wait_ge(cat_lo_ready, k + 1)

            def cat_parts_and_norms(k):
                if k == 1:
                    sums_of_squares()
                elif k == 3:
                    norms_spread()
                cat_parts(k)

            norm_banks = [start(f"rb{h}") for h in range(HEADS)]
            for hf in range(2):
                product(f"wo{hf}", [f"wo{hf}{t}" for t in range(NT)], cat_hi, cat_lo, False,
                        cat_parts if hf else cat_parts_and_norms)
            pe.wait_ge(keep_in, 48)
            lg = bank[JOB["lg"] % 8]
            assert JOB["lg"] - 8 == JOB["hT00"]

            def router(t):
                read_out(pe, f"hT{t}1")
                for k in range(KD):
                    j = k % 4
                    last = mm(partial_bank(t)[32 * j:32 * j + 32, 0:P], wrt[:, k, :], h2t[:, k, t * P:(t + 1) * P],
                              start=k < 4, stop=k >= 4, tile_position=(0, 32 * j), skip_group_check=True)
                last.then_inc(lgt_done, 1)

            def logits(t):
                pe.wait_ge(lgt_out, t + 1)
                return mm(lg[:, t * E_N:(t + 1) * E_N], logits_t[:, t * P:(t + 1) * P], fold, start=True, stop=True)

            for t in range(NT):
                for hf in range(2):
                    b = start(f"hT{t}{hf}")
                    h2_tile(pe, t)
                    for j in range(4):
                        k = 4 * hf + j
                        last = nc.tensor.transpose(b[:, j * P:(j + 1) * P], h2[:, t, k * P:(k + 1) * P], ident)
                    last.then_inc(job_done, 1)
                if t > 0:
                    router(t - 1)
                if t > 1:
                    logits(t - 2)
            router(NT - 1)
            start("lg")
            logits(NT - 2)
            logits(NT - 1).then_inc(job_done, 1)
            b = start("rk")
            pe.wait_ge(chosen, 1)
            for t in range(NT):
                for u in range(t + 1):
                    last = mm(b[:, t * E_N:(t + 1) * E_N], lower_b if u == t else ones_b, chosen_b[:, u, :],
                              start=u == 0, stop=u == t)
            last.then_inc(job_done, 1)
            b = start("cnt")
            for u in range(NT):
                last = mm(b[:, 0:E_N], ones_b, chosen_b[:, u, :], start=u == 0, stop=u == NT - 1)
            last.then_inc(job_done, 1)
            pe.wait_ge(out_vector, len(OUT_VECTOR))
            pe.wait_ge(out_scalar, len(OUT_SCALAR))

            A1, A3, TB, Y0, Y1, G0, G1, CA = bank
            SUM_BANKS = (TB, CA, Y0, Y1)
            EXTRA_BANKS = (TB, CA, A1, A3, G0, G1, Y0, Y1)
            extra_n = pe.alloc_register("pe_extra_rounds")
            pe.reg_mov(extra_n, 0)

            def gather(done=None):
                for hf, g in ((0, G0), (1, G1)):
                    c = slice(hf * 512, (hf + 1) * 512)
                    for t in range(NT):
                        mm(g[:, :], onehot_t[:, t, :], h2_hi[:, t, c], start=t == 0, stop=False)
                        last = mm(g[:, :], onehot_t[:, t, :], h2_lo[:, t, c], start=False, stop=t == NT - 1)
                    if done is not None:
                        last.then_inc(done, 1)
                return last

            def turn_rows(rows_, done=None):
                for k in range(KD):
                    g = (G0, G1)[k // 4]
                    last = nc.tensor.transpose(g[:, (k % 4) * P:(k % 4 + 1) * P], rows_[:, k * P:(k + 1) * P], ident)
                    if done is not None and k % 4 == 3:
                        last.then_inc(done, 1)
                return last

            def slots_to_partitions():
                for t in range(NT):
                    nc.tensor.transpose(CA[:, t * P:(t + 1) * P], onehot[:, t, :], ident)
                for e in range(2):
                    for t in range(NT):
                        last = mm(A1[e * CAP:(e + 1) * CAP, 0:1], onehot[:, t, e * CAP:(e + 1) * CAP],
                                  gw_pair[:, t, e:e + 1], start=t == 0, stop=t == NT - 1)
                return last

            def up_product(n0, xb, w):
                bk = (A1, A3)[w]
                for k in range(KD):
                    for e in range(2):
                        n = n0 + 2 * w + e
                        last = mm(bk[e * CAP:(e + 1) * CAP, :], xb[:, k, e * CAP:(e + 1) * CAP],
                                  unit(n % SLOTS, KD)[:, k, :], start=k == 0, stop=k == KD - 1)
                return last

            def down_half(n0, hf):
                bk = (Y0, Y1)[hf]
                for k in range(KF):
                    for e in range(2):
                        n = n0 + 4 + e
                        last = mm(bk[e * CAP:(e + 1) * CAP, :], hid_t[:, k, e * CAP:(e + 1) * CAP],
                                  unit(n % SLOTS, KF)[:, k, hf * 512:(hf + 1) * 512],
                                  start=k == 0, stop=k == KF - 1)
                return last

            def combine_group(g, pt, bk):
                t, hf = g // 2, g % 2
                c = slice(hf * 512, (hf + 1) * 512)
                mm(bk[:, :], slot_tok[:, pt, t * P:(t + 1) * P], y_hi[:, c], start=True, stop=False)
                return mm(bk[:, :], slot_tok[:, pt, t * P:(t + 1) * P], y_lo[:, c], start=False, stop=True)

            def combine(p, pt, groups):
                for g in groups:
                    if g == 0:
                        pe.wait_ge(yh_ready, 2 * p + 2)
                        pe.wait_ge(yl_ready, 2 * p + 2)
                        pe.wait_ge(pt_ready, p + 2)
                        pe.wait_ge(hidt_ready, p + 1)
                    elif g >= 4:
                        pe.wait_ge(acc_done, 8 * p + (g - 3))
                    combine_group(g, pt, SUM_BANKS[g % 4]).then_inc(c_done, 1)

            def next_gather(q, first=False):
                pe.wait_ge(p_ready, q + 1)
                if not first:
                    pe.wait_ge(xg_ready, 2 * q)
                gather(gath)
                if not first:
                    pe.wait_ge(acc_done, 8 * q)
                    pe.wait_ge(sil_ready, q)
                else:
                    pe.wait_ge(first_weights, 1)
                    pe.wait_ge(routed, 1)
                slots_to_partitions().then_inc(pt_psum, 1)

            def next_turn(q):
                pe.wait_ge(rows_ready, 2 * q + 2)
                turn_rows(xg_rows, turned)

            pe.wait_ge(moe_init, 1)
            pe.wait_ge(h2_lo_ready, NT)
            next_gather(0, first=True)
            next_turn(0)
            def pair(it, j, last_pair=False):
                p = it * PPI + j
                n0 = UPP * j
                pe.wait_ge(xg_ready, 2 * p + 2)
                pe.wait_ge(w_ready, p + 1)
                for w in range(2):
                    if w == 1:
                        pe.wait_ge(hid_ready, p + 1)
                    for e in range(2):
                        n = n0 + 2 * w + e
                        pe.wait_ge(landed[n % SLOTS], landed_at(n, it))
                    up_product(n0, xg[:, j % 2], w).then_inc(a_done, 1)
                    combine(p, (j + 1) % 2, range(4 * w, 4 * w + 4))

                def extra_round(r):
                    done = pe.snap(extra_n)
                    b0 = done * EXTRA_STEPS + EXTRA_AHEAD
                    pe.wait_ge(hid_ready, p + 2)
                    pe.wait_ge(acc_done, 8 * p + 8)
                    for e in range(2):
                        n = n0 + 4 + e
                        pe.wait_ge(landed[n % SLOTS], landed_at(n, it))
                    pe.wait_ge(extra, b0 + 1)
                    gather()
                    slots_to_partitions().then_inc(extra, 1)
                    pe.wait_ge(extra, b0 + 3)
                    turn_rows(extra_rows).then_inc(extra, 1)
                    pe.wait_ge(extra, b0 + 5)
                    up_product(n0, xg[:, (j + 1) % 2], 0).then_inc(extra_a1, 1)
                    up_product(n0, xg[:, (j + 1) % 2], 1).then_inc(extra, 1)
                    pe.wait_ge(extra, b0 + 7)
                    for k in range(KF):
                        last = nc.tensor.transpose(TB[:, k * P:(k + 1) * P], hid_x[:, k * P:(k + 1) * P], ident)
                    last.then_inc(extra, 1)
                    pe.wait_ge(extra, b0 + 9)
                    for hf in range(2):
                        down_half(n0, hf).then_inc(extra_down, 1)
                    for i, g in enumerate(HALVES_FIRST):
                        if i % 4 == 0:
                            pe.wait_ge(extra_lo, done * 2 + (i // 4 + 1))
                        last = combine_group(g, (j + 1) % 2, EXTRA_BANKS[i])
                        if i % 2:
                            last.then_inc(extra_c, 1)
                    pe.wait_ge(extra, b0 + EXTRA_STEPS)
                    pe.reg_add(extra_n, extra_n, 1)

                further_rounds(pe, p, extra_round)
                pe.wait_ge(hid_ready, p + 2)
                pe.wait_ge(acc_done, 8 * p + 5)
                for k in range(KF):
                    last = nc.tensor.transpose(TB[:, k * P:(k + 1) * P], hid[:, k * P:(k + 1) * P], ident)
                last.then_inc(t_done, 1)
                if not last_pair:
                    next_gather(p + 1)
                pe.wait_ge(hidt_ready, p + 2)
                for e in range(2):
                    n = n0 + 4 + e
                    pe.wait_ge(landed[n % SLOTS], landed_at(n, it))
                pe.wait_ge(acc_done, 8 * p + 8)
                down_half(n0, 0).then_inc(y_done, 1)
                if not last_pair:
                    next_turn(p + 1)
                down_half(n0, 1).then_inc(y_done, 1)
            with pe.Fori(0, ITERS - 1) as it:
                for j in range(PPI):
                    pair(it, j)
            for j in range(PPI):
                pair(ITERS - 1, j, j == PPI - 1)
            pe.wait_ge(pt_ready, PAIRS + 1)
            pe.wait_ge(hidt_ready, PAIRS + 1)
            for i, g in enumerate(HALVES_FIRST):
                if i % 4 == 0:
                    pe.wait_ge(yh_ready, 2 * PAIRS + 1 + i // 4)
                    pe.wait_ge(yl_ready, 2 * PAIRS + 1 + i // 4)
                combine_group(g, (PAIRS + 1) % 2, EXTRA_BANKS[i]).then_inc(c_done, 1)

        def part_free(eng, c):
            if c >= DEPTH:
                u, k = divmod(c - DEPTH, KD)
                if k < KD - 1:
                    eng.wait_ge(chunk_used, (KD - 1) * u + k + 1)
                else:
                    eng.wait_ge(job_done, JOB[LAST_JOB[u]] + 1)

        def raw_chunk(c):
            slot = SU[SPLIT[c // KD]] % PRE_SLOTS
            return unit(slot, KD)[:, c % KD, :]

        @block.scalar
        def _(act):
            a = nc.scalar.activation

            act.dma_start(cp, A["const_keep"]).then_inc(ident_in, 16)
            act.dma_start(ct, A["const_tmp"]).then_inc(tmp_in, 16)
            act.wait_ge(cols_in, 16)
            a(cs, col["c"], ACT.Silu).then_inc(cs_ready, 1)
            for t in range(NT):
                act.wait_ge(x_in[t], 16)
                a(xn[:, t, :], x1[:, t, :], ACT.Square, accum_out=ssq[:, t:t + 1]).then_inc(ssq_ready, 1)
            act.wait_ge(ssq_ready, NT)
            a(rstd, ssq, ACT.Sqrt, bias=col["eps"], scale=1.0 / D).then_inc(std_ready, 1)
            for i in range(4):
                b = full(act, f"mr{i}")
                nc.scalar.copy(modr[:, i * 512:(i + 1) * 512], b[:, :]).then_inc(out_scalar, 1)
            act.dma_start(wr_raw, A["wr"]).then_inc(wr_in, 16)
            act.dma_start(wup.rearrange("p d c -> p (d c)"), A["wup"]).then_inc(small_in, 16)
            act.dma_start(wpool.rearrange("p k c -> p (k c)"), A["wpool"]).then_inc(small_in, 16)
            act.dma_start(masks, A["masks"]).then_inc(small_in, 16)
            act.dma_start(wrt.rearrange("p k e -> p (k e)"), A["wrt"]).then_inc(keep_in, 16)
            act.dma_start(iota32, A["iota32"]).then_inc(keep_in, 16)
            act.dma_start(b_rt, A["b_router"].rearrange("(a n) -> a n", a=1).to_broadcast([P, E_N])).then_inc(keep_in, 16)
            def high_parts(c0, c1):
                for c in range(c0, c1):
                    n = SU[SPLIT[c // KD]]
                    if SPLIT[c // KD][0] == "w":
                        act.wait_ge(scaled, c - 4 * KD + 1)
                    elif c % KD == 0 or c == c0:
                        act.wait_ge(landed[n % PRE_SLOTS], 16 * (n // PRE_SLOTS + 1))
                    part_free(act, c)
                    nc.scalar.copy(w_hi[:, c % DEPTH, :], raw_chunk(c)).then_inc(w_hi_ready, 1)

            read_out(act, "mcol")
            for k in range(KD):
                b = full(act, f"xT{k}")
                if k >= 2:
                    act.wait_ge(h_parts, k - 1)
                a(h_tmp[:, k % 2, :], b[:, :], ACT.Identity, bias=modc[:, k:k + 1], scale=modc[:, 8 + k:9 + k]).then_inc(out_scalar, 1)
                if k < DEPTH:
                    high_parts(k, k + 1)
            high_parts(4, 12)
            act.wait_ge(pads_zero, 1)
            for g in range(4):
                b = full(act, f"u{g}")
                o, left, _ = POOL_AT[g]
                nc.scalar.copy(up[:, o + left:o + left + S], b[:, :]).then_inc(out_scalar, 1)
            b = full(act, "r")
            nc.scalar.copy(r_t, b[0:2 * RANK, :]).then_inc(out_scalar, 1)
            high_parts(12, 20)
            for i, name in enumerate(("q0", "q1", "k0", "k1")):
                b = full(act, name)
                dst = (q_s, q_s, k_s, k_s)[i][:, i % 2, :]
                a(dst, b[:, :], ACT.Copy, scale=DK ** -0.5 if i < 2 else 1.0).then_inc(out_scalar, 1)
            for i in range(4):
                b = full(act, f"gk{i}")
                a(la[:, i // 2, i % 2, :], b[:, :], ACT.Identity, bias=col["bgk"][:, i:i + 1]).then_inc(out_scalar, 1)
            high_parts(20, 22)
            for i in range(4):
                act.wait_ge(neg_abs, i + 1)
                a(bb[:, i // 2, i % 2, :], bb[:, i // 2, i % 2, :], ACT.Exp).then_inc(gate_exp, 1)
            high_parts(22, 24)
            for i in range(4):
                act.wait_ge(gate_exp, i + 1)
                a(bb[:, i // 2, i % 2, :], bb[:, i // 2, i % 2, :], ACT.Ln, bias=1.0).then_inc(softplus, 1)
            high_parts(24, 28)
            for g in range(4):
                b = full(act, f"yp{g}")
                a(cat[:, g, :], b[:, :], ACT.Copy, scale=col["pscale"][:, g:g + 1]).then_inc(out_scalar, 1)
            high_parts(28, 32)
            for h in range(HEADS):
                b = full(act, f"g{h}")
                a(g_s[:, h, :], b[:, :], ACT.Silu).then_inc(out_scalar, 1)
            act.wait_ge(b_ready, 4)

            def decays(i):
                d, pr = i // 2, i % 2
                a(qe[:, d, pr, :], bb[:, d, pr, :], ACT.Exp, scale=1.0 / GATE_NORM).then_inc(exp_ready, 1)
                a(ke[:, d, pr, :], bb[:, d, pr, :], ACT.Exp, scale=-1.0 / GATE_NORM).then_inc(exp_ready, 1)
                whole = bb[:, d, pr, :].rearrange("p (c n) -> p c n", n=CHUNK)[:, :, (CHUNK - 1) if d == 0 else 0]
                a(decay[:, i, :], whole, ACT.Exp, scale=1.0 / GATE_NORM).then_inc(exp_ready, 1)

            def mod_part(i):
                b = full(act, f"mr{i}")
                if i >= 6:
                    act.wait_ge(job_done, JOB[f"mb{i - 2}"] + 1)
                nc.scalar.copy(mrow[:, i % 2, :], b[:, :]).then_inc(out_scalar, 1)

            for i in range(4):
                decays(i)
                mod_part(4 + i)
            for i in range(4):
                b = full(act, f"kdt{i // 2}{i % 2}")
                if i == 0:
                    act.wait_ge(kd_ready, 4)
                nc.scalar.copy(kdtok[:, i // 2, i % 2, :, :].rearrange("p t c -> p (t c)"), b[:, :]).then_inc(out_scalar, 1)
            for i in range(8, 12):
                mod_part(i)
            def high_cat(k):
                nc.scalar.copy(cat_hi[k // 4][:, k % 4, :], cat[:, k, :]).then_inc(cat_hi_ready, 1)

            read_out(act, "yp3")
            act.wait_ge(job_done, JOB["upd111"] + 1)
            for k in range(4):
                high_cat(k)
            act.wait_ge(job_done, JOB["mb11"] + 1)
            act.wait_ge(g2_saved, 16)
            high_parts(32, 36)
            for h in range(HEADS):
                b = full(act, f"o{h}")
                a(cat[:, 4 + h, :], b[:, :], ACT.Copy, scale=col["ng"])
                a(sq[:, h, :], b[:, :], ACT.Square).then_inc(out_scalar, 1)
            act.wait_ge(ss_done, 1)
            a(rst, bank[JOB["rb3"] % 8][:, :], ACT.Sqrt, bias=col["eps"], scale=1.0 / DV).then_inc(ss_root, 1)
            for k in range(4, KD):
                high_parts(4 * KD + k, 4 * KD + k + 1)
                act.wait_ge(cat_ready, k - 3)
                high_cat(k)
            high_parts(40, 48)
            for t in range(NT):
                read_out(act, f"wo1{t}")
                a(h2[:, t, :], x1[:, t, :], ACT.Square, accum_out=ssq[:, t:t + 1]).then_inc(ssq_ready, 1)
                act.wait_ge(ssq_ready, NT + t + 1)
                a(rstd[:, t:t + 1], ssq[:, t:t + 1], ACT.Sqrt, bias=col["eps"], scale=1.0 / D).then_inc(std_ready, 1)
            a(table_in, col["eps"], ACT.Sigmoid)

            def partial_sums(t):
                act.wait_ge(lgt_done, t + 1)
                c = slice(t * P, (t + 1) * P)
                nc.scalar.copy(logits_t[:, c], partial_bank(t)[:, 0:P]).then_inc(lgt_out, 1)

            for t in range(NT):
                for hf in range(2):
                    b = full(act, f"hT{t}{hf}")
                    dst = h2t[:, 4 * hf:4 * hf + 4, t * P:(t + 1) * P]
                    nc.scalar.copy(dst, b[:, :].rearrange("p (k t) -> p k t", k=4)).then_inc(out_scalar, 1)
                if t > 0:
                    partial_sums(t - 1)
            partial_sums(NT - 1)
            b = full(act, "lg")
            a(rt_s.rearrange("p t e -> p (t e)"), b[:, 0:NT * E_N], ACT.Sigmoid).then_inc(out_scalar, 1)

            A1, A3, TB, Y0, Y1, G0, G1, CA = bank
            extra_n = act.alloc_register("act_extra_rounds")
            act.reg_mov(extra_n, 0)

            def take_rows(to, done=None, gate=None):
                for hf, g in ((0, G0), (1, G1)):
                    if gate is not None:
                        act.wait_ge(gath, gate + hf)
                    ins = nc.scalar.copy(to[:, hf * 512:(hf + 1) * 512], g[:, :])
                    if done is not None:
                        ins.then_inc(done, 1)
                return ins

            def take_turned(buf, hf):
                return nc.scalar.copy(xg[:, buf, 4 * hf:4 * hf + 4, :].rearrange("p k s -> p (k s)"), (G0, G1)[hf][:, :])

            def gathered(q, buf, first=False):
                take_rows(xg_rows, rows_ready, 2 * q + 1)
                act.wait_ge(pt_psum, q + 1)
                if not first:
                    act.wait_ge(c_done, 8 * q)
                nc.scalar.copy(slot_tok[:, buf, :], CA[:, :]).then_inc(pt_ready, 1)
                if not first:
                    act.wait_ge(yl_ready, 2 * q)
                nc.scalar.copy(w_slot[:, buf:buf + 1], A1[:, 0:1]).then_inc(w_ready, 1)

            def turned_rows(q, buf, first=False):
                if not first:
                    act.wait_ge(a_done, 2 * q)
                for hf in range(2):
                    act.wait_ge(turned, 2 * q + hf + 1)
                    take_turned(buf, hf).then_inc(xg_ready, 1)

            def take_down(buf, hf):
                return a(y_hi[:, hf * 512:(hf + 1) * 512], (Y0, Y1)[hf][:, :], ACT.Copy, scale=w_slot[:, buf:buf + 1])

            act.wait_ge(moe_init, 1)
            gathered(0, 0, first=True)
            turned_rows(0, 0, first=True)
            def pair(it, j, last_pair=False):
                p = it * PPI + j
                act.wait_ge(a_done, 2 * p + 1 + A_AHEAD)
                act.wait_ge(hid_ready, p + 1)
                a(sil, A1[:, :], ACT.Silu).then_inc(sil_ready, 1)

                def extra_round(r):
                    done = act.snap(extra_n)
                    b0 = done * EXTRA_STEPS + EXTRA_AHEAD
                    nb = (j + 1) % 2
                    act.wait_ge(extra, b0 + 2)
                    take_rows(extra_rows).then_inc(extra, 1)
                    nc.scalar.copy(slot_tok[:, nb, :], CA[:, :])
                    nc.scalar.copy(w_slot[:, nb:nb + 1], A1[:, 0:1])
                    act.wait_ge(extra, b0 + 4)
                    take_turned(nb, 0)
                    take_turned(nb, 1).then_inc(extra, 1)
                    act.wait_ge(extra_a1, done + 2)
                    a(sil, A1[:, :], ACT.Silu).then_inc(extra_sil, 1)
                    act.wait_ge(extra, b0 + 8)
                    nc.scalar.copy(hid_t.rearrange("p k s -> p (k s)"), TB[:, :]).then_inc(extra, 1)
                    for hf in range(2):
                        act.wait_ge(extra_down, done * 2 + (hf + 1))
                        take_down(nb, hf).then_inc(extra_hi, 1)
                    act.reg_add(extra_n, extra_n, 1)

                further_rounds(act, p, extra_round)
                act.wait_ge(t_done, p + 1)
                act.wait_ge(y_done, 2 * p + Y_AHEAD)
                nc.scalar.copy(hid_t.rearrange("p k s -> p (k s)"), TB[:, :]).then_inc(hidt_ready, 1)
                if last_pair:
                    act.wait_ge(c_done, 8 * p + 8)
                    for hf in range(2):
                        c = slice(hf * 512, (hf + 1) * 512)
                        act.wait_ge(end_ready, hf + 1)
                        nc.scalar.copy(y_hi[:, c], y_end[:, c]).then_inc(yh_ready, 1)
                    return
                gathered(p + 1, (j + 1) % 2)
                act.wait_ge(y_done, 2 * p + 1 + Y_AHEAD)
                take_down(j % 2, 0).then_inc(yh_ready, 1)
                turned_rows(p + 1, (j + 1) % 2)
                act.wait_ge(y_done, 2 * p + 2 + Y_AHEAD)
                take_down(j % 2, 1).then_inc(yh_ready, 1)

            with act.Fori(0, ITERS - 1) as it:
                for j in range(PPI):
                    pair(it, j)
            for j in range(PPI):
                pair(ITERS - 1, j, j == PPI - 1)
            a(rstd[:, 0:1], col["eps"], ACT.Sqrt).then_inc(fin_table, 1)
            act.wait_ge(fin_table, 1)
            for t in range(NT):
                act.wait_ge(acc_done, 8 * PAIRS + HALVES_FIRST.index(2 * t + 1) + 1)
                a(x1[:, t, :], acc[:, t, :], ACT.Square, accum_out=ssq[:, t:t + 1]).then_inc(fin_ssq, 1)
                act.wait_ge(fin_ssq, t + 1)
                a(rstd[:, t:t + 1], ssq[:, t:t + 1], ACT.Sqrt, bias=col["eps"], scale=1.0 / D).then_inc(fin_std, 1)

        @block.vector
        def _(dve):
            v = nc.vector
            n_chain = [0]

            def link(ins):
                n_chain[0] += 1
                ins.then_inc(vector_chain, 1)
                dve.wait_ge(vector_chain, n_chain[0])

            dve.wait_ge(cs_ready, 1)
            v.tensor_copy(cb, cs.unsqueeze(2).to_broadcast([P, KD, 32])).then_inc(cb_ready, 1)
            dve.wait_ge(std_ready, 1)
            link(v.reciprocal(rstd, rstd))
            for t in range(NT):
                v.tensor_scalar(xn[:, t, :], x1[:, t, :], rstd[:, t:t + 1], None, ALU.mult).then_inc(xn_ready, 1)
            b = full(dve, "mcol")
            link(v.tensor_tensor(modc, b[:, 0:16], col["bmod"], ALU.add))
            v.tensor_scalar(modc[:, 8:16], modc[:, 8:16], 1.0, None, ALU.add).then_inc(out_vector, 1)
            def low_weights(c0, c1):
                for c in range(c0, c1):
                    dve.wait_ge(w_hi_ready, c + 1)
                    v.tensor_tensor(w_lo[:, c % DEPTH, :], raw_chunk(c), w_hi[:, c % DEPTH, :].bitcast(F32),
                                    ALU.subtract).then_inc(w_lo_ready, 1)

            for k in range(KD):
                read_out(dve, f"xT{k}")
                link(v.tensor_copy(h_hi[:, k, :], h_tmp[:, k % 2, :]))
                v.tensor_tensor(h_lo[:, k, :], h_tmp[:, k % 2, :], h_hi[:, k, :].bitcast(F32), ALU.subtract).then_inc(h_parts, 1)
                if k < DEPTH:
                    low_weights(k, k + 1)
            low_weights(4, 6)
            dve.wait_ge(wr_in, 16)
            link(v.tensor_copy(wr_hi[:, :, :].rearrange("p k c -> p (k c)"), wr_raw))
            v.tensor_tensor(wr_lo[:, :, :].rearrange("p k c -> p (k c)"), wr_raw,
                            wr_hi[:, :, :].rearrange("p k c -> p (k c)").bitcast(F32), ALU.subtract).then_inc(wr_parts, 1)
            low_weights(6, 20)
            for i in range(4):
                read_out(dve, f"gk{i}")
                y, t = la[:, i // 2, i % 2, :], bb[:, i // 2, i % 2, :]
                v.scalar_tensor_tensor(t, y, -1.0, y, ALU.mult, ALU.min).then_inc(neg_abs, 1)
            low_weights(20, 24)
            dve.wait_ge(tmp_in, 16)
            v.tensor_copy(lower_b, lower)
            v.tensor_copy(ones_b, ones)
            for i in range(4):
                dve.wait_ge(softplus, i + 1)
                y, t = la[:, i // 2, i % 2, :], bb[:, i // 2, i % 2, :]
                link(v.scalar_tensor_tensor(y, y, 0.0, t, ALU.min, ALU.subtract))
                if i // 2 == 0:
                    ins = v.tensor_tensor_scan(t, reset, y, 0.0, ALU.mult, ALU.add)
                else:
                    ins = v.tensor_tensor_scan(t[:, ::-1], reset, y[:, ::-1], 0.0, ALU.mult, ALU.add)
                ins.then_inc(b_ready, 1)
            low_weights(24, 28)
            for t in range(NT):
                b = full(dve, f"v{t}")
                v.tensor_copy(v_s[:, t, :], b[:, :]).then_inc(out_vector, 1)
            low_weights(28, 32)
            read_out(dve, "k1")

            def decayed(i):
                d, pr = i // 2, i % 2
                dve.wait_ge(exp_ready, 3 * i + 3)
                v.tensor_tensor(qe[:, d, pr, :], qe[:, d, pr, :], q_s[:, pr, :], ALU.mult)
                v.tensor_tensor(ke[:, d, pr, :], ke[:, d, pr, :], k_s[:, pr, :], ALU.mult).then_inc(qe_ready, 1)
                dve.wait_ge(qe_ready, i + 1)
                v.tensor_tensor(kd[:, d, pr, :].rearrange("p (c n) -> p c n", n=CHUNK),
                                ke[:, d, pr, :].rearrange("p (c n) -> p c n", n=CHUNK),
                                decay[:, i, :].unsqueeze(2).to_broadcast([P, NCH, CHUNK]), ALU.mult).then_inc(kd_ready, 1)

            def mod_row(i):
                b = full(dve, f"mb{i}")
                c = slice((i % 2) * 512, (i % 2 + 1) * 512)
                bias = bias_b[:, (i - 4) * 512:(i - 3) * 512]
                if i < 10:
                    v.scalar_tensor_tensor((g1b, sh2b, sc2b)[(i - 4) // 2][:, c], b[:, :], 1.0 if i in (8, 9) else 0.0, bias,
                                           ALU.add, ALU.add).then_inc(out_vector, 1)
                else:
                    v.tensor_tensor(g2row[:, c], b[0:1, :], bias[0:1, :], ALU.add).then_inc(out_vector, 1)

            dve.wait_ge(h_parts, KD)
            dve.wait_ge(wr_parts, 1)
            dve.wait_ge(bias_in, 16)
            decayed(0)
            decayed(1)
            mod_row(4)
            mod_row(5)
            decayed(2)
            decayed(3)
            mod_row(6)
            mod_row(7)
            dve.wait_ge(att_zero, 1)
            dve.wait_ge(small_in, 48)
            for d in range(2):
                for h in range(HEADS):
                    b = full(dve, f"att{d}{h}")
                    if d:
                        read_out(dve, f"att0{h}")
                    m = masks[:, d * P:(d + 1) * P].bitcast(I32).unsqueeze(1).to_broadcast([P, NT, P])
                    v.copy_predicated(att[:, h, :].rearrange("p (t i) -> p t i", t=NT), m,
                                      b[:, :].rearrange("p (t i) -> p t i", t=NT)).then_inc(out_vector, 1)
            mod_row(8)
            mod_row(9)
            for d in range(2):
                for pr in range(2):
                    full(dve, f"upd{d}{pr}0")
                    full(dve, f"upd{d}{pr}1")

                    def upd(n):
                        bk = bank[JOB[f"upd{d}{pr}{n % 2}"] % 8]
                        return bk[:, (n // 2) * P:(n // 2 + 1) * P]
                    order = list(range(NCH - 1)) if d == 0 else list(range(NCH - 1, 0, -1))
                    for i, n in enumerate(order):
                        s_out = st[d][:, pr, n if d == 0 else n - 1, :]
                        if i == 0:
                            ins = v.tensor_copy(s_out, upd(n))
                        else:
                            s_in = st[d][:, pr, n - 1 if d == 0 else n, :]
                            ins = v.scalar_tensor_tensor(s_out, s_in, decay[:, 2 * d + pr, n:n + 1], upd(n), ALU.mult, ALU.add)
                        if i < NCH - 2:
                            link(ins)
                        else:
                            ins.then_inc(out_vector, 2)
            mod_row(10)
            mod_row(11)

            def low_cat(k):
                dve.wait_ge(cat_hi_ready, k + 1)
                v.tensor_tensor(cat_lo[k // 4][:, k % 4, :], cat[:, k, :], cat_hi[k // 4][:, k % 4, :].bitcast(F32),
                                ALU.subtract).then_inc(cat_lo_ready, 1)

            read_out(dve, "mb11")
            for k in range(4):
                low_cat(k)
            low_weights(32, 36)
            dve.wait_ge(ss_root, 1)
            v.reciprocal(rst, rst).then_inc(rst_ready, 1)
            for h in range(HEADS):
                b = full(dve, f"rb{h}")
                o_ = cat[:, 4 + h, :]
                v.tensor_tensor(o_, b[:, :], o_, ALU.mult).then_inc(out_vector, 1)
                read_out(dve, f"rb{h}")
                v.tensor_tensor(o_, o_, g_s[:, h, :], ALU.mult).then_inc(cat_ready, 1)
                low_weights(4 * KD + 4 + h, 4 * KD + 5 + h)
                low_cat(4 + h)
            low_weights(40, 44)

            def residual(hf, t):
                b = full(dve, f"wo{hf}{t}")
                c = slice(hf * 512, (hf + 1) * 512)
                return v.tensor_tensor(x1[:, t, c], x1[:, t, c], b[:, :], ALU.add).then_inc(out_vector, 1)

            for t in range(NT):
                residual(0, t)
            low_weights(44, 48)
            for t in range(NT):
                residual(1, t)
            for t in range(NT):
                dve.wait_ge(std_ready, 2 + t)
                link(v.reciprocal(rstd[:, t:t + 1], rstd[:, t:t + 1]))
                v.scalar_tensor_tensor(h2[:, t, :], x1[:, t, :], rstd[:, t:t + 1], sc2b, ALU.mult,
                                       ALU.mult).then_inc(h2_scaled, 1)
                if t >= POOL_T:
                    dve.wait_ge(h2_scaled, t + 1)
                    v.tensor_tensor(h2[:, t, :], h2[:, t, :], sh2b, ALU.add).then_inc(h2_ready, 1)

            for t in range(NT):
                h2_tile(dve, t)
                v.tensor_copy(h2_hi[:, t, :], h2[:, t, :]).then_inc(h2_hi_ready, 1)
            dve.wait_ge(x1_saved, 16)
            for t in range(POOL_T, NT):
                dve.wait_ge(h2_hi_ready, t + 1)
                v.tensor_tensor(h2_lo[:, t, :], h2[:, t, :], h2_hi[:, t, :].bitcast(F32), ALU.subtract).then_inc(h2_lo_ready, 1)
            for s_, n_ in ((a_done, A_AHEAD), (y_done, Y_AHEAD), (hid_ready, 1), (hidt_ready, 1), (pt_ready, 1),
                           (yh_ready, 2), (yl_ready, 2), (extra, EXTRA_AHEAD), (extra_a1, 1)):
                dve.sem_inc(s_, n_)
            dve.sem_inc(moe_init, 1)
            v.memset(rankm[:, :, E_N:E_N + 2], 0.0)
            v.memset(gwt[:, :, E_N:E_N + 2], 0.0)

            dve.wait_ge(keep_in, 48)
            read_out(dve, "lg")
            gview = lambda z: z.rearrange("p t (g e) -> p t g e", g=G_N)
            big4 = [P, NT, G_N, EPG]
            iota_g = iota32[:, 0:G_N].unsqueeze(1).to_broadcast([P, NT, G_N])
            iota_e = iota32[:, 0:EPG].unsqueeze(1).to_broadcast([P, NT, EPG])
            link(v.tensor_tensor(rt_sel, rt_s, b_rt.unsqueeze(1).to_broadcast([P, NT, E_N]), ALU.add))
            for t in range(NT):
                for g in range(G_N):
                    ins = v.max(rt_srt[:, t, g, :], rt_sel[:, t, g * EPG:(g + 1) * EPG])
            link(ins)
            link(v.tensor_tensor(rt_gs, rt_srt[:, :, :, 0], rt_srt[:, :, :, 1], ALU.add))

            def first_of(onehot_out, values, target, n, iota_n, taken=None):
                link(v.tensor_tensor(onehot_out, values, target.unsqueeze(2).to_broadcast([P, NT, n]), ALU.is_equal))
                link(v.scalar_tensor_tensor(onehot_out, onehot_out, -100.0, iota_n, ALU.mult, ALU.add))
                if taken is not None:
                    link(v.scalar_tensor_tensor(onehot_out, taken, 1000.0, onehot_out, ALU.mult, ALU.add))
                link(v.tensor_reduce(rt_m, onehot_out, AX_X, ALU.min))
                link(v.tensor_tensor(onehot_out, onehot_out, rt_m.unsqueeze(2).to_broadcast([P, NT, n]), ALU.is_equal))

            link(v.tensor_reduce(rt_top, rt_gs, AX_X, ALU.max))
            first_of(rt_goh, rt_gs, rt_top, G_N, iota_g)
            goh4 = rt_goh.unsqueeze(3).to_broadcast(big4)
            link(v.tensor_tensor(gview(rt_tmp), gview(rt_sel), goh4, ALU.mult))
            link(v.tensor_reduce(rt_in, gview(rt_tmp).rearrange("p t g e -> p t e g"), AX_X, ALU.add))
            link(v.tensor_tensor(rt_srt, rt_srt, goh4, ALU.mult))
            link(v.tensor_reduce(rt_t12, rt_srt[:, :, :, 0:2].rearrange("p t g e -> p t e g"), AX_X, ALU.add))
            first_of(rt_oh1, rt_in, rt_t12[:, :, 0], EPG, iota_e)
            first_of(rt_oh2, rt_in, rt_t12[:, :, 1], EPG, iota_e, taken=rt_oh1)
            link(v.tensor_tensor(rt_oh1, rt_oh1, rt_oh2, ALU.add))
            link(v.tensor_tensor(gview(rt_a), goh4, rt_oh1.unsqueeze(2).to_broadcast(big4), ALU.mult))
            v.tensor_copy(chosen_b, rt_a).then_inc(chosen, 1)
            b = full(dve, "rk")
            v.scalar_tensor_tensor(rankm[:, :, 0:E_N], b[:, 0:NT * E_N].rearrange("p (t e) -> p t e", t=NT), 1.0, rt_a,
                                   ALU.add, ALU.mult).then_inc(out_vector, 1)
            b = full(dve, "cnt")
            v.tensor_reduce(count_f, b[:, 0:E_N].rearrange("p (a e) -> p a e", e=2), AX_X, ALU.max).then_inc(out_vector, 1)
            dve.wait_ge(out_vector, len(OUT_VECTOR))

            A1, A3, TB, Y0, Y1, G0, G1, CA = bank
            SUM_BANKS = (TB, CA, Y0, Y1)
            EXTRA_BANKS = (TB, CA, A1, A3, G0, G1, Y0, Y1)
            extra_n = dve.alloc_register("dve_extra_rounds")
            dve.reg_mov(extra_n, 0)
            iota8 = iota.unsqueeze(1).to_broadcast([P, NT * 2, CAP])

            def one_hot(q, off, cols_ready, cols_count, weights=True):
                v.tensor_scalar(rank_pair, rankm[:, :, bass.ds(2 * q, 2)], off, None, ALU.add).then_inc(cols_ready, 1)
                if weights:
                    v.tensor_copy(gw_pair, gwt[:, :, bass.ds(2 * q, 2)])
                dve.wait_ge(cols_ready, cols_count)
                return v.tensor_tensor(onehot_t[:, :, :].rearrange("p t (e s) -> p (t e) s", e=2),
                                       rank_pair.rearrange("p t e -> p (t e)").unsqueeze(2).to_broadcast([P, NT * 2, CAP]),
                                       iota8, ALU.is_equal)

            def low_part(buf, hf):
                c = slice(hf * 512, (hf + 1) * 512)
                return v.scalar_tensor_tensor(y_lo[:, c], (Y0, Y1)[hf][:, :], w_slot[:, buf:buf + 1], y_hi[:, c].bitcast(F32),
                                              ALU.mult, ALU.subtract)

            def add_group(g, bk):
                t, hf = g // 2, g % 2
                c = slice(hf * 512, (hf + 1) * 512)
                return v.tensor_tensor(acc[:, t, c], acc[:, t, c], bk[:, :], ALU.add)

            def add_up(p, groups):
                for g in groups:
                    dve.wait_ge(c_done, 8 * p + g + 1)
                    add_group(g, SUM_BANKS[g % 4]).then_inc(acc_done, 1)

            dve.wait_ge(job_done, len(JOBS))
            dve.wait_ge(out_scalar, len(OUT_SCALAR))
            one_hot(0, 0.0, rank_cols, 1, weights=False).then_inc(p_ready, 1)
            link(v.tensor_tensor(gwt[:, :, 0:E_N], rt_a, rt_s, ALU.mult))
            link(v.tensor_reduce(rt_m, gwt[:, :, 0:E_N], AX_X, ALU.add))
            link(v.reciprocal(rt_m, rt_m))
            link(v.tensor_tensor(gwt[:, :, 0:E_N], gwt[:, :, 0:E_N], rt_m.unsqueeze(2).to_broadcast([P, NT, E_N]), ALU.mult))
            v.tensor_copy(gw_pair, gwt[:, :, 0:2]).then_inc(first_weights, 1)
            v.tensor_copy(count_i, count_f).then_inc(routed, 1)
            dve.wait_ge(sum_zero, 1)
            def at_the_end(p, j):
                dve.wait_ge(tail_in, 48)
                dve.wait_ge(acc_done, 8 * p + 8)
                for t in range(2):
                    v.tensor_tensor(acc[:, t, :], acc[:, t, :], tail_g2, ALU.mult).then_inc(fin_mul, 1)
                for t in range(2):
                    dve.wait_ge(fin_mul, t + 1)
                    v.tensor_tensor(acc[:, t, :], acc[:, t, :], tail_x[:, t, :], ALU.add).then_inc(fin_add, 1)
                dve.wait_ge(w_ready, p + 1)
                for hf in range(2):
                    c = slice(hf * 512, (hf + 1) * 512)
                    dve.wait_ge(y_done, 2 * p + 1 + hf + Y_AHEAD)
                    v.scalar_tensor_tensor(y_end[:, c], (Y0, Y1)[hf][:, :], w_slot[:, j % 2:j % 2 + 1], tail_g2[:, c],
                                           ALU.mult, ALU.mult).then_inc(end_ready, 1)
                    dve.wait_ge(yh_ready, 2 * p + 3 + hf)
                    v.tensor_tensor(y_lo[:, c], y_end[:, c], y_hi[:, c].bitcast(F32), ALU.subtract).then_inc(yl_ready, 1)
                dve.wait_ge(fin_add, 2)

            def pair(it, j, last_pair=False):
                p = it * PPI + j
                if not last_pair:
                    dve.wait_ge(pt_psum, p + 1)
                    one_hot(p + 1, 0.0, rank_cols, p + 2).then_inc(p_ready, 1)
                add_up(p, range(4))
                dve.wait_ge(a_done, 2 * p + 2 + A_AHEAD)
                dve.wait_ge(sil_ready, p + 1)
                v.tensor_tensor(hid, sil, A3[:, :], ALU.mult).then_inc(hid_ready, 1)
                add_up(p, range(4, 8))

                def extra_round(r):
                    done = dve.snap(extra_n)
                    b0 = done * EXTRA_STEPS + EXTRA_AHEAD
                    nb = (j + 1) % 2
                    dve.wait_ge(p_ready, p + (1 if last_pair else 2))
                    dve.wait_ge(pt_psum, p + 1)
                    off = offs[:, r:r + 1] if isinstance(r, int) else offs[:, bass.ds(r, 1)]
                    one_hot(p, off, extra_vector, 2 * done + 1).then_inc(extra, 1)
                    dve.wait_ge(extra_sil, done + 1)
                    dve.wait_ge(extra, b0 + 6)
                    v.tensor_tensor(hid_x, sil, A3[:, :], ALU.mult).then_inc(extra, 1)
                    if last_pair:
                        dve.sem_inc(extra_vector, 1)
                    else:
                        dve.wait_ge(extra, b0 + 8)
                        one_hot(p + 1, 0.0, extra_vector, 2 * done + 2)
                    for hf in range(2):
                        dve.wait_ge(extra_hi, done * 2 + (hf + 1))
                        low_part(nb, hf).then_inc(extra_lo, 1)
                    for i, g in enumerate(HALVES_FIRST):
                        if i % 2 == 0:
                            dve.wait_ge(extra_c, done * 4 + (i // 2 + 1))
                        ins = add_group(g, EXTRA_BANKS[i])
                    ins.then_inc(extra, 1)
                    dve.wait_ge(extra, b0 + EXTRA_STEPS)
                    dve.reg_add(extra_n, extra_n, 1)

                further_rounds(dve, p, extra_round)
                if last_pair:
                    at_the_end(p, j)
                    return
                for hf in range(2):
                    dve.wait_ge(yh_ready, 2 * p + 3 + hf)
                    low_part(j % 2, hf).then_inc(yl_ready, 1)

            with dve.Fori(0, ITERS - 1) as it:
                for j in range(PPI):
                    pair(it, j)
            for j in range(PPI):
                pair(ITERS - 1, j, j == PPI - 1)
            for i, g in enumerate(HALVES_FIRST):
                dve.wait_ge(c_done, 8 * PAIRS + i + 1)
                if g >= 4:
                    dve.wait_ge(end_pool, g // 2 - 1)
                add_group(g, EXTRA_BANKS[i]).then_inc(acc_done, 1)
            for t in range(NT):
                dve.wait_ge(fin_std, t + 1)
                v.reciprocal(rstd[:, t:t + 1], rstd[:, t:t + 1]).then_inc(fin_rec, 1)
                dve.wait_ge(fin_rec, t + 1)
                v.scalar_tensor_tensor(acc[:, t, :], acc[:, t, :], rstd[:, t:t + 1], tail_fg,
                                       ALU.mult, ALU.mult).then_inc(fin, 1)

        @block.gpsimd
        def _(pool):
            g_ = nc.gpsimd
            n_chain = [0]

            def link(ins):
                n_chain[0] += 1
                ins.then_inc(pool_chain, 1)
                pool.wait_ge(pool_chain, n_chain[0])

            pool.wait_ge(job_done, JOB["mcol"] + 1)
            g_.memset(up, 0.0).then_inc(pads_zero, 1)
            pool.wait_ge(tmp_in, 16)
            for g, w in enumerate(WINDOWS):
                o, left, ed = POOL_AT[g]
                read_out(pool, f"u{g}")
                src, n, m = up[:, o:o + S + w - 1], S + w - 1, 1
                dst = (ta, tb)
                i = 0
                while m < w:
                    n -= m
                    to = dst[i % 2][:, 0:n]
                    link(g_.tensor_tensor(to, src[:, 0:n], src[:, m:m + n], ALU.add))
                    src, m, i = to, 2 * m, i + 1
                link(g_.tensor_tensor(src[:, 0:left], src[:, 0:left], edge[:, ed:ed + left], ALU.mult))
                if left > 1:
                    link(g_.tensor_tensor(src[:, S - left + 1:S], src[:, S - left + 1:S], edge[:, ed + left:ed + w - 1], ALU.mult))
                u = up[:, o + left:o + left + S]
                link(g_.tensor_scalar(src[:, 0:S], src[:, 0:S], 1.0 / w, None, ALU.mult))
                g_.tensor_tensor(u, src[:, 0:S], u, ALU.subtract).then_inc(pooled, 1)
                pool.wait_ge(pooled, g + 1)
            pool.wait_ge(job_done, JOB["g3"] + 1)
            pool.dma_start(bias_b, A["b_mod"][:, 2 * D:6 * D].to_broadcast([P, 4 * D])).then_inc(bias_in, 16)
            pool.wait_ge(qe_ready, 4)
            g_.memset(scr[:, 0:2048], 0.0).then_inc(att_zero, 1)

            def with_g1(c0, c1):
                for c in range(c0, c1):
                    if c % KD == 0:
                        n = SU[SPLIT[c // KD]]
                        pool.wait_ge(landed[n % PRE_SLOTS], 16 * (n // PRE_SLOTS + 1))
                    hf = c // KD - 4
                    w = raw_chunk(c)
                    g_.tensor_tensor(w, w, g1b[:, hf * 512:(hf + 1) * 512], ALU.mult).then_inc(scaled, 1)

            read_out(pool, "mb5")
            with_g1(4 * KD, 4 * KD + 6)
            read_out(pool, "mb11")
            pool.dma_start(g2_row, g2row).then_inc(g2_saved, 16)
            with_g1(4 * KD + 6, 6 * KD)
            for t in range(POOL_T):
                pool.wait_ge(h2_scaled, t + 1)
                g_.tensor_tensor(h2[:, t, :], h2[:, t, :], sh2b, ALU.add).then_inc(h2_first, 1)
            pool.wait_ge(h2_first, POOL_T)
            h2_tile(pool, NT - 1)
            g_.memset(y_hi[:, :].bitcast(F32), 0.0)
            g_.memset(y_lo[:, :].bitcast(F32), 0.0)
            g_.memset(slot_tok[:, 1, :].bitcast(F32), 0.0)
            pool.wait_ge(x1_saved, 16)
            for t in range(POOL_T):
                pool.wait_ge(h2_hi_ready, t + 1)
                g_.tensor_tensor(h2_lo[:, t, :], h2[:, t, :], h2_hi[:, t, :].bitcast(F32), ALU.subtract).then_inc(h2_lo_ready, 1)
            pool.wait_ge(h2_lo_ready, NT)
            pool.wait_ge(job_done, JOB["hT31"] + 1)
            g_.memset(mid[:, :], 0.0).then_inc(sum_zero, 1)
            pool.wait_ge(tail_in, 48)
            pool.wait_ge(fin_mul, 1)
            for t in range(2, NT):
                link(g_.tensor_tensor(acc[:, t, :], acc[:, t, :], tail_g2, ALU.mult))
                g_.tensor_tensor(acc[:, t, :], acc[:, t, :], tail_x[:, t, :], ALU.add).then_inc(end_pool, 1)


def kernel(**inputs):
    import numpy as _np
    import concourse.bacc as _bacc
    from concourse import mybir as _mybir
    from concourse.bass_utils import run_bass_kernel_spmd as _run

    f32 = _np.float32
    z = {k: _np.asarray(v) for k, v in inputs.items()}
    cp, ct, cm, i32 = constants()

    def columns(v):
        return v.reshape(-1, P).T

    arrays = {n: z[n] for n in ("x", "w_mod", "w_in", "w_out", "w1", "w3", "w2", "b_mod", "b_router", "final_g")}
    arrays["cols"] = _np.concatenate([columns(z["c"][0]), columns(z["b_mod"][0, :2 * D]), columns(z["pool_scale"][0]),
                                      columns(z["b_gk"][0].reshape(-1)), columns(z["gla_norm_g"][0]),
                                      _np.full((P, 1), EPS, f32)], 1)
    wr = _np.zeros((P, KD, P), f32)
    wr[:, :, :2 * RANK] = z["w_in"][0][:, 2048:].reshape(KD, P, 2 * RANK).transpose(1, 0, 2)
    arrays["wr"] = wr.reshape(P, -1)
    arrays["wrt"] = z["w_router"].reshape(KD, P, E_N).transpose(1, 0, 2).reshape(P, -1)
    arrays["wpool"] = z["w_pool"][0].transpose(1, 0, 2).reshape(P, -1)
    wup = _np.zeros((2 * RANK, 2, HEADS * DK), f32)
    wup[:RANK, 0], wup[RANK:, 1] = z["w_gk_up"][0, 0], z["w_gk_up"][0, 1]
    arrays["wup"] = wup.reshape(2 * RANK, -1)
    arrays.update(const_keep=cp, const_tmp=ct, masks=cm, iota32=i32)

    nc = _bacc.Bacc("TRN2", target_bir_lowering=False, num_devices=1)
    A = {}
    for n in arrays:
        arrays[n] = _np.ascontiguousarray(arrays[n])
        A[n] = nc.dram_tensor(f"in_{n}", arrays[n].shape, _mybir.dt.from_np(arrays[n].dtype), kind="ExternalInput").ap()
    out = nc.dram_tensor("out_0", (1, S, D), F32, kind="ExternalOutput").ap()
    g2_row = nc.dram_tensor("g2_row", (1, D), F32, kind="Internal").ap()
    x1_row = nc.dram_tensor("x1_rows", (S, D), F32, kind="Internal").ap()
    build(nc, A, out, g2_row, x1_row)
    r = _run(nc, [{f"in_{n}": a for n, a in arrays.items()}], core_ids=[0])
    return r.results[0]["out_0"]
```
